# Optimizing a Trainium2 kernel written in Bass

```python
import jax, jax.numpy as jnp
from jax import lax
import numpy as np

D_MODEL = 1024
BATCH = 1
SEQ = 1024
DEPTH = 2

GRID_W = 64
CTX_LEN = 256
NORM_EPS = 1e-6
ROPE_BASE = 10000.0
NEG_INF = -1e30

A_HEADS = 8
A_KV_HEADS = 2
A_HEAD_DIM = 64
A_WINDOW = 128
A_BLOCK = 128

B_HEADS = 4
B_HEAD_DIM = 128
B_CONV = 3
B_CHUNK = 64

C_HEADS = 16
C_NOPE = 64
C_ROPE = 32
C_V = 64
C_Q_RANK = 384
C_KV_RANK = 256
C_QBLOCK = 128

FFN_HIDDEN = ((8 * D_MODEL + 3 * 256 - 1) // (3 * 256)) * 256

A_Q_W = A_HEADS * A_HEAD_DIM
A_KV_W = A_KV_HEADS * A_HEAD_DIM
B_W = B_HEADS * B_HEAD_DIM
AB_SIZES = (A_Q_W, A_KV_W, A_KV_W, 3 * B_W, B_W, 2 * B_HEADS, 2 * B_HEADS)
AB_IN = sum(AB_SIZES)
AB_SPLITS = tuple(int(s) for s in np.cumsum(AB_SIZES)[:-1])
AB_OUT = A_Q_W + B_W
C_IN = C_Q_RANK + C_KV_RANK + C_ROPE
C_SPLITS = (C_Q_RANK, C_Q_RANK + C_KV_RANK)
C_OUT = C_HEADS * C_V

kernel_name = "hybrid_dit_swa_gdn_mla"

def rms_norm(x, gain):
    xf = x.astype(jnp.float32)
    y = xf * lax.rsqrt(jnp.mean(xf * xf, axis=-1, keepdims=True) + NORM_EPS)
    return (y * gain.astype(jnp.float32)).astype(x.dtype)

def l2_normalize(x):
    return x * lax.rsqrt(jnp.sum(x * x, axis=-1, keepdims=True) + NORM_EPS)

def modulate(x, gain, shift, scale):
    return rms_norm(x, gain) * (1 + scale) + shift

def adaln(cond, w, b):
    return jax.nn.silu(cond) @ w + b

def swiglu(u, w_gate, w_up, w_down):
    return (jax.nn.silu(u @ w_gate) * (u @ w_up)) @ w_down

def flip_seq(t):
    return t[:, ::-1]

def axial_rope_tables(rows, rot_dim):
    n_freq = rot_dim // 4
    inv_freq = ROPE_BASE ** (-jnp.arange(n_freq, dtype=jnp.float32) / n_freq)
    row = jnp.repeat(jnp.arange(rows, dtype=jnp.float32), GRID_W)
    col = jnp.tile(jnp.arange(GRID_W, dtype=jnp.float32), rows)
    ang = jnp.concatenate([row[:, None] * inv_freq, col[:, None] * inv_freq], axis=-1)
    return jnp.cos(ang), jnp.sin(ang)

def apply_rope(x, cos, sin):
    half = x.shape[-1] // 2
    x1, x2 = x[..., :half], x[..., half:]
    cs = cos[:, None, :].astype(x.dtype)
    sn = sin[:, None, :].astype(x.dtype)
    return jnp.concatenate([x1 * cs - x2 * sn, x1 * sn + x2 * cs], axis=-1)

def softmax_with_sink(s, sink_logit):
    s_sink = jnp.broadcast_to(sink_logit, s.shape[:-1] + (1,))
    return jax.nn.softmax(jnp.concatenate([s, s_sink], axis=-1), axis=-1)[..., :-1]

def window_attention(q, k, v, kc, vc, sink_logit):
    B, S, H, d = q.shape
    Hkv = k.shape[2]
    G = H // Hkv
    nb = S // A_BLOCK
    scale = d ** -0.5

    def band(t):
        tp = jnp.pad(t, ((0, 0), (A_BLOCK, A_BLOCK), (0, 0), (0, 0))).reshape(B, nb + 2, A_BLOCK, Hkv, d)
        tb = jnp.concatenate([tp[:, :-2], tp[:, 1:-1], tp[:, 2:]], axis=2)
        return jnp.moveaxis(tb, 1, 0)

    qb = jnp.moveaxis(q.reshape(B, nb, A_BLOCK, Hkv, G, d), 1, 0)
    kb, vb = band(k), band(v)
    rel = jnp.arange(3 * A_BLOCK)[None, :] - A_BLOCK - jnp.arange(A_BLOCK)[:, None]
    in_window = jnp.abs(rel) <= A_WINDOW

    def one_block(args):
        n, qn, kn, vn = args
        kpos = n * A_BLOCK - A_BLOCK + jnp.arange(3 * A_BLOCK)
        valid = in_window & ((kpos >= 0) & (kpos < S))[None, :]
        s_loc = jnp.einsum('bqhgd,bkhd->bhgqk', qn, kn).astype(jnp.float32) * scale
        s_loc = jnp.where(valid, s_loc, NEG_INF)
        s_ctx = jnp.einsum('bqhgd,bchd->bhgqc', qn, kc).astype(jnp.float32) * scale
        p = softmax_with_sink(jnp.concatenate([s_loc, s_ctx], axis=-1), sink_logit).astype(vn.dtype)
        return (jnp.einsum('bhgqk,bkhd->bqhgd', p[..., :3 * A_BLOCK], vn)
                + jnp.einsum('bhgqc,bchd->bqhgd', p[..., 3 * A_BLOCK:], vc))

    o = lax.map(one_block, (jnp.arange(nb), qb, kb, vb))
    return jnp.moveaxis(o, 0, 1).reshape(B, S, H * d)

def context_sink_attention(q, k, v, sink_logit):
    B, L, H, d = q.shape
    Hkv = k.shape[2]
    qg = q.reshape(B, L, Hkv, H // Hkv, d)
    s = jnp.einsum('bqhgd,bkhd->bhgqk', qg, k).astype(jnp.float32) * d ** -0.5
    p = softmax_with_sink(s, sink_logit).astype(v.dtype)
    return jnp.einsum('bhgqk,bkhd->bqhgd', p, v).reshape(B, L, H * d)

def depthwise_conv_centred(x, w):
    return lax.conv_general_dilated(x, w[:, None, :].astype(x.dtype), window_strides=(1,), padding='SAME',
                                    dimension_numbers=('NWC', 'WIO', 'NWC'), feature_group_count=x.shape[-1])

def delta_inputs(qkv, dec, beta, conv_w, a_log, dt_bias):
    B, L, _ = qkv.shape
    qkv = jax.nn.silu(depthwise_conv_centred(qkv, conv_w)).astype(jnp.float32)
    q, k, v = [t.reshape(B, L, B_HEADS, B_HEAD_DIM) for t in jnp.split(qkv, 3, axis=-1)]
    q = l2_normalize(q) * B_HEAD_DIM ** -0.5
    k = l2_normalize(k)
    dec = dec.astype(jnp.float32).reshape(B, L, 2, B_HEADS)
    log_decay = -jnp.exp(a_log.astype(jnp.float32)) * jax.nn.softplus(dec + dt_bias.astype(jnp.float32))
    beta = jax.nn.sigmoid(beta.astype(jnp.float32).reshape(B, L, 2, B_HEADS))
    return q, k, v, log_decay, beta

def gated_delta_rule(q, k, v, log_decay, beta, state):
    B, L, H, dk = k.shape
    dv = v.shape[-1]
    C = B_CHUNK
    nc = L // C

    def to_chunks(t):
        t = t.reshape((B, nc, C, H) + t.shape[3:])
        return jnp.moveaxis(jnp.moveaxis(t, 1, 0), 3, 2)

    qc, kc, vc, bc = to_chunks(q), to_chunks(k), to_chunks(v), to_chunks(beta)
    gc = jnp.cumsum(to_chunks(log_decay), axis=-1)
    idx = jnp.arange(C)
    lower = idx[:, None] >= idx[None, :]
    strict = idx[:, None] > idx[None, :]
    decay = jnp.exp(jnp.where(lower, gc[..., :, None] - gc[..., None, :], -jnp.inf))
    kbeta = kc * bc[..., None]
    a_kk = jnp.where(strict, jnp.einsum('...id,...jd->...ij', kbeta, kc) * decay, 0.0)
    rhs = jnp.concatenate([vc * bc[..., None], kbeta * jnp.exp(gc)[..., None]], axis=-1)
    sol = lax.linalg.triangular_solve(a_kk + jnp.eye(C, dtype=jnp.float32), rhs,
                                      left_side=True, lower=True, unit_diagonal=True)
    u, w = sol[..., :dv], sol[..., dv:]
    a_qk = jnp.einsum('...id,...jd->...ij', qc, kc) * decay
    g_last = gc[..., -1]
    k_tail = kc * jnp.exp(g_last[..., None] - gc)[..., None]
    q_head = qc * jnp.exp(gc)[..., None]

    def step(S, xs):
        u_i, w_i, qh_i, a_i, kt_i, gl_i = xs
        v_new = u_i - jnp.einsum('bhck,bhkv->bhcv', w_i, S)
        o = jnp.einsum('bhck,bhkv->bhcv', qh_i, S) + jnp.einsum('bhij,bhjv->bhiv', a_i, v_new)
        S = S * jnp.exp(gl_i)[..., None, None] + jnp.einsum('bhck,bhcv->bhkv', kt_i, v_new)
        return S, o

    S, o = lax.scan(step, state, (u, w, q_head, a_qk, k_tail, g_last))
    o = jnp.moveaxis(jnp.moveaxis(o, 0, 1), 2, 3).reshape(B, L, H, dv)
    return o, S

def gated_head_norm(o, gate, gain):
    B, L = o.shape[:2]
    y = rms_norm(o, gain) * jax.nn.silu(gate.astype(jnp.float32).reshape(o.shape))
    return y.reshape(B, L, -1).astype(gate.dtype)

def split_ab(p):
    B, L, _ = p.shape
    qa, ka, va, qkvb, gb, dec, beta = jnp.split(p, AB_SPLITS, axis=-1)
    return (qa.reshape(B, L, A_HEADS, A_HEAD_DIM), ka.reshape(B, L, A_KV_HEADS, A_HEAD_DIM),
            va.reshape(B, L, A_KV_HEADS, A_HEAD_DIM), qkvb, gb, dec, beta)

def hybrid_ab_mixer(u_lat, u_ctx, w_in, sink, conv_w, a_log, dt_bias, out_norm, w_out, cos, sin, with_ctx):
    B = u_lat.shape[0]
    qa_l, ka_l, va_l, qkv_l, gate_l, dec_l, beta_l = split_ab(u_lat @ w_in)
    qa_c, ka_c, va_c, qkv_c, gate_c, dec_c, beta_c = split_ab(u_ctx @ w_in)
    sink_logit = sink.astype(jnp.float32).reshape(A_KV_HEADS, A_HEADS // A_KV_HEADS, 1, 1)
    oa_l = window_attention(apply_rope(qa_l, cos, sin), apply_rope(ka_l, cos, sin), va_l, ka_c, va_c, sink_logit)
    q_l, k_l, v_l, g_l, b_l = delta_inputs(qkv_l, dec_l, beta_l, conv_w, a_log, dt_bias)
    q_c, k_c, v_c, g_c, b_c = delta_inputs(qkv_c, dec_c, beta_c, conv_w, a_log, dt_bias)
    zero = jnp.zeros((B, B_HEADS, B_HEAD_DIM, B_HEAD_DIM), jnp.float32)
    o_cf, s_f = gated_delta_rule(q_c, k_c, v_c, g_c[:, :, 0], b_c[:, :, 0], zero)
    o_cb, s_b = gated_delta_rule(flip_seq(q_c), flip_seq(k_c), flip_seq(v_c),
                                 flip_seq(g_c[:, :, 1]), flip_seq(b_c[:, :, 1]), zero)
    o_lf, _ = gated_delta_rule(q_l, k_l, v_l, g_l[:, :, 0], b_l[:, :, 0], s_f)
    o_lb, _ = gated_delta_rule(flip_seq(q_l), flip_seq(k_l), flip_seq(v_l),
                               flip_seq(g_l[:, :, 1]), flip_seq(b_l[:, :, 1]), s_b)
    ob_l = gated_head_norm(o_lf + flip_seq(o_lb), gate_l, out_norm)
    y_lat = jnp.concatenate([oa_l, ob_l.astype(oa_l.dtype)], axis=-1) @ w_out
    if not with_ctx:
        return y_lat, None
    oa_c = context_sink_attention(qa_c, ka_c, va_c, sink_logit)
    ob_c = gated_head_norm(o_cf + flip_seq(o_cb), gate_c, out_norm)
    y_ctx = jnp.concatenate([oa_c, ob_c.astype(oa_c.dtype)], axis=-1) @ w_out
    return y_lat, y_ctx

def mla_queries(cq, q_norm, w_qb):
    B, L, _ = cq.shape
    q = (rms_norm(cq, q_norm) @ w_qb).reshape(B, L, C_HEADS, C_NOPE + C_ROPE)
    return q[..., :C_NOPE], q[..., C_NOPE:]

def mla_keys(ckv, kv_norm, w_kvb):
    B, L, _ = ckv.shape
    kv = (rms_norm(ckv, kv_norm) @ w_kvb).reshape(B, L, C_HEADS, C_NOPE + C_V)
    return kv[..., :C_NOPE], kv[..., C_NOPE:]

def mla_attend(q_nope, q_pe, k_nope, k_pe, v):
    s = (jnp.einsum('bqhd,bkhd->bhqk', q_nope, k_nope)
         + jnp.einsum('bqhd,bkd->bhqk', q_pe, k_pe)).astype(jnp.float32) * (C_NOPE + C_ROPE) ** -0.5
    p = jax.nn.softmax(s, axis=-1).astype(v.dtype)
    return jnp.einsum('bhqk,bkhd->bqhd', p, v)

def mla_mixer(u_lat, u_ctx, w_in, q_norm, kv_norm, w_qb, w_kvb, w_out, cos, sin, with_ctx):
    B, S, _ = u_lat.shape
    Lc = u_ctx.shape[1]
    cq_l, ckv_l, kpe_l = jnp.split(u_lat @ w_in, C_SPLITS, axis=-1)
    cq_c, ckv_c, kpe_c = jnp.split(u_ctx @ w_in, C_SPLITS, axis=-1)
    qn_l, qp_l = mla_queries(cq_l, q_norm, w_qb)
    qp_l = apply_rope(qp_l, cos, sin)
    kpe_l = apply_rope(kpe_l[:, :, None, :], cos, sin)[:, :, 0]
    kn_l, v_l = mla_keys(ckv_l, kv_norm, w_kvb)
    kn_c, v_c = mla_keys(ckv_c, kv_norm, w_kvb)
    k_nope = jnp.concatenate([kn_c, kn_l], axis=1)
    k_pe = jnp.concatenate([kpe_c, kpe_l], axis=1)
    v = jnp.concatenate([v_c, v_l], axis=1)
    nb = S // C_QBLOCK

    def blocks(t):
        return jnp.moveaxis(t.reshape((B, nb, C_QBLOCK) + t.shape[2:]), 1, 0)

    o = lax.map(lambda qs: mla_attend(qs[0], qs[1], k_nope, k_pe, v), (blocks(qn_l), blocks(qp_l)))
    y_lat = jnp.moveaxis(o, 0, 1).reshape(B, S, C_OUT) @ w_out
    if not with_ctx:
        return y_lat, None
    qn_c, qp_c = mla_queries(cq_c, q_norm, w_qb)
    y_ctx = mla_attend(qn_c, qp_c, kn_c, kpe_c, v_c).reshape(B, Lc, C_OUT) @ w_out
    return y_lat, y_ctx

def setup_inputs(seed: int = 0) -> dict:
    key = jax.random.key(seed)
    ks = jax.random.split(key, 24)
    n_even = (DEPTH + 1) // 2
    n_odd = DEPTH // 2
    f32 = jnp.float32

    def nrm(k, shape, fan_in):
        return jax.random.normal(k, shape, f32) * fan_in ** -0.5

    dt = jnp.exp(jax.random.uniform(ks[13], (n_even, 2, B_HEADS), f32, np.log(1e-3), np.log(1e-1)))
    return {
        "x": jax.random.normal(ks[0], (BATCH, SEQ, D_MODEL), f32),
        "c": jax.random.normal(ks[1], (BATCH, D_MODEL), f32),
        "ctx": jax.random.normal(ks[2], (BATCH, CTX_LEN, D_MODEL), f32),
        "c_ctx": jax.random.normal(ks[3], (D_MODEL,), f32),
        "mod_w": nrm(ks[4], (DEPTH, D_MODEL, 6 * D_MODEL), D_MODEL),
        "mod_b": 0.02 * jax.random.normal(ks[5], (DEPTH, 6 * D_MODEL), f32),
        "norm_gains": 1.0 + 0.05 * jax.random.normal(ks[6], (DEPTH, 4, D_MODEL), f32),
        "ffn_w_gate": nrm(ks[7], (DEPTH, D_MODEL, FFN_HIDDEN), D_MODEL),
        "ffn_w_up": nrm(ks[8], (DEPTH, D_MODEL, FFN_HIDDEN), D_MODEL),
        "ffn_w_down": nrm(ks[9], (DEPTH, FFN_HIDDEN, D_MODEL), FFN_HIDDEN),
        "ab_w_in": nrm(ks[10], (n_even, D_MODEL, AB_IN), D_MODEL),
        "ab_sink": 0.5 * jax.random.normal(ks[11], (n_even, A_HEADS), f32),
        "ab_conv": nrm(ks[12], (n_even, B_CONV, 3 * B_W), B_CONV),
        "ab_a_log": jnp.log(jax.random.uniform(ks[14], (n_even, 2, B_HEADS), f32, 1.0, 16.0)),
        "ab_dt_bias": dt + jnp.log(-jnp.expm1(-dt)),
        "ab_out_norm": 1.0 + 0.05 * jax.random.normal(ks[15], (n_even, B_HEAD_DIM), f32),
        "ab_w_out": nrm(ks[16], (n_even, AB_OUT, D_MODEL), AB_OUT),
        "mla_w_in": nrm(ks[17], (n_odd, D_MODEL, C_IN), D_MODEL),
        "mla_q_norm": 1.0 + 0.05 * jax.random.normal(ks[18], (n_odd, C_Q_RANK), f32),
        "mla_kv_norm": 1.0 + 0.05 * jax.random.normal(ks[19], (n_odd, C_KV_RANK), f32),
        "mla_w_qb": nrm(ks[20], (n_odd, C_Q_RANK, C_HEADS * (C_NOPE + C_ROPE)), C_Q_RANK),
        "mla_w_kvb": nrm(ks[21], (n_odd, C_KV_RANK, C_HEADS * (C_NOPE + C_V)), C_KV_RANK),
        "mla_w_out": nrm(ks[22], (n_odd, C_OUT, D_MODEL), C_OUT),
    }

def reference(x, c, ctx, c_ctx, mod_w, mod_b, norm_gains, ffn_w_gate, ffn_w_up, ffn_w_down,
              ab_w_in, ab_sink, ab_conv, ab_a_log, ab_dt_bias, ab_out_norm, ab_w_out,
              mla_w_in, mla_q_norm, mla_kv_norm, mla_w_qb, mla_w_kvb, mla_w_out):
    S = x.shape[1]
    ROWS = S // GRID_W
    cos_a, sin_a = axial_rope_tables(ROWS, A_HEAD_DIM)
    cos_c, sin_c = axial_rope_tables(ROWS, C_ROPE)
    h, hc = x, ctx
    for layer in range(DEPTH):
        with_ctx = layer < DEPTH - 1
        gains = norm_gains[layer]
        m = jnp.split(adaln(c, mod_w[layer], mod_b[layer])[:, None, :], 6, axis=-1)
        mc = jnp.split(adaln(c_ctx, mod_w[layer], mod_b[layer])[None, None, :], 6, axis=-1)
        u = modulate(h, gains[0], m[0], m[1])
        uc = modulate(hc, gains[0], mc[0], mc[1])
        i = layer // 2
        if layer % 2 == 0:
            y, yc = hybrid_ab_mixer(u, uc, ab_w_in[i], ab_sink[i], ab_conv[i], ab_a_log[i], ab_dt_bias[i],
                                    ab_out_norm[i], ab_w_out[i], cos_a, sin_a, with_ctx)
        else:
            y, yc = mla_mixer(u, uc, mla_w_in[i], mla_q_norm[i], mla_kv_norm[i], mla_w_qb[i], mla_w_kvb[i],
                              mla_w_out[i], cos_c, sin_c, with_ctx)
        h = h + m[2] * rms_norm(y, gains[1])
        h = h + m[5] * rms_norm(swiglu(modulate(h, gains[2], m[3], m[4]),
                                       ffn_w_gate[layer], ffn_w_up[layer], ffn_w_down[layer]), gains[3])
        if with_ctx:
            hc = hc + mc[2] * rms_norm(yc, gains[1])
            hc = hc + mc[5] * rms_norm(swiglu(modulate(hc, gains[2], mc[3], mc[4]),
                                              ffn_w_gate[layer], ffn_w_up[layer], ffn_w_down[layer]), gains[3])
    return h


_drawn_inputs = setup_inputs


def setup_inputs(seed=0):
    import zlib

    import numpy as np

    out = dict(_drawn_inputs(seed))
    spreads = {}
    factors = {'ab_sink': 8.0, 'mla_q_norm': 8.0, 'mla_kv_norm': 2.751}
    for name, (base, spread) in spreads.items():
        noise = np.random.default_rng([zlib.crc32(name.encode()), seed]).standard_normal(out[name].shape)
        drawn = base * np.exp(spread * noise) if base else spread * noise
        out[name] = __import__('jax').numpy.asarray(drawn.astype(out[name].dtype))
    for name, factor in factors.items():
        out[name] = (out[name] * factor).astype(out[name].dtype)
    return out
```

```python
from contextlib import ExitStack

import numpy as np
import concourse.bass as bass
from concourse import mybir

ALU = mybir.AluOpType
ACT = mybir.ActivationFunctionType
F32 = mybir.dt.float32
AX_X = mybir.AxisListType.X

P = 128
D_MODEL, SEQ, CTX_LEN, DEPTH, GRID_W = 1024, 1024, 256, 2, 64
EPS = 1e-6
TOK = SEQ + CTX_LEN
KD = D_MODEL // P
NT, CT = TOK // P, CTX_LEN // P
LT = NT - CT
A_HEADS, A_KV, A_DIM = 8, 2, 64
B_HEADS, B_DIM = 4, 128
C_HEADS, C_NOPE, C_ROPE, C_V = 16, 64, 32, 64
C_QK = C_NOPE + C_ROPE
QR, KVR = 384, 256
FFN = 2816
FB = FFN // P
AB_IN = 2832
NEG = -1e30
ALL_CHUNKS = ((0, 512), (512, 512), (1024, 256))
LAT_CHUNKS = ((256, 512), (768, 512))
LEVELS = 7
MATS = (["ident", "ones", "swap", "dup0", "dup1", "dupswap0", "dupswap1", "kpe_place", "kpe_swap", "q_swap",
         "cum0", "cum1", "decay_mask0", "decay_mask1"]
        + [f"level{d}_{l}" for d in range(2) for l in range(LEVELS)])
ROWS_A = (("mod_b", 96), ("c", KD), ("c_ctx", KD), ("q_norm", 3), ("kv_norm", 2), ("out_norm", 1))
ROWS_B = (("norm_gains", 64), ("conv", 36))


def give(eng, sems, n=1):
    for s in sems:
        eng.sem_inc(s, n)


class Stage:
    used_semaphores = []

    def __init__(self, nc, name):
        self.nc, self.name, self.stack = nc, name, ExitStack()

    @classmethod
    def recycle(cls, nc):
        nc.clear_and_free_semaphores(cls.used_semaphores)
        cls.used_semaphores = []
        nc.all_engine_barrier()

    def __enter__(self):
        self.stack.__enter__()
        return self

    def __exit__(self, *a):
        return self.stack.__exit__(*a)

    def sb(self, name, *shape):
        return self.stack.enter_context(self.nc.sbuf_tensor(f"{self.name}_{name}", list(shape), F32))

    def ps(self, name, *shape):
        return self.stack.enter_context(self.nc.psum_tensor(f"{self.name}_{name}", list(shape), F32))

    def sem(self, name, n=None):
        sems = [self.nc.alloc_semaphore(f"{self.name}_{name}{i}") for i in range(n or 1)]
        Stage.used_semaphores += sems
        return sems if n else sems[0]


def rows_at(spec, name):
    at = 0
    for n, k in spec:
        if n == name:
            return at, at + k
        at += k
    raise KeyError(name)


def load_constants(nc, a, sb):
    with Stage(nc, "const") as st:
        rows = [st.sb("rows_a", P, P), st.sb("rows_b", P, P)]
        turned = [st.ps("turned_a", P, P), st.ps("turned_b", P, P)]
        loaded, cleared, transposed, columns = st.sem("loaded"), st.sem("cleared"), st.sem("transposed"), st.sem("columns")
        srcs = {
            "mod_b": a["mod_b"].rearrange("l (b p) -> (l b) p", p=P),
            "c": a["c"].rearrange("o (b p) -> (o b) p", p=P),
            "c_ctx": a["c_ctx"].rearrange("(b p) -> b p", p=P),
            "q_norm": a["mla_q_norm"].rearrange("o (b p) -> (o b) p", p=P),
            "kv_norm": a["mla_kv_norm"].rearrange("o (b p) -> (o b) p", p=P),
            "out_norm": a["ab_out_norm"],
            "norm_gains": a["norm_gains"].rearrange("l g (b p) -> (l g b) p", p=P),
            "conv": a["ab_conv"].rearrange("o j (b p) -> (o j b) p", p=P),
        }
        with nc.Block() as block:
            @block.vector
            def _(dve):
                for r in rows:
                    dve.memset(r[:, :], 0.0).then_inc(cleared, 1)
                dve.wait_ge(transposed, 2).then_inc(transposed, -2)
                dve.tensor_copy(sb["cols_a"][:, :], turned[0][:, :]).then_inc(columns, 1)
                dve.tensor_copy(sb["cols_b"][:, :], turned[1][:, :]).then_inc(columns, 1)

            @block.sync
            def _(sp):
                sp.dma_start(sb["ident"][:, :], a["mats"][MATS.index("ident")]).then_inc(loaded, 16)
                sp.dma_start(sb["ones"][:, :], a["mats"][MATS.index("ones")]).then_inc(loaded, 16)
                sp.wait_ge(cleared, 2)
                for spec, r in ((ROWS_A, rows[0]), (ROWS_B, rows[1])):
                    for name, _k in spec:
                        lo, hi = rows_at(spec, name)
                        sp.dma_start(r[lo:hi, :], srcs[name]).then_inc(loaded, 16)

            @block.tensor
            def _(pe):
                pe.wait_ge(loaded, 16 * (2 + len(ROWS_A) + len(ROWS_B)))
                for r, t in zip(rows, turned):
                    pe.transpose(t[:, :], r[:, :], sb["ident"][:, :]).then_inc(transposed, 1)

            @block.scalar
            def _(act):
                act.wait_ge(columns, 2)
                lo, _hi = rows_at(ROWS_A, "c")
                act.activation(sb["silu_c"][:, :, :], sb["cols_a"][:, lo:lo + 2 * KD].rearrange("p (c k) -> p k c", c=2),
                               ACT.Silu)


def adaln(nc, a, sb):
    NG, NS = 12, 3
    with Stage(nc, "adaln") as st:
        w = [st.sb(f"w{s}", P, KD, 512) for s in range(NS)]
        out = [st.ps(f"out{s}", P, 2, 4) for s in range(NS)]
        mod = st.sb("mod", P, DEPTH, 2, 48)
        w_in, w_free = st.sem("w_in", NS), st.sem("w_free", NS)
        out_full, out_free = st.sem("out_full", NS), st.sem("out_free", NS)
        mod_done, coef_step = st.sem("mod_done"), st.sem("coef_step")
        b_lo, _ = rows_at(ROWS_A, "mod_b")
        g_lo, _ = rows_at(ROWS_B, "norm_gains")
        with nc.Block() as block:
            @block.sync
            def _(sp):
                for layer in range(DEPTH):
                    w_v = a["mod_w"][layer].rearrange("(k p) n -> p k n", p=P)
                    with sp.Fori(0, NG // NS) as i:
                        for s in range(NS):
                            sp.wait_ge(w_free[s], 1).then_inc(w_free[s], -1)
                            sp.dma_start(w[s][:, :, :], w_v[:, :, bass.ds((i * NS + s) * 512, 512)]).then_inc(w_in[s], 16)

            @block.tensor
            def _(pe):
                for layer in range(DEPTH):
                    with pe.Fori(0, NG // NS) as i:
                        for s in range(NS):
                            pe.wait_ge(w_in[s], 16).then_inc(w_in[s], -16)
                            pe.wait_ge(out_free[s], 1).then_inc(out_free[s], -1)
                            for b in range(4):
                                for k in range(KD):
                                    mm = pe.matmul(out[s][:, :, b], w[s][:, k, b * P:(b + 1) * P], sb["silu_c"][:, k, :],
                                                   start=(k == 0), stop=(k == KD - 1))
                            mm.then_inc(out_full[s], 1)

            @block.vector
            def _(dve):
                give(dve, w_free)
                give(dve, out_free)
                for layer in range(DEPTH):
                    with dve.Fori(0, NG // NS) as i:
                        for s in range(NS):
                            dve.wait_ge(out_full[s], 1).then_inc(out_full[s], -1)
                            dve.sem_inc(w_free[s], 1)
                            for cond in range(2):
                                at = (i * NS + s) * 4
                                dve.tensor_tensor(mod[:, layer, cond, bass.ds(at, 4)], out[s][:, cond, :],
                                                  sb["cols_a"][:, bass.ds(at + b_lo + layer * 48, 4)],
                                                  ALU.add).then_inc(mod_done, 1)
                            dve.wait_ge(mod_done, 2).then_inc(mod_done, -2)
                            dve.sem_inc(out_free[s], 1)
                for layer in range(DEPTH):
                    for half in range(2):
                        for cond in range(2):
                            m = [mod[:, layer, cond, (3 * half + j) * KD:(3 * half + j + 1) * KD] for j in range(3)]
                            g = [sb["cols_b"][:, g_lo + (layer * 4 + 2 * half + j) * KD:g_lo + (layer * 4 + 2 * half + j + 1) * KD]
                                 for j in range(2)]
                            c = sb["coef"]
                            dve.tensor_copy(c[:, layer, half, cond, 0, :], m[0])
                            dve.scalar_tensor_tensor(out=c[:, layer, half, cond, 1, :], in0=m[1], scalar=1.0, in1=g[0],
                                                     op0=ALU.add, op1=ALU.mult)
                            dve.tensor_tensor(c[:, layer, half, cond, 2, :], m[2], g[1], ALU.mult)


def norms(nc, a, sb, name, segs, layer_y=None, y=None, layer_u=None, u=None):
    with Stage(nc, name) as st:
        h = [st.sb(f"h{s}", P, D_MODEL) for s in range(2)]
        sq = st.sb("sq", P, D_MODEL)
        stat = st.sb("stat", P, 2, 2, 4)
        eps = st.sb("eps", P, 1)
        h_in, h_free, h_out = st.sem("h_in", 2), st.sem("h_free", 2), st.sem("h_out", 2)
        h_new, h_new_act, h_new_dma = st.sem("h_new"), st.sem("h_new_act"), st.sem("h_new_dma", 2)
        act_step, root, sub, eps_set = st.sem("act_step"), st.sem("root"), st.sem("sub"), st.sem("eps_set")
        if y is not None:
            y_slot = [st.sb(f"y{s}", P, KD, P) for s in range(2)]
            y_tok = [st.ps(f"ytok{s}", P, D_MODEL) for s in range(2)]
            gate = st.sb("gate", P, 2, D_MODEL)
            tmp = st.sb("tmp", P, D_MODEL)
            y_in, y_free, y_full, y_read = st.sem("y_in", 2), st.sem("y_free", 2), st.sem("y_full", 2), st.sem("y_read", 2)
            gate_full, gate_read, gate_set = st.sem("gate_full"), st.sem("gate_read"), st.sem("gate_set")
        if u is not None:
            hn = [st.sb(f"hn{s}", P, D_MODEL) for s in range(2)]
            u_ps = [st.ps(f"ups{s}", P, D_MODEL) for s in range(2)]
            hn_full, hn_free, u_full, u_free = st.sem("hn_full", 2), st.sem("hn_free", 2), st.sem("u_full", 2), st.sem("u_free", 2)
            h_read = st.sem("h_read", 2)
        conds = [s[0] for s in segs]
        with nc.Block() as block:
            @block.sync
            def _(sp):
                for cond, t0, n, src, dst in segs:
                    with sp.Fori(0, n // 2) as i:
                        for s in range(2):
                            sp.wait_ge(h_free[s], 1).then_inc(h_free[s], -1)
                            sp.dma_start(h[s][:, :], src[bass.ds((2 * i + s) * P, P), :]).then_inc(h_in[s], 16)
                            if y is not None:
                                sp.wait_ge(y_free[s], 1).then_inc(y_free[s], -1)
                                sp.dma_start(y_slot[s][:, :, :], y[:, :, bass.ds((2 * i + s + t0) * P, P)]).then_inc(y_in[s], 16)

            @block.tensor
            def _(pe):
                if y is not None:
                    for cond in conds:
                        pe.wait_ge(gate_read, 1).then_inc(gate_read, -1)
                        for k in range(KD):
                            col = sb["coef"][:, layer_y[0], layer_y[1], cond, 2, k:k + 1]
                            mm = pe.matmul(y_tok[0][:, k * P:(k + 1) * P], col.to_broadcast([P, P]), sb["ident"][:, :],
                                           start=True, stop=True)
                        mm.then_inc(gate_full, 1)
                    pe.wait_ge(gate_read, 1).then_inc(gate_read, -1)
                for cond, t0, n, src, dst in segs:
                    with pe.Fori(0, n // 2) as i:
                        if y is not None:
                            for s in range(2):
                                pe.wait_ge(y_in[s], 16).then_inc(y_in[s], -16)
                                pe.wait_ge(y_read[s], 1).then_inc(y_read[s], -1)
                                for k in range(KD):
                                    mm = pe.transpose(y_tok[s][:, k * P:(k + 1) * P], y_slot[s][:, k, :], sb["ident"][:, :])
                                mm.then_inc(y_full[s], 1)
                        if u is not None:
                            for s in range(2):
                                pe.wait_ge(hn_full[s], 1).then_inc(hn_full[s], -1)
                                pe.wait_ge(u_free[s], 1).then_inc(u_free[s], -1)
                                for k in range(KD):
                                    mm = pe.transpose(u_ps[s][:, k * P:(k + 1) * P], hn[s][:, k * P:(k + 1) * P], sb["ident"][:, :])
                                mm.then_inc(u_full[s], 1)

            def root_mean_square(act, src, to):
                act.activation(sq[:, :], src, ACT.Square, accum_out=to[:, 0:1]).then_inc(act_step, 1)
                act.wait_ge(act_step, 1).then_inc(act_step, -1)
                act.activation(to[:, 1:2], to[:, 0:1], ACT.Sqrt, scale=1.0 / D_MODEL, bias=eps[:, :]).then_inc(root, 1)

            @block.scalar
            def _(act):
                act.wait_ge(eps_set, 1)
                for cond, t0, n, src, dst in segs:
                    with act.Fori(0, n // 2) as i:
                        for s in range(2):
                            if y is not None:
                                act.wait_ge(y_full[s], 1).then_inc(y_full[s], -1)
                                act.sem_inc(y_free[s], 1)
                                root_mean_square(act, y_tok[s][:, :], stat[:, s, 0, :])
                        for s in range(2):
                            if y is None:
                                act.wait_ge(h_in[s], 16).then_inc(h_in[s], -16)
                            else:
                                act.wait_ge(h_new_act, 1).then_inc(h_new_act, -1)
                            if u is not None:
                                root_mean_square(act, h[s][:, :], stat[:, s, 1, :])
                            if dst is not None:
                                act.dma_start(dst[bass.ds((2 * i + s) * P, P), :], h[s][:, :]).then_inc(h_out[s], 16)
                        if u is not None:
                            for s in range(2):
                                act.wait_ge(u_full[s], 1).then_inc(u_full[s], -1)
                                act.sem_inc(hn_free[s], 1)
                                c = sb["coef"]
                                for k in range(KD):
                                    act.activation(u[:, k, bass.ds((2 * i + s + t0) * P, P)], u_ps[s][:, k * P:(k + 1) * P],
                                                   ACT.Identity, scale=c[:, layer_u[0], layer_u[1], cond, 1, k:k + 1],
                                                   bias=c[:, layer_u[0], layer_u[1], cond, 0, k:k + 1]).then_inc(act_step, 1)
                                act.wait_ge(act_step, KD).then_inc(act_step, -KD)
                                act.sem_inc(u_free[s], 1)

            @block.vector
            def _(dve):
                dve.memset(eps[:, :], EPS).then_inc(eps_set, 1)
                give(dve, h_free)
                if y is not None:
                    give(dve, y_free)
                    give(dve, y_read)
                    give(dve, [gate_read])
                    for cond in conds:
                        dve.wait_ge(gate_full, 1).then_inc(gate_full, -1)
                        dve.tensor_copy(gate[:, cond, :], y_tok[0][:, :]).then_inc(gate_set, 1)
                        dve.wait_ge(gate_set, 1).then_inc(gate_set, -1)
                        dve.sem_inc(gate_read, 1)
                if u is not None:
                    give(dve, hn_free)
                    give(dve, u_free)
                for cond, t0, n, src, dst in segs:
                    with dve.Fori(0, n // 2) as i:
                        for s in range(2):
                            if y is not None:
                                r = stat[:, s, 0, 2:3]
                                dve.wait_ge(root, 1).then_inc(root, -1)
                                dve.reciprocal(r, stat[:, s, 0, 1:2]).then_inc(sub, 1)
                                dve.wait_ge(sub, 1).then_inc(sub, -1)
                                dve.scalar_tensor_tensor(out=tmp[:, :], in0=y_tok[s][:, :], scalar=r, in1=gate[:, cond, :],
                                                         op0=ALU.mult, op1=ALU.mult).then_inc(sub, 1)
                                dve.wait_ge(sub, 1).then_inc(sub, -1)
                                dve.sem_inc(y_read[s], 1)
                                dve.wait_ge(h_in[s], 16).then_inc(h_in[s], -16)
                                dve.tensor_tensor(h[s][:, :], h[s][:, :], tmp[:, :], ALU.add).then_inc(sub, 1)
                                dve.wait_ge(sub, 1).then_inc(sub, -1)
                                dve.sem_inc(h_new_act, 1)
                            if y is not None and u is None:
                                dve.wait_ge(h_out[s], 16).then_inc(h_out[s], -16)
                                dve.sem_inc(h_free[s], 1)
                        if u is not None:
                            for s in range(2):
                                r = stat[:, s, 1, 2:3]
                                dve.wait_ge(root, 1).then_inc(root, -1)
                                dve.reciprocal(r, stat[:, s, 1, 1:2]).then_inc(sub, 1)
                                dve.wait_ge(sub, 1).then_inc(sub, -1)
                                dve.wait_ge(hn_free[s], 1).then_inc(hn_free[s], -1)
                                dve.tensor_scalar(hn[s][:, :], h[s][:, :], r, None, ALU.mult).then_inc(sub, 1)
                                dve.wait_ge(sub, 1).then_inc(sub, -1)
                                dve.sem_inc(hn_full[s], 1)
                                if dst is not None:
                                    dve.wait_ge(h_out[s], 16).then_inc(h_out[s], -16)
                                dve.sem_inc(h_free[s], 1)


def project(nc, name, segs, x, k_tiles, chunks):
    nch = len(chunks)
    with Stage(nc, name) as st:
        w_slot = [st.sb(f"w{s}", P, k_tiles, P) for s in range(2)]
        acc = [[st.ps(f"acc{s}{j}", P, 512) for j in range(nch)] for s in range(2)]
        w_in, w_free = st.sem("w_in", 2), st.sem("w_free", 2)
        acc_full = [st.sem(f"acc_full{s}", nch) for s in range(2)]
        acc_free = [st.sem(f"acc_free{s}", nch) for s in range(2)]
        copied = st.sem("copied")

        def over_blocks(eng, nblk, body):
            if nblk > 1:
                with eng.Fori(0, nblk // 2) as i:
                    for s in range(2):
                        body(s, 2 * i + s)
            if nblk % 2:
                body(0, nblk - 1)

        with nc.Block() as block:
            @block.sync
            def _(sp):
                for w, col0, m, nblk, dst, blk0 in segs:
                    w_v = w.rearrange("(k p) n -> p k n", p=P)

                    def load(s, b):
                        sp.wait_ge(w_free[s], 1).then_inc(w_free[s], -1)
                        sp.dma_start(w_slot[s][:, :, 0:m], w_v[:, :, bass.ds(b * m + col0, m)]).then_inc(w_in[s], 16)
                    over_blocks(sp, nblk, load)

            @block.tensor
            def _(pe):
                for w, col0, m, nblk, dst, blk0 in segs:
                    def products(s, b):
                        pe.wait_ge(w_in[s], 16).then_inc(w_in[s], -16)
                        for j, (t0, n) in enumerate(chunks):
                            pe.wait_ge(acc_free[s][j], 1).then_inc(acc_free[s][j], -1)
                            for k in range(k_tiles):
                                mm = pe.matmul(acc[s][j][0:m, 0:n], w_slot[s][:, k, 0:m], x[:, k, t0:t0 + n],
                                               start=(k == 0), stop=(k == k_tiles - 1))
                            mm.then_inc(acc_full[s][j], 1)
                    over_blocks(pe, nblk, products)

            @block.vector
            def _(dve):
                give(dve, w_free)
                for s in range(2):
                    give(dve, acc_free[s])
                for w, col0, m, nblk, dst, blk0 in segs:
                    def copy_out(s, b):
                        for j, (t0, n) in enumerate(chunks):
                            dve.wait_ge(acc_full[s][j], 1).then_inc(acc_full[s][j], -1)
                            if j == nch - 1:
                                dve.sem_inc(w_free[s], 1)
                            dve.tensor_copy(dst[0:m, bass.ds(b + blk0, 1), t0:t0 + n], acc[s][j][0:m, 0:n].rearrange("p (o n) -> p o n", o=1)).then_inc(copied, 1)
                            dve.wait_ge(copied, 1).then_inc(copied, -1)
                            dve.sem_inc(acc_free[s][j], 1)
                    over_blocks(dve, nblk, copy_out)


def ffn_hidden(nc, name, w_gate, w_up, u, hid, chunks):
    nch = len(chunks)
    with Stage(nc, name) as st:
        w_slot = [st.sb(f"w{s}", P, 2, KD, P) for s in range(2)]
        acc = [[st.ps(f"acc{j}{g}", P, 512) for g in range(2)] for j in range(nch)]
        act_out = [st.sb(f"silu{j}", P, 512) for j in range(nch)]
        w_in, w_free = st.sem("w_in", 2), st.sem("w_free", 2)
        gate_full, up_full = st.sem("gate_full", nch), st.sem("up_full", nch)
        silu_full, pair_free = st.sem("silu_full", nch), st.sem("pair_free", nch)
        done = st.sem("done")
        with nc.Block() as block:
            @block.sync
            def _(sp):
                wv = [w.rearrange("(k p) n -> p k n", p=P) for w in (w_gate, w_up)]
                with sp.Fori(0, FB // 2) as i:
                    for s in range(2):
                        sp.wait_ge(w_free[s], 1).then_inc(w_free[s], -1)
                        for g in range(2):
                            sp.dma_start(w_slot[s][:, g, :, :], wv[g][:, :, bass.ds((2 * i + s) * P, P)]).then_inc(w_in[s], 16)

            @block.tensor
            def _(pe):
                with pe.Fori(0, FB // 2) as i:
                    for s in range(2):
                        pe.wait_ge(w_in[s], 32).then_inc(w_in[s], -32)
                        for j, (t0, n) in enumerate(chunks):
                            pe.wait_ge(pair_free[j], 1).then_inc(pair_free[j], -1)
                            for g, full in ((0, gate_full), (1, up_full)):
                                for k in range(KD):
                                    mm = pe.matmul(acc[j][g][:, 0:n], w_slot[s][:, g, k, :], u[:, k, t0:t0 + n],
                                                   start=(k == 0), stop=(k == KD - 1))
                                mm.then_inc(full[j], 1)

            @block.scalar
            def _(act):
                with act.Fori(0, FB // 2) as i:
                    for s in range(2):
                        for j, (t0, n) in enumerate(chunks):
                            act.wait_ge(gate_full[j], 1).then_inc(gate_full[j], -1)
                            act.activation(act_out[j][:, 0:n], acc[j][0][:, 0:n], ACT.Silu).then_inc(silu_full[j], 1)

            @block.vector
            def _(dve):
                give(dve, w_free)
                give(dve, pair_free)
                with dve.Fori(0, FB // 2) as i:
                    for s in range(2):
                        for j, (t0, n) in enumerate(chunks):
                            dve.wait_ge(up_full[j], 1).then_inc(up_full[j], -1)
                            if j == nch - 1:
                                dve.sem_inc(w_free[s], 1)
                            dve.wait_ge(silu_full[j], 1).then_inc(silu_full[j], -1)
                            dve.tensor_tensor(hid[:, bass.ds(2 * i + s, 1), t0:t0 + n], acc[j][1][:, 0:n].rearrange("p (o n) -> p o n", o=1),
                                              act_out[j][:, 0:n].rearrange("p (o n) -> p o n", o=1), ALU.mult).then_inc(done, 1)
                            dve.wait_ge(done, 1).then_inc(done, -1)
                            dve.sem_inc(pair_free[j], 1)


def decay_columns(nc, a, sb, u, cols):
    w_col = AB_IN - 4 * B_HEADS
    nh = 2 * B_HEADS
    with Stage(nc, "decay") as st:
        w = st.sb("w", P, KD, 2 * nh)
        alog, dtb = st.sb("alog", P, nh), st.sb("dtb", P, nh)
        cum = [st.sb(f"cum{d}", P, P) for d in range(2)]
        x, e, sp_, total = (st.sb(n, P, NT, nh) for n in ("x", "e", "sp", "total"))
        raw = st.ps("raw", P, NT, 2 * nh)
        sums = st.ps("sums", P, 2, NT, nh)
        loaded, raw_full, step, act_step = st.sem("loaded"), st.sem("raw_full"), st.sem("step"), st.sem("act_step")
        go_act, go_dve, ld_full, sums_full = st.sem("go_act"), st.sem("go_dve"), st.sem("ld_full"), st.sem("sums_full")

        def kind(k, d):
            return cols[:, :, d, k, :]

        def heads(t, d):
            return t[:, :, d * B_HEADS:(d + 1) * B_HEADS]

        with nc.Block() as block:
            @block.sync
            def _(sp):
                sp.dma_start(w[:, :, :], a["ab_w_in"][0].rearrange("(k p) n -> p k n", p=P)[:, :, w_col:AB_IN]).then_inc(loaded, 16)
                sp.dma_start(alog[:, :], a["ab_a_log"].rearrange("o d h -> o (d h)").to_broadcast([P, nh])).then_inc(loaded, 16)
                sp.dma_start(dtb[:, :], a["ab_dt_bias"].rearrange("o d h -> o (d h)").to_broadcast([P, nh])).then_inc(loaded, 16)
                for d in range(2):
                    sp.dma_start(cum[d][:, :], a["mats"][MATS.index(f"cum{d}")]).then_inc(loaded, 16)

            @block.tensor
            def _(pe):
                pe.wait_ge(loaded, 80)
                for t in range(NT):
                    for k in range(KD):
                        mm = pe.matmul(raw[:, t, :], u[:, k, t * P:(t + 1) * P], w[:, k, :], start=(k == 0), stop=(k == KD - 1))
                mm.then_inc(raw_full, 1)
                pe.wait_ge(ld_full, 1).then_inc(ld_full, -1)
                for d in range(2):
                    ld = sp_[:, :, d * B_HEADS:(d + 1) * B_HEADS]
                    pe.matmul(sums[:, 0, :, d * B_HEADS:(d + 1) * B_HEADS], cum[d][:, :], ld, start=True, stop=True)
                    mm = pe.matmul(sums[:, 1, :, d * B_HEADS:(d + 1) * B_HEADS], sb["ones"][:, :], ld, start=True, stop=True)
                mm.then_inc(sums_full, 1)

            @block.vector
            def _(dve):
                def done(ins, n=1):
                    ins.then_inc(step, 1)
                    dve.wait_ge(step, 1).then_inc(step, -1)

                dve.wait_ge(loaded, 80)
                dve.wait_ge(raw_full, 1).then_inc(raw_full, -1)
                done(dve.tensor_tensor(x[:, :, :], raw[:, :, 0:nh], dtb[:, :].rearrange("p (o n) -> p o n", o=1).to_broadcast([P, NT, nh]), ALU.add))
                done(dve.tensor_copy(total[:, :, :], raw[:, :, nh:2 * nh]))
                dve.sem_inc(go_act, 1)
                dve.wait_ge(go_dve, 1).then_inc(go_dve, -1)
                done(dve.tensor_scalar(e[:, :, :], e[:, :, :], 1.0, None, ALU.add))
                done(dve.reciprocal(e[:, :, :], e[:, :, :]))
                for d in range(2):
                    dve.tensor_copy(kind(2, d), heads(e, d))
                done(dve.tensor_scalar(x[:, :, :], x[:, :, :], 0.0, None, ALU.max))
                done(dve.tensor_tensor(x[:, :, :], x[:, :, :], sp_[:, :, :], ALU.add))
                done(dve.scalar_tensor_tensor(out=sp_[:, :, :], in0=x[:, :, :], scalar=-1.0,
                                              in1=alog[:, :].rearrange("p (o n) -> p o n", o=1).to_broadcast([P, NT, nh]), op0=ALU.mult, op1=ALU.mult))
                dve.sem_inc(ld_full, 1)
                for d in range(2):
                    dve.tensor_copy(kind(0, d), heads(sp_, d))
                dve.wait_ge(sums_full, 1).then_inc(sums_full, -1)
                done(dve.tensor_copy(x[:, :, :], sums[:, 0, :, :]))
                done(dve.tensor_copy(total[:, :, :], sums[:, 1, :, :]))
                for d in range(2):
                    dve.tensor_copy(kind(1, d), heads(x, d))
                done(dve.tensor_tensor(sp_[:, :, :], total[:, :, :], x[:, :, :], ALU.subtract))
                dve.sem_inc(go_act, 1)
                dve.wait_ge(go_dve, 1).then_inc(go_dve, -1)
                done(dve.tensor_tensor(sp_[:, :, :], sp_[:, :, :], e[:, :, :], ALU.mult))
                for d in range(2):
                    dve.tensor_scalar(kind(3, d), heads(x, d), -1.0, None, ALU.mult)
                    dve.tensor_copy(kind(4, d), heads(sp_, d))
                    dve.tensor_copy(kind(5, d), heads(total, d))

            @block.scalar
            def _(act):
                def done(ins):
                    ins.then_inc(act_step, 1)
                    act.wait_ge(act_step, 1).then_inc(act_step, -1)

                act.wait_ge(go_act, 1).then_inc(go_act, -1)
                done(act.activation(e[:, :, :], total[:, :, :], ACT.Exp, scale=-1.0))
                done(act.activation(alog[:, :], alog[:, :], ACT.Exp))
                done(act.activation(sp_[:, :, :], x[:, :, :], ACT.Abs))
                done(act.activation(sp_[:, :, :], sp_[:, :, :], ACT.Exp, scale=-1.0))
                done(act.activation(sp_[:, :, :], sp_[:, :, :], ACT.Ln, bias=1.0))
                act.sem_inc(go_dve, 1)
                act.wait_ge(go_act, 1).then_inc(go_act, -1)
                done(act.activation(x[:, :, :], x[:, :, :], ACT.Exp))
                done(act.activation(sp_[:, :, :], sp_[:, :, :], ACT.Exp))
                done(act.activation(total[:, :, :], total[:, :, :], ACT.Exp))
                act.sem_inc(go_dve, 1)


def conv_qkv(nc, a, sb, pb, qkv_dram):
    c_lo, _ = rows_at(ROWS_B, "conv")
    with Stage(nc, "conv") as st:
        y = [st.sb(f"y{s}", P, TOK) for s in range(2)]
        z = [st.sb(f"z{s}", P, TOK) for s in range(2)]
        sq = [st.sb(f"sq{s}", P, TOK) for s in range(2)]
        eps = st.sb("eps", P, 1)
        norm = [[st.ps(f"norm{s}{j}", P, 512) for j in range(3)] for s in range(2)]
        eps_set, step, act_step = st.sem("eps_set"), st.sem("step"), st.sem("act_step")
        y_full, z_full, sq_full, norm_full, root_full = (st.sem(n, 2) for n in ("y_full", "z_full", "sq_full", "norm_full", "root_full"))
        out_ready, stored = st.sem("out_ready", 2), st.sem("stored", 2)
        groups = ((0, float(B_DIM) ** -0.5), (4, 1.0), (8, None))
        with nc.Block() as block:
            @block.vector
            def _(dve):
                dve.memset(eps[:, :], EPS).then_inc(eps_set, 1)
                give(dve, stored, 16)
                for b0, scale in groups:
                    with dve.Fori(0, 2) as i:
                        for s in range(2):
                            b = 2 * i + s + b0
                            taps = [sb["cols_b"][:, bass.ds(b + c_lo + 12 * j, 1)] for j in range(3)]
                            dve.wait_ge(stored[s], 16).then_inc(stored[s], -16)
                            dve.tensor_scalar(y[s][:, :].rearrange("p (o n) -> p o n", o=1), pb[:, bass.ds(b, 1), :], taps[1], None, ALU.mult).then_inc(step, 1)
                            dve.wait_ge(step, 1).then_inc(step, -1)
                            for j, (src, dst) in ((0, (0, 1)), (2, (1, 0))):
                                for lo, n in ((0, CTX_LEN), (CTX_LEN, SEQ)):
                                    o = y[s][:, lo + dst:lo + dst + n - 1].rearrange("p (o n) -> p o n", o=1)
                                    dve.scalar_tensor_tensor(out=o, in0=pb[:, bass.ds(b, 1), lo + src:lo + src + n - 1],
                                                             scalar=taps[j], in1=o, op0=ALU.mult, op1=ALU.add).then_inc(step, 1)
                                dve.wait_ge(step, 2).then_inc(step, -2)
                            dve.sem_inc(y_full[s], 1)
                        if scale is not None:
                            for s in range(2):
                                dve.wait_ge(root_full[s], 1).then_inc(root_full[s], -1)
                                dve.reciprocal(y[s][:, :], y[s][:, :]).then_inc(step, 1)
                                dve.wait_ge(step, 1).then_inc(step, -1)
                                dve.scalar_tensor_tensor(out=z[s][:, :], in0=y[s][:, :], scalar=scale, in1=z[s][:, :],
                                                         op0=ALU.mult, op1=ALU.mult).then_inc(out_ready[s], 1)

            @block.scalar
            def _(act):
                act.wait_ge(eps_set, 1)
                for b0, scale in groups:
                    with act.Fori(0, 2) as i:
                        for s in range(2):
                            act.wait_ge(y_full[s], 1).then_inc(y_full[s], -1)
                            ins = act.activation(z[s][:, :], y[s][:, :], ACT.Silu)
                            if scale is None:
                                ins.then_inc(out_ready[s], 1)
                                continue
                            ins.then_inc(act_step, 1)
                            act.wait_ge(act_step, 1).then_inc(act_step, -1)
                            act.activation(sq[s][:, :], z[s][:, :], ACT.Square).then_inc(sq_full[s], 1)
                        if scale is not None:
                            for s in range(2):
                                act.wait_ge(norm_full[s], 1).then_inc(norm_full[s], -1)
                                for j, (t0, n) in enumerate(ALL_CHUNKS):
                                    act.activation(y[s][:, t0:t0 + n], norm[s][j][:, 0:n], ACT.Sqrt, bias=eps[:, :]).then_inc(act_step, 1)
                                act.wait_ge(act_step, 3).then_inc(act_step, -3)
                                act.sem_inc(root_full[s], 1)

            @block.tensor
            def _(pe):
                for b0, scale in groups:
                    if scale is None:
                        continue
                    with pe.Fori(0, 2) as i:
                        for s in range(2):
                            pe.wait_ge(sq_full[s], 1).then_inc(sq_full[s], -1)
                            for j, (t0, n) in enumerate(ALL_CHUNKS):
                                mm = pe.matmul(norm[s][j][:, 0:n], sb["ones"][:, :], sq[s][:, t0:t0 + n], start=True, stop=True)
                            mm.then_inc(norm_full[s], 1)

            @block.sync
            def _(sp):
                for b0, scale in groups:
                    with sp.Fori(0, 2) as i:
                        for s in range(2):
                            sp.wait_ge(out_ready[s], 1).then_inc(out_ready[s], -1)
                            sp.dma_start(qkv_dram[bass.ds(2 * i + s + b0, 1), :, :].rearrange("o p n -> p o n"),
                                         z[s][:, :].rearrange("p (o n) -> p o n", o=1)).then_inc(stored[s], 16)
                for s in range(2):
                    sp.wait_ge(stored[s], 16)


def window_prepare(nc, a, sb, pa, k_dup, v_tok):
    with Stage(nc, "wprep") as st:
        names = ("swap", "dup0", "dup1", "dupswap0", "dupswap1")
        m = {n: st.sb(n, P, P) for n in names}
        cos, sin = st.sb("cos", P, TOK), st.sb("sin", P, TOK)
        tmp = [st.sb(f"tmp{i}", P, 512) for i in range(2)]
        rot = [st.ps(f"rot{j}", P, 512) for j in range(4)]
        vt = [st.ps(f"vt{j}", P, 512) for j in range(3)]
        loaded, full, free, step, v_full = st.sem("loaded"), st.sem("full", 4), st.sem("free", 4), st.sem("step"), st.sem("v_full")
        q_free = st.sem("q_free")
        with nc.Block() as block:
            @block.sync
            def _(sp):
                for n in names:
                    sp.dma_start(m[n][:, :], a["mats"][MATS.index(n)]).then_inc(loaded, 16)
                sp.dma_start(cos[:, :], a["rope_a"][0]).then_inc(loaded, 16)
                sp.dma_start(sin[:, :], a["rope_a"][1]).then_inc(loaded, 16)

            @block.tensor
            def _(pe):
                pe.wait_ge(loaded, 112)
                with pe.Fori(0, 4) as b:
                    for j, (t0, n) in enumerate(ALL_CHUNKS):
                        pe.wait_ge(free[j], 1).then_inc(free[j], -1)
                        pe.matmul(rot[j][:, 0:n], m["swap"][:, :], pa[:, bass.ds(b, 1), t0:t0 + n].rearrange("p o n -> p (o n)"), start=True, stop=True).then_inc(full[j], 1)
                for kv in range(2):
                    for j, (t0, n) in enumerate(ALL_CHUNKS):
                        for h, name in enumerate((f"dup{kv}", f"dupswap{kv}")):
                            r = (2 * j + h) % 4
                            pe.wait_ge(free[r], 1).then_inc(free[r], -1)
                            pe.matmul(rot[r][:, 0:n], m[name][:, :], pa[:, 4, t0:t0 + n], start=True, stop=True).then_inc(full[r], 1)
                for t in range(NT):
                    mm = pe.transpose(vt[t // 4][:, t % 4 * P:(t % 4 + 1) * P], pa[:, 5, t * P:(t + 1) * P], sb["ident"][:, :])
                mm.then_inc(v_full, 1)

            @block.vector
            def _(dve):
                def done(ins, n=1):
                    ins.then_inc(step, 1)
                    dve.wait_ge(step, 1).then_inc(step, -1)

                give(dve, free)
                dve.wait_ge(loaded, 112)
                with dve.Fori(0, 4) as b:
                    for j, (t0, n) in enumerate(ALL_CHUNKS):
                        q = pa[:, bass.ds(b, 1), t0:t0 + n]
                        w = lambda ap: ap.rearrange("p (o n) -> p o n", o=1)
                        dve.wait_ge(full[j], 1).then_inc(full[j], -1)
                        done(dve.tensor_tensor(tmp[0][:, 0:n], rot[j][:, 0:n], sin[:, t0:t0 + n], ALU.mult))
                        done(dve.tensor_tensor(q, q, w(cos[:, t0:t0 + n]), ALU.mult))
                        done(dve.tensor_tensor(q, q, w(tmp[0][:, 0:n]), ALU.add))
                        dve.sem_inc(free[j], 1)
                for kv in range(2):
                    dve.memset(k_dup[:, kv, 0:P], 0.0)
                    dve.memset(k_dup[:, kv, P + TOK:], 0.0)
                    for j, (t0, n) in enumerate(ALL_CHUNKS):
                        r = (2 * j) % 4
                        dve.wait_ge(full[r], 1).then_inc(full[r], -1)
                        done(dve.tensor_tensor(tmp[0][:, 0:n], rot[r][:, 0:n], cos[:, t0:t0 + n], ALU.mult))
                        dve.sem_inc(free[r], 1)
                        dve.wait_ge(full[r + 1], 1).then_inc(full[r + 1], -1)
                        done(dve.tensor_tensor(tmp[1][:, 0:n], rot[r + 1][:, 0:n], sin[:, t0:t0 + n], ALU.mult))
                        dve.sem_inc(free[r + 1], 1)
                        done(dve.tensor_tensor(k_dup[:, kv, P + t0:P + t0 + n], tmp[0][:, 0:n], tmp[1][:, 0:n], ALU.add))
                dve.memset(v_tok[:, 0, :], 0.0)
                dve.memset(v_tok[:, NT + 1, :], 0.0)
                dve.wait_ge(v_full, 1).then_inc(v_full, -1)
                for j, (t0, n) in enumerate(ALL_CHUNKS):
                    dve.tensor_copy(v_tok[:, 1 + 4 * j:1 + 4 * j + n // P, :], vt[j][:, 0:n].rearrange("p (t d) -> p t d", d=P))


def window_attention(nc, a, sb, pa, k_dup, v_tok, x):
    W = 3 * P
    KEYS = CTX_LEN + W
    scale = float(A_DIM) ** -0.5
    with Stage(nc, "watt") as st:
        q = [st.sb(f"q{s}", P, 4, P) for s in range(2)]
        k = [st.sb(f"k{s}", P, A_KV, W) for s in range(2)]
        mask = [st.sb(f"mask{s}", P, W) for s in range(2)]
        sink = st.sb("sink", P, A_HEADS)
        s_sb = [st.sb(f"s{s}", P, KEYS) for s in range(2)]
        p_t = [st.sb(f"pt{s}", P, KEYS) for s in range(2)]
        stat = st.sb("stat", P, 2, 8)
        o_tok = [st.sb(f"o{s}", P, 4 * P) for s in range(2)]
        s_ps = [st.ps(f"sps{s}", P, 1024) for s in range(2)]
        t_ps = st.ps("tps", P, 1024)
        o_ps = [st.ps(f"ops{s}", P, 512) for s in range(2)]
        q_in, q_free = st.sem("q_in", 2), st.sem("q_free", 2)
        sink_in = st.sem("sink_in")
        s_full, s_free, s_scaled = st.sem("s_full", 2), st.sem("s_free", 2), st.sem("s_scaled", 2)
        p_full, pt_free, t_full, t_read, pt_full = st.sem("p_full", 2), st.sem("pt_free", 2), st.sem("t_full"), st.sem("t_read"), st.sem("pt_full", 2)
        o_full, o_free, sums = st.sem("o_full", 2), st.sem("o_free", 2), st.sem("sums", 2)
        step, act_step, neg_max, sexp_free, p_used = st.sem("step"), st.sem("act_step"), st.sem("neg_max", 2), st.sem("sexp_free", 2), st.sem("p_used", 2)
        o_done, ot_full, ot_free = st.sem("o_done", 2), st.sem("ot_full", 2), st.sem("ot_free", 2)
        C0 = 512 - CTX_LEN

        with nc.Block() as block:
            @block.sync
            def _(sp):
                sp.dma_start(sink[:, :], a["ab_sink"].to_broadcast([P, A_HEADS])).then_inc(sink_in, 16)
                with sp.Fori(0, NT // 2) as i:
                    for s in range(2):
                        t = 2 * i + s
                        sp.wait_ge(q_free[s], 1).then_inc(q_free[s], -1)
                        sp.dma_start(q[s][:, :, :], pa[:, 0:4, bass.ds(t * P, P)]).then_inc(q_in[s], 16)
                        sp.dma_start(k[s][:, :, :], k_dup[:, :, bass.ds(t * P, W)]).then_inc(q_in[s], 16)
                        sp.dma_start(mask[s][:, :], a["window"][bass.ds(t, 1), :, :].rearrange("o p n -> p (o n)")).then_inc(q_in[s], 16)

            @block.tensor
            def _(pe):
                def scores(s, h):
                    r, kv, lo = h % 2, h // (A_HEADS // A_KV), (h % 2) * A_DIM
                    pe.wait_ge(s_free[r], 1).then_inc(s_free[r], -1)
                    qh = q[s][lo:lo + A_DIM, h // 2, :]
                    pe.matmul(s_ps[r][:, C0:512], qh, k_dup[lo:lo + A_DIM, kv, P:P + CTX_LEN], start=True, stop=True)
                    pe.matmul(s_ps[r][:, 512:512 + W], qh, k[s][lo:lo + A_DIM, kv, :], start=True, stop=True).then_inc(s_full[r], 1)

                def values(s, h, t):
                    r, kv = h % 2, h // (A_HEADS // A_KV)
                    pe.wait_ge(p_full[r], 1).then_inc(p_full[r], -1)
                    pe.wait_ge(t_read, 1).then_inc(t_read, -1)
                    for j in range(KEYS // P):
                        mm = pe.transpose(t_ps[:, j * P:(j + 1) * P], s_sb[r][:, j * P:(j + 1) * P], sb["ident"][:, :])
                    mm.then_inc(t_full, 1)
                    pe.wait_ge(pt_full[r], 1).then_inc(pt_full[r], -1)
                    pe.wait_ge(o_free[r], 1).then_inc(o_free[r], -1)
                    for j in range(KEYS // P):
                        v = (v_tok[:, 1 + j, kv * A_DIM:(kv + 1) * A_DIM] if j < CT
                             else v_tok[:, bass.ds(t + (j - CT), 1), kv * A_DIM:(kv + 1) * A_DIM].rearrange("p o n -> p (o n)"))
                        mm = pe.matmul(o_ps[r][:, 0:A_DIM], p_t[r][:, j * P:(j + 1) * P], v, start=(j == 0), stop=(j == KEYS // P - 1))
                    mm.then_inc(o_full[r], 1)

                with pe.Fori(0, NT // 2) as i:
                    for s in range(2):
                        t = 2 * i + s
                        pe.wait_ge(q_in[s], 48).then_inc(q_in[s], -48)
                        scores(s, 0)
                        for h in range(A_HEADS):
                            if h + 1 < A_HEADS:
                                scores(s, h + 1)
                            values(s, h, t)
                        pe.wait_ge(o_done[s], 1).then_inc(o_done[s], -1)
                        pe.wait_ge(t_read, 1).then_inc(t_read, -1)
                        for b in range(4):
                            mm = pe.transpose(t_ps[:, b * P:(b + 1) * P], o_tok[s][:, b * P:(b + 1) * P], sb["ident"][:, :])
                        mm.then_inc(ot_full[s], 1)

            @block.vector
            def _(dve):
                def done(ins):
                    ins.then_inc(step, 1)
                    dve.wait_ge(step, 1).then_inc(step, -1)

                give(dve, q_free)
                give(dve, s_free)
                give(dve, o_free)
                give(dve, [t_read])
                dve.wait_ge(sink_in, 16)

                def scaled(s, h):
                    r = h % 2
                    dve.wait_ge(s_full[r], 1).then_inc(s_full[r], -1)
                    dve.wait_ge(p_used[r], 1).then_inc(p_used[r], -1)
                    dve.tensor_scalar(s_sb[r][:, 0:CTX_LEN], s_ps[r][:, C0:512], scale, None, ALU.mult).then_inc(step, 1)
                    dve.scalar_tensor_tensor(out=s_sb[r][:, CTX_LEN:], in0=s_ps[r][:, 512:512 + W], scalar=scale, in1=mask[s][:, :],
                                             op0=ALU.mult, op1=ALU.add).then_inc(step, 1)
                    dve.wait_ge(step, 2).then_inc(step, -2)
                    dve.sem_inc(s_free[r], 1)
                    if h == A_HEADS - 1:
                        dve.sem_inc(q_free[s], 1)
                    done(dve.tensor_reduce(stat[:, r, 0:1], s_sb[r][:, :], AX_X, ALU.max))
                    done(dve.tensor_tensor(stat[:, r, 0:1], stat[:, r, 0:1], sink[:, h:h + 1], ALU.max))
                    done(dve.tensor_scalar(stat[:, r, 1:2], stat[:, r, 0:1], -1.0, None, ALU.mult))
                    dve.sem_inc(neg_max[r], 1)

                def weighted(s, h):
                    r = h % 2
                    dve.wait_ge(t_full, 1).then_inc(t_full, -1)
                    dve.sem_inc(p_used[r], 1)
                    done(dve.tensor_copy(p_t[r][:, :], t_ps[:, 0:KEYS]))
                    dve.sem_inc(t_read, 1)
                    dve.sem_inc(pt_full[r], 1)
                    dve.wait_ge(sums[r], 1).then_inc(sums[r], -1)
                    done(dve.tensor_tensor(stat[:, r, 4:5], stat[:, r, 2:3], stat[:, r, 3:4], ALU.add))
                    done(dve.reciprocal(stat[:, r, 5:6], stat[:, r, 4:5]))
                    dve.wait_ge(o_full[r], 1).then_inc(o_full[r], -1)
                    done(dve.tensor_scalar(o_tok[s][:, h * A_DIM:(h + 1) * A_DIM], o_ps[r][:, 0:A_DIM], stat[:, r, 5:6], None, ALU.mult))
                    dve.sem_inc(o_free[r], 1)

                give(dve, p_used)
                with dve.Fori(0, NT // 2) as i:
                    for s in range(2):
                        t = 2 * i + s
                        scaled(s, 0)
                        for h in range(A_HEADS):
                            if h + 1 < A_HEADS:
                                scaled(s, h + 1)
                            weighted(s, h)
                        dve.sem_inc(o_done[s], 1)
                        dve.wait_ge(ot_full[s], 1).then_inc(ot_full[s], -1)
                        done(dve.tensor_copy(x[:, 0:4, bass.ds(t * P, P)], t_ps[:, 0:4 * P].rearrange("p (b n) -> p b n", b=4)))
                        dve.sem_inc(t_read, 1)

            @block.scalar
            def _(act):
                act.wait_ge(sink_in, 16)
                with act.Fori(0, NT // 2) as i:
                    for s in range(2):
                        for h in range(A_HEADS):
                            r = h % 2
                            act.wait_ge(neg_max[r], 1).then_inc(neg_max[r], -1)
                            act.activation(stat[:, r, 3:4], sink[:, h:h + 1], ACT.Exp, bias=stat[:, r, 1:2]).then_inc(act_step, 1)
                            act.activation(s_sb[r][:, :], s_sb[r][:, :], ACT.Exp, bias=stat[:, r, 1:2],
                                           accum_out=stat[:, r, 2:3]).then_inc(act_step, 1)
                            act.wait_ge(act_step, 2).then_inc(act_step, -2)
                            act.sem_inc(p_full[r], 1)
                            act.sem_inc(sums[r], 1)


def delta_rule(nc, a, sb, qkv_dram, cols, o_dirs):
    HP = [P, B_HEADS, P]
    with Stage(nc, "delta") as st:
        levels = [[st.sb(f"level{d}{l}", P, P) for l in range(LEVELS)] for d in range(2)]
        cum = [st.sb(f"cum{d}", P, P) for d in range(2)]
        dmask = [st.sb(f"dmask{d}", P, P) for d in range(2)]
        qkv = [[st.sb(f"qkv{d}{s}", P, 12, P) for s in range(2)] for d in range(2)]
        names = ("ld", "col", "dec", "egrow", "b", "aqk", "uu", "vv", "ww", "ktok", "vtok", "vn", "vt", "state")
        t = [{n: st.sb(f"{n}{d}", P, 6, B_HEADS) if n == "col" else st.sb(f"{n}{d}", *HP) for n in names} for d in range(2)]
        bank = [[st.ps(f"bank{d}{j}", *HP) for j in range(4)] for d in range(2)]
        E = lambda n: st.sem(n, 2)
        loaded = st.sem("loaded")
        qkv_in = [st.sem(f"qkv_in{d}", 2) for d in range(2)]
        qkv_free = [st.sem(f"qkv_free{d}", 2) for d in range(2)]
        ld_full, ld_free, col_full, col_free, pool_step = E("ld_full"), E("ld_free"), E("col_full"), E("col_free"), st.sem("pool_step")
        grow_full, grow_read, decay_raw, decay_full, egrow_full = E("grow_full"), E("grow_read"), E("decay_raw"), E("decay_full"), E("egrow_full")
        tok_copied, kk_full, kq_full, tok_full, tok_read, vtok_full = E("tok_copied"), E("kk_full"), E("kq_full"), E("tok_full"), E("tok_read"), E("vtok_full")
        b_full, w_psum, w_full, v_psum, u_psum, uv_full = E("b_full"), E("w_psum"), E("w_full"), E("v_psum"), E("u_psum"), E("uv_full")
        ks_full, r_full, vn_psum, vn_full = E("ks_full"), E("r_full"), E("vn_psum"), E("vn_full")
        o_full, o_read, s_psum, s_full = E("o_full"), E("o_read"), E("s_psum"), E("s_full")
        step, act_step = st.sem("step"), st.sem("act_step")

        def bc(m):
            return m[:, :].rearrange("p (o n) -> p o n", o=1).to_broadcast(HP)

        def per_head(d, kind):
            return t[d]["col"][:, kind, :].rearrange("p (h o) -> p h o", o=1).to_broadcast(HP)

        def over_chunks(eng, body):
            for s in range(CT):
                body(s, (s, CT - 1 - s))
            with eng.Fori(0, LT // 2) as i:
                for s in range(2):
                    body(s, (2 * i + s + CT, NT - 1 - s - 2 * i))

        with nc.Block() as block:
            @block.sync
            def _(sp):
                for d in range(2):
                    for l in range(LEVELS):
                        sp.dma_start(levels[d][l][:, :], a["mats"][MATS.index(f"level{d}_{l}")]).then_inc(loaded, 16)
                    sp.dma_start(cum[d][:, :], a["mats"][MATS.index(f"cum{d}")]).then_inc(loaded, 16)
                    sp.dma_start(dmask[d][:, :], a["mats"][MATS.index(f"decay_mask{d}")]).then_inc(loaded, 16)

                def load(s, tiles):
                    for d in range(2):
                        sp.wait_ge(qkv_free[d][s], 1).then_inc(qkv_free[d][s], -1)
                        sp.dma_start(qkv[d][s][:, :, :], qkv_dram.rearrange("b p n -> p b n")[:, :, bass.ds(tiles[d] * P, P)]).then_inc(qkv_in[d][s], 16)
                over_chunks(sp, load)

            @block.gpsimd
            def _(pool):
                def spread(s, tiles):
                    for d in range(2):
                        pool.wait_ge(col_free[d], 1).then_inc(col_free[d], -1)
                        pool.tensor_copy(t[d]["col"][:, :, :].rearrange("p k h -> p (k h)"),
                                         cols[:, bass.ds(tiles[d], 1), d, :, :].rearrange("p o k h -> p (o k h)")).then_inc(pool_step, 1)
                        pool.wait_ge(pool_step, 1).then_inc(pool_step, -1)
                        pool.sem_inc(col_full[d], 1)
                        pool.wait_ge(ld_free[d], 1).then_inc(ld_free[d], -1)
                        pool.tensor_copy(t[d]["ld"][:, :, :], per_head(d, 0)).then_inc(ld_full[d], 1)
                over_chunks(pool, spread)

            @block.tensor
            def _(pe):
                pe.wait_ge(loaded, 16 * 2 * (LEVELS + 2))

                def heads4(d, j, lhs, rhs, start=True, stop=True):
                    for h in range(B_HEADS):
                        mm = pe.matmul(bank[d][j][:, h, :], lhs(h), rhs(h), start=start, stop=stop)
                    return mm

                def chunk(s, tiles):
                    T = lambda d, n: (lambda h: t[d][n][:, h, :])
                    Q = lambda d: (lambda h: qkv[d][s][:, h, :])
                    K = lambda d: (lambda h: qkv[d][s][:, B_HEADS + h, :])
                    ident = lambda h: sb["ident"][:, :]
                    for d in range(2):
                        pe.wait_ge(ld_full[d], 1).then_inc(ld_full[d], -1)
                        pe.wait_ge(o_read[d], 1).then_inc(o_read[d], -1)
                        heads4(d, 0, T(d, "ld"), lambda h: cum[d][:, :]).then_inc(grow_full[d], 1)
                    for d in range(2):
                        pe.wait_ge(qkv_in[d][s], 16).then_inc(qkv_in[d][s], -16)
                        heads4(d, 1, K(d), K(d)).then_inc(kk_full[d], 1)
                        heads4(d, 2, K(d), Q(d)).then_inc(kq_full[d], 1)
                        pe.wait_ge(s_full[d], 1).then_inc(s_full[d], -1)
                        for h in range(B_HEADS):
                            pe.transpose(bank[d][3][:, h, :], K(d)(h), sb["ident"][:, :])
                        pe.wait_ge(grow_read[d], 1).then_inc(grow_read[d], -1)
                        for h in range(B_HEADS):
                            mm = pe.transpose(bank[d][0][:, h, :], qkv[d][s][:, 2 * B_HEADS + h, :], sb["ident"][:, :])
                        mm.then_inc(tok_full[d], 1)
                    for d in range(2):
                        pe.wait_ge(b_full[d], 1).then_inc(b_full[d], -1)
                        heads4(d, 1, T(d, "b"), ident).then_inc(w_psum[d], 1)
                    for l in range(1, LEVELS):
                        for d in range(2):
                            pe.wait_ge(uv_full[d], 1).then_inc(uv_full[d], -1)
                            if l == 1:
                                pe.wait_ge(tok_read[d], 1).then_inc(tok_read[d], -1)
                            heads4(d, 2, T(d, "b"), T(d, "vv")).then_inc(w_psum[d], 1)
                        for d in range(2):
                            pe.wait_ge(w_full[d], 1).then_inc(w_full[d], -1)
                            if l == 1:
                                pe.wait_ge(tok_copied[d], 1).then_inc(tok_copied[d], -1)
                            if l < LEVELS - 1:
                                heads4(d, 1, T(d, "uu"), T(d, "ww")).then_inc(v_psum[d], 1)
                            heads4(d, 3, T(d, "ww"), T(d, "uu")).then_inc(u_psum[d], 1)
                    for d in range(2):
                        heads4(d, 1, K(d), T(d, "state")).then_inc(ks_full[d], 1)
                    for d in range(2):
                        pe.wait_ge(r_full[d], 1).then_inc(r_full[d], -1)
                        heads4(d, 2, T(d, "uu"), T(d, "vv")).then_inc(vn_psum[d], 1)
                    for d in range(2):
                        pe.wait_ge(vn_full[d], 1).then_inc(vn_full[d], -1)
                        for h in range(B_HEADS):
                            pe.matmul(bank[d][0][:, h, :], t[d]["state"][:, h, :], t[d]["egrow"][:, h, :], start=True, stop=False)
                            mm = pe.matmul(bank[d][0][:, h, :], t[d]["vn"][:, h, :], t[d]["aqk"][:, h, :], start=False, stop=True)
                        mm.then_inc(o_full[d], 1)
                        heads4(d, 3, T(d, "ktok"), T(d, "vt")).then_inc(s_psum[d], 1)
                over_chunks(pe, chunk)

            @block.vector
            def _(dve):
                def done(ins, *to):
                    ins.then_inc(step, 1)
                    dve.wait_ge(step, 1).then_inc(step, -1)
                    for x in to:
                        dve.sem_inc(x, 1)

                dve.wait_ge(loaded, 16 * 2 * (LEVELS + 2))
                for d in range(2):
                    give(dve, qkv_free[d])
                    dve.memset(t[d]["state"][:, :, :], 0.0).then_inc(step, 1)
                dve.wait_ge(step, 2).then_inc(step, -2)
                for g in (col_free, ld_free, o_read, s_full):
                    give(dve, g)

                def chunk(s, tiles):
                    for d in range(2):
                        x = t[d]
                        dve.wait_ge(col_full[d], 1).then_inc(col_full[d], -1)
                        dve.wait_ge(grow_full[d], 1).then_inc(grow_full[d], -1)
                        dve.sem_inc(ld_free[d], 1)
                        for h in range(B_HEADS):
                            dve.scalar_tensor_tensor(out=x["dec"][:, h, :], in0=bank[d][0][:, h, :], scalar=x["col"][:, 1, h:h + 1],
                                                     in1=dmask[d][:, :], op0=ALU.subtract, op1=ALU.add).then_inc(step, 1)
                        dve.wait_ge(step, B_HEADS).then_inc(step, -B_HEADS)
                        dve.sem_inc(decay_raw[d], 1)
                    for d in range(2):
                        x = t[d]
                        dve.wait_ge(kk_full[d], 1).then_inc(kk_full[d], -1)
                        dve.wait_ge(decay_full[d], 1).then_inc(decay_full[d], -1)
                        for h in range(B_HEADS):
                            dve.scalar_tensor_tensor(out=x["b"][:, h, :], in0=bank[d][1][:, h, :], scalar=x["col"][:, 2, h:h + 1],
                                                     in1=x["dec"][:, h, :], op0=ALU.mult, op1=ALU.mult).then_inc(step, 1)
                        dve.wait_ge(step, B_HEADS).then_inc(step, -B_HEADS)
                        dve.sem_inc(b_full[d], 1)
                        done(dve.tensor_tensor(x["uu"][:, :, :], x["b"][:, :, :], bc(levels[1 - d][0]), ALU.mult))
                        done(dve.scalar_tensor_tensor(out=x["uu"][:, :, :], in0=x["uu"][:, :, :], scalar=-1.0, in1=bc(sb["ident"]), op0=ALU.mult, op1=ALU.add))
                    for d in range(2):
                        x = t[d]
                        dve.wait_ge(w_psum[d], 1).then_inc(w_psum[d], -1)
                        done(dve.tensor_tensor(x["vv"][:, :, :], bank[d][1][:, :, :], bc(levels[d][0]), ALU.mult))
                        done(dve.scalar_tensor_tensor(out=x["vv"][:, :, :], in0=x["vv"][:, :, :], scalar=-1.0, in1=bc(sb["ident"]), op0=ALU.mult, op1=ALU.add), uv_full[d])
                    for d in range(2):
                        x = t[d]
                        dve.wait_ge(kq_full[d], 1).then_inc(kq_full[d], -1)
                        done(dve.tensor_tensor(x["aqk"][:, :, :], bank[d][2][:, :, :], x["dec"][:, :, :], ALU.mult), tok_read[d])
                        dve.wait_ge(egrow_full[d], 1).then_inc(egrow_full[d], -1)
                        done(dve.tensor_tensor(x["egrow"][:, :, :], qkv[d][s][:, 0:B_HEADS, :], x["egrow"][:, :, :], ALU.mult))
                    for l in range(1, LEVELS):
                        for d in range(2):
                            dve.wait_ge(w_psum[d], 1).then_inc(w_psum[d], -1)
                            done(dve.tensor_tensor(t[d]["ww"][:, :, :], bank[d][2][:, :, :], bc(levels[d][l]), ALU.mult), w_full[d])
                        for d in range(2):
                            x = t[d]
                            if l < LEVELS - 1:
                                dve.wait_ge(v_psum[d], 1).then_inc(v_psum[d], -1)
                                done(dve.tensor_tensor(x["vv"][:, :, :], x["vv"][:, :, :], bank[d][1][:, :, :], ALU.subtract))
                            dve.wait_ge(u_psum[d], 1).then_inc(u_psum[d], -1)
                            done(dve.tensor_tensor(x["uu"][:, :, :], x["uu"][:, :, :], bank[d][3][:, :, :], ALU.subtract))
                            if l < LEVELS - 1:
                                dve.sem_inc(uv_full[d], 1)
                    for d in range(2):
                        x = t[d]
                        dve.wait_ge(ks_full[d], 1).then_inc(ks_full[d], -1)
                        dve.wait_ge(vtok_full[d], 1).then_inc(vtok_full[d], -1)
                        dve.sem_inc(qkv_free[d][s], 1)
                        for h in range(B_HEADS):
                            dve.scalar_tensor_tensor(out=x["vv"][:, h, :], in0=bank[d][1][:, h, :], scalar=x["col"][:, 3, h:h + 1],
                                                     in1=x["vtok"][:, h, :], op0=ALU.mult, op1=ALU.add).then_inc(step, 1)
                        dve.wait_ge(step, B_HEADS).then_inc(step, -B_HEADS)
                        dve.sem_inc(r_full[d], 1)
                    for d in range(2):
                        x = t[d]
                        dve.wait_ge(vn_psum[d], 1).then_inc(vn_psum[d], -1)
                        done(dve.tensor_tensor(x["vn"][:, :, :], bank[d][2][:, :, :], per_head(d, 2), ALU.mult))
                        done(dve.tensor_tensor(x["vt"][:, :, :], bank[d][2][:, :, :], per_head(d, 4), ALU.mult), vn_full[d])
                    for d in range(2):
                        x = t[d]
                        dve.wait_ge(s_psum[d], 1).then_inc(s_psum[d], -1)
                        for h in range(B_HEADS):
                            dve.scalar_tensor_tensor(out=x["state"][:, h, :], in0=x["state"][:, h, :], scalar=x["col"][:, 5, h:h + 1],
                                                     in1=bank[d][3][:, h, :], op0=ALU.mult, op1=ALU.add).then_inc(step, 1)
                        dve.wait_ge(step, B_HEADS).then_inc(step, -B_HEADS)
                        dve.sem_inc(s_full[d], 1)
                        dve.sem_inc(col_free[d], 1)
                over_chunks(dve, chunk)

            @block.scalar
            def _(act):
                def done(ins, *to):
                    ins.then_inc(act_step, 1)
                    act.wait_ge(act_step, 1).then_inc(act_step, -1)
                    for x in to:
                        act.sem_inc(x, 1)

                def chunk(s, tiles):
                    for d in range(2):
                        x = t[d]
                        act.wait_ge(decay_raw[d], 1).then_inc(decay_raw[d], -1)
                        done(act.activation(x["egrow"][:, :, :], bank[d][0][:, :, :], ACT.Exp), grow_read[d], egrow_full[d])
                        done(act.activation(x["dec"][:, :, :], x["dec"][:, :, :], ACT.Exp), decay_full[d])
                    for d in range(2):
                        x = t[d]
                        act.wait_ge(tok_full[d], 1).then_inc(tok_full[d], -1)
                        act.activation(x["ktok"][:, :, :], bank[d][3][:, :, :], ACT.Copy).then_inc(act_step, 1)
                        act.activation(x["vtok"][:, :, :], bank[d][0][:, :, :], ACT.Copy).then_inc(act_step, 1)
                        act.wait_ge(act_step, 2).then_inc(act_step, -2)
                        act.sem_inc(vtok_full[d], 1)
                        act.sem_inc(tok_copied[d], 1)
                    for d in range(2):
                        act.wait_ge(o_full[d], 1).then_inc(o_full[d], -1)
                        done(act.activation(o_dirs[d][:, :, bass.ds(tiles[d] * P, P)], bank[d][0][:, :, :], ACT.Copy), o_read[d])
                over_chunks(act, chunk)


def head_norm(nc, a, sb, o_f, o_b, gate):
    g_lo, _ = rows_at(ROWS_A, "out_norm")
    with Stage(nc, "hnorm") as st:
        sq = [st.sb(f"sq{s}", P, TOK) for s in range(2)]
        rt, sg = ([st.sb(f"{n}{h}", P, TOK) for h in range(B_HEADS)] for n in ("rt", "sg"))
        eps = st.sb("eps", P, 1)
        ss = [[st.ps(f"ss{s}{j}", P, 512) for j in range(3)] for s in range(2)]
        eps_set, sum_full, sq_full, ss_full, rt_full, sg_full, step = (st.sem(n) for n in
            ("eps_set", "sum_full", "sq_full", "ss_full", "rt_full", "sg_full", "step"))
        act_step = st.sem("act_step")
        with nc.Block() as block:
            @block.vector
            def _(dve):
                dve.memset(eps[:, :], EPS).then_inc(eps_set, 1)
                for h in range(B_HEADS):
                    dve.tensor_tensor(o_f[:, h, :], o_f[:, h, :], o_b[:, h, :], ALU.add).then_inc(sum_full, 1)
                for h in range(B_HEADS):
                    dve.wait_ge(rt_full, 1).then_inc(rt_full, -1)
                    dve.reciprocal(rt[h][:, :], rt[h][:, :]).then_inc(step, 1)
                    dve.wait_ge(step, 1).then_inc(step, -1)
                    dve.scalar_tensor_tensor(out=o_f[:, h, :], in0=o_f[:, h, :], scalar=sb["cols_a"][:, g_lo:g_lo + 1],
                                             in1=rt[h][:, :], op0=ALU.mult, op1=ALU.mult).then_inc(step, 1)
                    dve.wait_ge(step, 1).then_inc(step, -1)
                    dve.wait_ge(sg_full, 1).then_inc(sg_full, -1)
                    dve.tensor_tensor(o_f[:, h, :], o_f[:, h, :], sg[h][:, :], ALU.mult).then_inc(step, 1)
                    dve.wait_ge(step, 1).then_inc(step, -1)

            @block.scalar
            def _(act):
                act.wait_ge(eps_set, 1)
                for h in range(B_HEADS):
                    s = h % 2
                    act.wait_ge(sum_full, h + 1)
                    act.activation(sq[s][:, :], o_f[:, h, :], ACT.Square).then_inc(sq_full, 1)
                    act.wait_ge(ss_full, h + 1)
                    for j, (t0, n) in enumerate(ALL_CHUNKS):
                        act.activation(rt[h][:, t0:t0 + n], ss[s][j][:, 0:n], ACT.Sqrt, scale=1.0 / B_DIM, bias=eps[:, :]).then_inc(act_step, 1)
                    act.wait_ge(act_step, 3).then_inc(act_step, -3)
                    act.sem_inc(rt_full, 1)
                for h in range(B_HEADS):
                    act.activation(sg[h][:, :], gate[:, h, :], ACT.Silu).then_inc(sg_full, 1)

            @block.tensor
            def _(pe):
                for h in range(B_HEADS):
                    s = h % 2
                    pe.wait_ge(sq_full, h + 1)
                    for j, (t0, n) in enumerate(ALL_CHUNKS):
                        mm = pe.matmul(ss[s][j][:, 0:n], sb["ones"][:, :], sq[s][:, t0:t0 + n], start=True, stop=True)
                    mm.then_inc(ss_full, 1)


def latent_norms(nc, a, sb, c5, kpe, kpe_rot):
    q_lo, _ = rows_at(ROWS_A, "q_norm")
    with Stage(nc, "lnorm") as st:
        sq = [st.sb(f"sq{b}", P, TOK) for b in range(5)]
        rt = st.sb("rt", P, 2, TOK)
        place, swap = st.sb("place", P, P), st.sb("swap", P, P)
        cos, sin = st.sb("cos", P, TOK), st.sb("sin", P, TOK)
        tmp = [st.sb(f"tmp{i}", P, 512) for i in range(2)]
        eps = st.sb("eps", P, 1)
        ss = [[st.ps(f"ss{g}{j}", P, 512) for j in range(3)] for g in range(2)]
        rot = [st.ps(f"rot{i}", P, 512) for i in range(2)]
        loaded, eps_set, sq_full, ss_full, act_step, rt_full, step, rot_full, rot_free = (st.sem(n) for n in
            ("loaded", "eps_set", "sq_full", "ss_full", "act_step", "rt_full", "step", "rot_full", "rot_free"))
        groups = ((range(0, 3), QR, LAT_CHUNKS), (range(3, 5), KVR, ALL_CHUNKS))
        rr = slice(C_NOPE, C_QK)
        with nc.Block() as block:
            @block.sync
            def _(sp):
                sp.dma_start(place[:, :], a["mats"][MATS.index("kpe_place")]).then_inc(loaded, 16)
                sp.dma_start(swap[:, :], a["mats"][MATS.index("kpe_swap")]).then_inc(loaded, 16)
                sp.dma_start(cos[:, :], a["rope_c"][0]).then_inc(loaded, 16)
                sp.dma_start(sin[:, :], a["rope_c"][1]).then_inc(loaded, 16)

            @block.scalar
            def _(act):
                act.wait_ge(eps_set, 1)
                for b in range(5):
                    lo = CTX_LEN if b < 3 else 0
                    act.activation(sq[b][:, lo:], c5[:, b, lo:], ACT.Square).then_inc(sq_full, 1)
                for g, (blocks, rank, chunks) in enumerate(groups):
                    for j, (t0, n) in enumerate(chunks):
                        act.wait_ge(ss_full, 1).then_inc(ss_full, -1)
                        act.activation(rt[:, g, t0:t0 + n], ss[g][j][:, 0:n], ACT.Sqrt, scale=1.0 / rank, bias=eps[:, :]).then_inc(rt_full, 1)

            @block.tensor
            def _(pe):
                for g, (blocks, rank, chunks) in enumerate(groups):
                    pe.wait_ge(sq_full, blocks[-1] + 1)
                    for j, (t0, n) in enumerate(chunks):
                        for b in blocks:
                            mm = pe.matmul(ss[g][j][:, 0:n], sb["ones"][:, :], sq[b][:, t0:t0 + n], start=(b == blocks[0]), stop=(b == blocks[-1]))
                        mm.then_inc(ss_full, 1)
                pe.wait_ge(loaded, 64)
                for j, (t0, n) in enumerate(ALL_CHUNKS):
                    pe.wait_ge(rot_free, 1).then_inc(rot_free, -1)
                    pe.matmul(rot[0][:, 0:n], place[0:C_ROPE, :], kpe[:, 0, t0:t0 + n], start=True, stop=True)
                    pe.matmul(rot[1][:, 0:n], swap[0:C_ROPE, :], kpe[:, 0, t0:t0 + n], start=True, stop=True).then_inc(rot_full, 1)

            @block.vector
            def _(dve):
                def done(ins, n=1):
                    ins.then_inc(step, 1)
                    dve.wait_ge(step, 1).then_inc(step, -1)

                dve.memset(eps[:, :], EPS).then_inc(eps_set, 1)
                dve.wait_ge(loaded, 64)
                give(dve, [rot_free])
                for g, (blocks, rank, chunks) in enumerate(groups):
                    dve.wait_ge(rt_full, len(chunks)).then_inc(rt_full, -len(chunks))
                    lo = chunks[0][0]
                    done(dve.reciprocal(rt[:, g, lo:], rt[:, g, lo:]))
                    for b in blocks:
                        dve.scalar_tensor_tensor(out=c5[:, b, lo:], in0=c5[:, b, lo:], scalar=sb["cols_a"][:, q_lo + b:q_lo + b + 1],
                                                 in1=rt[:, g, lo:], op0=ALU.mult, op1=ALU.mult)
                for j, (t0, n) in enumerate(ALL_CHUNKS):
                    dve.wait_ge(rot_full, 1).then_inc(rot_full, -1)
                    dve.tensor_tensor(tmp[0][rr, 0:n], rot[0][rr, 0:n], cos[rr, t0:t0 + n], ALU.mult).then_inc(step, 1)
                    dve.tensor_tensor(tmp[1][rr, 0:n], rot[1][rr, 0:n], sin[rr, t0:t0 + n], ALU.mult).then_inc(step, 1)
                    dve.wait_ge(step, 2).then_inc(step, -2)
                    dve.sem_inc(rot_free, 1)
                    done(dve.tensor_tensor(kpe_rot[rr, t0:t0 + n], tmp[0][rr, 0:n], tmp[1][rr, 0:n], ALU.add))


def latent_attention(nc, a, sb, c5, kpe_rot, x):
    scale = float(C_QK) ** -0.5
    NQ = LT
    rr = slice(C_NOPE, C_QK)
    with Stage(nc, "latt") as st:
        wq = [st.sb(f"wq{s}", P, 3, C_QK) for s in range(2)]
        wkv = [st.sb(f"wkv{s}", P, 2, C_NOPE + C_V) for s in range(2)]
        q_swap = st.sb("q_swap", P, P)
        cos, sin = st.sb("cos", P, SEQ), st.sb("sin", P, SEQ)
        kt = [st.sb(f"kt{s}", P, TOK) for s in range(2)]
        qt = [st.sb(f"qt{s}", P, SEQ) for s in range(2)]
        vt = [st.sb(f"vt{s}", P, NT, C_V) for s in range(2)]
        prob = [st.sb(f"prob{s}", P, TOK) for s in range(2)]
        prob_t = [st.sb(f"prob_t{s}", P, TOK) for s in range(2)]
        tmp = st.sb("tmp", P, 512)
        o_tok = st.sb("o_tok", P, NQ, 2 * C_V)
        stat = st.sb("stat", P, 2, 8)
        s_ps = [st.ps(f"s{r}", P, 1536) for r in range(2)]
        t_ps = st.ps("t", P, 512)
        o_ps = st.ps("o", P, 512)
        w_in, w_free = st.sem("w_in", 2), st.sem("w_free", 2)
        loaded, kpe_set = st.sem("loaded"), st.sem("kpe_set")
        q_proj, q_copied, rot_full, kv_proj, proj_read = st.sem("q_proj"), st.sem("q_copied"), st.sem("rot_full"), st.sem("kv_proj"), st.sem("proj_read")
        head_ready = st.sem("head_ready", 2)
        s_full, s_free, neg_max, p_full, p_free, sums = (st.sem(n, 2) for n in ("s_full", "s_free", "neg_max", "p_full", "p_free", "sums"))
        t_full, t_free, pt_full, pt_free, o_full, o_free = st.sem("t_full"), st.sem("t_free"), st.sem("pt_full"), st.sem("pt_free", 2), st.sem("o_full"), st.sem("o_free")
        step, act_step, turn_ready, turned = st.sem("step"), st.sem("act_step"), st.sem("turn_ready"), st.sem("turned")
        GR = ((0, 4), (4, 4), (8, 2))

        with nc.Block() as block:
            @block.sync
            def _(sp):
                sp.dma_start(q_swap[:, :], a["mats"][MATS.index("q_swap")]).then_inc(loaded, 16)
                sp.dma_start(cos[:, :], a["rope_c"][0, :, CTX_LEN:]).then_inc(loaded, 16)
                sp.dma_start(sin[:, :], a["rope_c"][1, :, CTX_LEN:]).then_inc(loaded, 16)
                for s in range(2):
                    sp.dma_start(kt[s][rr, :], kpe_rot[rr, :]).then_inc(kpe_set, 16)
                wq_v = a["mla_w_qb"][0].rearrange("(k p) n -> p k n", p=P)
                wkv_v = a["mla_w_kvb"][0].rearrange("(k p) n -> p k n", p=P)
                with sp.Fori(0, C_HEADS // 2) as i:
                    for s in range(2):
                        sp.wait_ge(w_free[s], 1).then_inc(w_free[s], -1)
                        sp.dma_start(wq[s][:, :, :], wq_v[:, :, bass.ds((2 * i + s) * C_QK, C_QK)]).then_inc(w_in[s], 16)
                        sp.dma_start(wkv[s][:, :, :], wkv_v[:, :, bass.ds((2 * i + s) * (C_NOPE + C_V), C_NOPE + C_V)]).then_inc(w_in[s], 16)

            @block.tensor
            def _(pe):
                pe.wait_ge(loaded, 48)
                pe.wait_ge(kpe_set, 32)

                def project_head(s):
                    pe.wait_ge(w_in[s], 32).then_inc(w_in[s], -32)
                    pe.wait_ge(s_free[0], 1).then_inc(s_free[0], -1)
                    pe.wait_ge(s_free[1], 1).then_inc(s_free[1], -1)
                    for j, (t0, n) in enumerate(LAT_CHUNKS):
                        for k in range(3):
                            mm = pe.matmul(s_ps[0][0:C_QK, j * 512:j * 512 + n], wq[s][:, k, :], c5[:, k, t0:t0 + n], start=(k == 0), stop=(k == 2))
                    mm.then_inc(q_proj, 1)
                    for j, (t0, n) in enumerate(ALL_CHUNKS):
                        for k in range(2):
                            mm = pe.matmul(s_ps[1][0:C_NOPE, t0:t0 + n], wkv[s][:, k, 0:C_NOPE], c5[:, 3 + k, t0:t0 + n], start=(k == 0), stop=(k == 1))
                    mm.then_inc(kv_proj, 1)
                    pe.wait_ge(q_copied, 1).then_inc(q_copied, -1)
                    for j, (t0, n) in enumerate(LAT_CHUNKS):
                        mm = pe.matmul(s_ps[0][:, j * 512:j * 512 + n], q_swap[0:C_QK, :], qt[s][0:C_QK, j * 512:j * 512 + n], start=True, stop=True)
                    mm.then_inc(rot_full, 1)
                    pe.wait_ge(proj_read, 1).then_inc(proj_read, -1)
                    for t in range(NT):
                        for k in range(2):
                            mm = pe.matmul(s_ps[1][:, t * C_V:(t + 1) * C_V], c5[:, 3 + k, t * P:(t + 1) * P], wkv[s][:, k, C_NOPE:], start=(k == 0), stop=(k == 1))
                    mm.then_inc(kv_proj, 1)

                def scores(s, qb):
                    r = qb % 2
                    pe.wait_ge(s_free[r], 1).then_inc(s_free[r], -1)
                    for j, (t0, n) in enumerate(ALL_CHUNKS):
                        mm = pe.matmul(s_ps[r][:, t0:t0 + n], qt[s][0:C_QK, qb * P:(qb + 1) * P], kt[s][0:C_QK, t0:t0 + n], start=True, stop=True)
                    mm.then_inc(s_full[r], 1)

                def values(s, qb):
                    r = qb % 2
                    pe.wait_ge(p_full[r], 1).then_inc(p_full[r], -1)
                    for g, (t0, n) in enumerate(GR):
                        pe.wait_ge(t_free, 1).then_inc(t_free, -1)
                        for t in range(t0, t0 + n):
                            mm = pe.transpose(t_ps[:, (t - t0) * P:(t - t0 + 1) * P], prob[r][:, t * P:(t + 1) * P], sb["ident"][:, :])
                        mm.then_inc(t_full, 1)
                    pe.wait_ge(o_free, 1).then_inc(o_free, -1)
                    pe.wait_ge(pt_full, 1).then_inc(pt_full, -1)
                    for t in range(NT):
                        mm = pe.matmul(o_ps[:, 0:C_V], prob_t[r][:, t * P:(t + 1) * P], vt[s][:, t, :], start=(t == 0), stop=(t == NT - 1))
                    mm.then_inc(o_full, 1)

                with pe.Fori(0, C_HEADS // 2) as i:
                    for s in range(2):
                        project_head(s)
                        pe.wait_ge(head_ready[s], 1).then_inc(head_ready[s], -1)
                        scores(s, 0)
                        for qb in range(NQ):
                            if qb + 1 < NQ:
                                scores(s, qb + 1)
                            values(s, qb)
                    pe.wait_ge(turn_ready, 1).then_inc(turn_ready, -1)
                    for b in range(NQ // 4):
                        pe.wait_ge(t_free, 1).then_inc(t_free, -1)
                        for q in range(4):
                            mm = pe.transpose(t_ps[:, q * P:(q + 1) * P], o_tok[:, 4 * b + q, :], sb["ident"][:, :])
                        mm.then_inc(turned, 1)

            @block.vector
            def _(dve):
                def done(ins):
                    ins.then_inc(step, 1)
                    dve.wait_ge(step, 1).then_inc(step, -1)

                dve.wait_ge(loaded, 48)
                for g in (w_free, s_free, p_free):
                    give(dve, g)
                give(dve, [t_free, o_free])

                def head(s):
                    dve.wait_ge(q_proj, 1).then_inc(q_proj, -1)
                    done(dve.tensor_copy(qt[s][0:C_QK, :], s_ps[0][0:C_QK, 0:SEQ]))
                    dve.sem_inc(q_copied, 1)
                    dve.wait_ge(kv_proj, 1).then_inc(kv_proj, -1)
                    done(dve.tensor_copy(kt[s][0:C_NOPE, :], s_ps[1][0:C_NOPE, 0:TOK]))
                    dve.sem_inc(proj_read, 1)
                    dve.wait_ge(rot_full, 1).then_inc(rot_full, -1)
                    for j in range(2):
                        c = slice(j * 512, (j + 1) * 512)
                        done(dve.tensor_tensor(tmp[rr, :], s_ps[0][rr, c], sin[rr, c], ALU.mult))
                        done(dve.tensor_tensor(qt[s][rr, c], qt[s][rr, c], cos[rr, c], ALU.mult))
                        done(dve.tensor_tensor(qt[s][rr, c], qt[s][rr, c], tmp[rr, :], ALU.add))
                    dve.wait_ge(kv_proj, 1).then_inc(kv_proj, -1)
                    dve.sem_inc(w_free[s], 1)
                    done(dve.tensor_copy(vt[s][:, :, :], s_ps[1][:, 0:NT * C_V].rearrange("p (t d) -> p t d", d=C_V)))
                    dve.sem_inc(s_free[0], 1)
                    dve.sem_inc(s_free[1], 1)
                    dve.sem_inc(head_ready[s], 1)

                def maximum(qb):
                    r = qb % 2
                    dve.wait_ge(s_full[r], 1).then_inc(s_full[r], -1)
                    done(dve.tensor_reduce(stat[:, r, 0:1], s_ps[r][:, 0:TOK], AX_X, ALU.max))
                    done(dve.tensor_scalar(stat[:, r, 1:2], stat[:, r, 0:1], -scale, None, ALU.mult))
                    dve.sem_inc(neg_max[r], 1)

                def weighted(s, qb):
                    r = qb % 2
                    for g, (t0, n) in enumerate(GR):
                        dve.wait_ge(t_full, 1).then_inc(t_full, -1)
                        done(dve.tensor_copy(prob_t[r][:, t0 * P:(t0 + n) * P], t_ps[:, 0:n * P]))
                        dve.sem_inc(t_free, 1)
                    dve.sem_inc(p_free[r], 1)
                    dve.sem_inc(pt_full, 1)
                    dve.wait_ge(sums[r], 1).then_inc(sums[r], -1)
                    done(dve.reciprocal(stat[:, r, 5:6], stat[:, r, 4:5]))
                    dve.wait_ge(o_full, 1).then_inc(o_full, -1)
                    done(dve.tensor_scalar(o_tok[:, qb, s * C_V:(s + 1) * C_V], o_ps[:, 0:C_V], stat[:, r, 5:6], None, ALU.mult))
                    dve.sem_inc(o_free, 1)

                with dve.Fori(0, C_HEADS // 2) as i:
                    for s in range(2):
                        head(s)
                        maximum(0)
                        for qb in range(NQ):
                            if qb + 1 < NQ:
                                maximum(qb + 1)
                            weighted(s, qb)
                    dve.sem_inc(turn_ready, 1)
                    for b in range(NQ // 4):
                        dve.wait_ge(turned, 1).then_inc(turned, -1)
                        done(dve.tensor_copy(x[:, bass.ds(i, 1), CTX_LEN + b * 512:CTX_LEN + (b + 1) * 512], t_ps[:, :].rearrange("p (o n) -> p o n", o=1)))
                        dve.sem_inc(t_free, 1)

            @block.scalar
            def _(act):
                with act.Fori(0, C_HEADS // 2) as i:
                    for s in range(2):
                        for qb in range(NQ):
                            r = qb % 2
                            act.wait_ge(neg_max[r], 1).then_inc(neg_max[r], -1)
                            act.wait_ge(p_free[r], 1).then_inc(p_free[r], -1)
                            act.activation(prob[r][:, :], s_ps[r][:, 0:TOK], ACT.Exp, scale=scale, bias=stat[:, r, 1:2],
                                           accum_out=stat[:, r, 4:5]).then_inc(act_step, 1)
                            act.wait_ge(act_step, 1).then_inc(act_step, -1)
                            act.sem_inc(s_free[r], 1)
                            act.sem_inc(p_full[r], 1)
                            act.sem_inc(sums[r], 1)


def program(nc, a, out):
    Stage.used_semaphores = []
    with ExitStack() as ctx:
        def sbt(name, *shape):
            return ctx.enter_context(nc.sbuf_tensor(name, list(shape), F32))

        sb = {
            "ident": sbt("ident", P, P), "ones": sbt("ones", P, P),
            "cols_a": sbt("cols_a", P, P), "cols_b": sbt("cols_b", P, P),
            "silu_c": sbt("silu_c", P, KD, 2),
            "coef": sbt("coef", P, DEPTH, 2, 2, 3, KD),
        }
        h_ctx = nc.dram_tensor("h_ctx", (CTX_LEN, D_MODEL), F32, kind="Internal").ap()
        h_lat = nc.dram_tensor("h_lat", (SEQ, D_MODEL), F32, kind="Internal").ap()
        x, cx = a["x"][0], a["ctx"][0]
        u = sbt("u", P, KD, TOK)
        load_constants(nc, a, sb)
        adaln(nc, a, sb)
        norms(nc, a, sb, "norm_ab", [(1, 0, CT, cx, None), (0, CT, LT, x, None)], layer_u=(0, 0), u=u)
        x_mix = u
        qkv_dram = nc.dram_tensor("qkv_dram", (12, P, TOK), F32, kind="Internal").ap()
        cols = sbt("cols", P, NT, 2, 6, B_HEADS)
        with Stage(nc, "layer0") as l0:
            pa = l0.sb("pa", P, 10, TOK)
            decay_columns(nc, a, sb, u, cols)
            with Stage(nc, "layer0b") as l0b:
                pb = l0b.sb("pb", P, 12, TOK)
                w = a["ab_w_in"][0]
                project(nc, "in_ab", [(w, 0, P, 6, pa, 0), (w, 2304, P, 4, pa, 6), (w, 768, P, 12, pb, 0)], u, KD, ALL_CHUNKS)
                conv_qkv(nc, a, sb, pb, qkv_dram)
            with Stage(nc, "layer0c") as l0c:
                k_dup = l0c.sb("k_dup", P, A_KV, (NT + 2) * P)
                v_tok = l0c.sb("v_tok", P, NT + 2, P)
                window_prepare(nc, a, sb, pa, k_dup, v_tok)
                window_attention(nc, a, sb, pa, k_dup, v_tok, x_mix)
            Stage.recycle(nc)
            delta_rule(nc, a, sb, qkv_dram, cols, (x_mix[:, 4:8, :], pa[:, 0:4, :]))
            head_norm(nc, a, sb, x_mix[:, 4:8, :], pa[:, 0:4, :], pa[:, 6:10, :])
        Stage.recycle(nc)
        cond_tiles = ((1, 0, CT), (0, CT, LT))
        with Stage(nc, "out0") as st:
            y = st.sb("y", P, KD, TOK)
            project(nc, "out_ab", [(a["ab_w_out"][0], 0, P, KD, y, 0)], x_mix, KD, ALL_CHUNKS)
            norms(nc, a, sb, "res_ab", [(*cond_tiles[0], cx, h_ctx), (*cond_tiles[1], x, h_lat)],
                  layer_y=(0, 0), y=y, layer_u=(0, 1), u=u)

        def ffn(layer, chunks):
            with Stage(nc, f"hid{layer}") as f:
                hid = f.sb("hid", P, FB, TOK)
                ffn_hidden(nc, f"ffn{layer}", a["ffn_w_gate"][layer], a["ffn_w_up"][layer], u, hid, chunks)
                project(nc, f"down{layer}", [(a["ffn_w_down"][layer], 0, P, KD, u, 0)], hid, FB, chunks)

        ffn(0, ALL_CHUNKS)
        norms(nc, a, sb, "res_ffn0", [(*cond_tiles[0], h_ctx, None), (*cond_tiles[1], h_lat, h_lat)],
              layer_y=(0, 1), y=u, layer_u=(1, 0), u=u)
        Stage.recycle(nc)

        with Stage(nc, "layer1") as l1:
            c5, kpe, kpe_rot = l1.sb("c5", P, 5, TOK), l1.sb("kpe", C_ROPE, 1, TOK), l1.sb("kpe_rot", P, TOK)
            w = a["mla_w_in"][0]
            project(nc, "in_mla", [(w, 0, P, 5, c5, 0), (w, QR + KVR, C_ROPE, 1, kpe, 0)], u, KD, ALL_CHUNKS)
            latent_norms(nc, a, sb, c5, kpe, kpe_rot)
            latent_attention(nc, a, sb, c5, kpe_rot, u)
        with Stage(nc, "out1") as st:
            y = st.sb("y", P, KD, TOK)
            project(nc, "out_mla", [(a["mla_w_out"][0], 0, P, KD, y, 0)], u, KD, LAT_CHUNKS)
            Stage.recycle(nc)
            norms(nc, a, sb, "res_mla", [(*cond_tiles[1], h_lat, h_lat)], layer_y=(1, 0), y=y, layer_u=(1, 1), u=u)
        ffn(1, LAT_CHUNKS)
        norms(nc, a, sb, "res_ffn1", [(*cond_tiles[1], h_lat, out[0])], layer_y=(1, 1), y=u)


def tables():
    i = np.arange(P)
    eye = np.eye(P, dtype=np.float32)

    def pick(src, rows=P):
        m = np.zeros((P, P), np.float32)
        for out, s in enumerate(src):
            if s is not None:
                m[s, out] = 1.0
        return m

    half = A_DIM // 2
    mats = {"ident": eye, "ones": np.ones((P, P), np.float32)}
    swap = [(m // A_DIM) * A_DIM + (m % A_DIM + half) % A_DIM for m in i]
    mats["swap"] = pick(swap)
    for kv in range(2):
        mats[f"dup{kv}"] = pick([kv * A_DIM + m % A_DIM for m in i])
        mats[f"dupswap{kv}"] = pick([kv * A_DIM + (m % A_DIM + half) % A_DIM for m in i])
    hr = C_ROPE // 2
    mats["kpe_place"] = pick([m - C_NOPE if C_NOPE <= m < C_QK else None for m in i])
    mats["kpe_swap"] = pick([(m - C_NOPE + hr) % C_ROPE if C_NOPE <= m < C_QK else None for m in i])
    mats["q_swap"] = pick([C_NOPE + (m - C_NOPE + hr) % C_ROPE if C_NOPE <= m < C_QK else None for m in i])
    upto = (i[:, None] <= i[None, :])
    mats["cum0"], mats["cum1"] = upto.astype(np.float32), upto.T.astype(np.float32)
    mats["decay_mask0"] = np.where(upto, 0, NEG).astype(np.float32)
    mats["decay_mask1"] = np.where(upto.T, 0, NEG).astype(np.float32)
    for l in range(LEVELS):
        b = i >> l
        m = ((b[:, None] >> 1) == (b[None, :] >> 1)) & (b[:, None] % 2 == 1) & (b[None, :] % 2 == 0)
        mats[f"level0_{l}"], mats[f"level1_{l}"] = m.astype(np.float32), m.T.astype(np.float32)

    def rope(dim):
        n = dim // 4
        inv = (np.float32(10000.0) ** (-np.arange(n, dtype=np.float32) / n)).astype(np.float32)
        t = np.arange(SEQ)
        ang = np.concatenate([(t // GRID_W)[None, :] * inv[:, None], (t % GRID_W)[None, :] * inv[:, None]], 0).astype(np.float32)
        c, s = np.cos(ang), np.sin(ang)
        cos = np.ones((dim, TOK), np.float32)
        sin = np.zeros((dim, TOK), np.float32)
        cos[:, CTX_LEN:] = np.concatenate([c, c], 0)
        sin[:, CTX_LEN:] = np.concatenate([-s, s], 0)
        return cos, sin

    rope_a = np.stack([np.tile(x, (2, 1)) for x in rope(A_DIM)])
    rope_c = np.zeros((2, P, TOK), np.float32)
    rope_c[:, C_NOPE:C_QK] = np.stack(rope(C_ROPE))
    rel = np.arange(3 * P)[None, :] - P - i[:, None]
    window = np.full((NT, P, 3 * P), NEG, np.float32)
    for t in range(CT, NT):
        key = (t - CT) * P - P + np.arange(3 * P)
        window[t] = np.where((np.abs(rel) <= 128) & ((key >= 0) & (key < SEQ))[None, :], 0, NEG)
    return {"mats": np.stack([mats[m] for m in MATS]), "rope_a": rope_a.astype(np.float32),
            "rope_c": rope_c, "window": window}


INPUTS = ["x", "c", "ctx", "c_ctx", "mod_w", "mod_b", "norm_gains", "ffn_w_gate", "ffn_w_up", "ffn_w_down",
          "ab_w_in", "ab_sink", "ab_conv", "ab_a_log", "ab_dt_bias", "ab_out_norm", "ab_w_out",
          "mla_w_in", "mla_q_norm", "mla_kv_norm", "mla_w_qb", "mla_w_kvb", "mla_w_out"]


def kernel(**inputs):
    import concourse.bacc as bacc
    from concourse.bass_utils import run_bass_kernel_spmd

    nc = bacc.Bacc("TRN2", target_bir_lowering=False, num_devices=1)
    arrays = {n: np.ascontiguousarray(inputs[n]) for n in INPUTS}
    arrays.update(tables())
    aps = {n: nc.dram_tensor(f"in_{n}", v.shape, F32, kind="ExternalInput").ap() for n, v in arrays.items()}
    out = nc.dram_tensor("out", (1, SEQ, D_MODEL), F32, kind="ExternalOutput").ap()
    program(nc, aps, out)
    r = run_bass_kernel_spmd(nc, [{f"in_{n}": v for n, v in arrays.items()}], core_ids=[0])
    return r.results[0]["out"]
```

```python
from contextlib import ExitStack

import numpy as np
import concourse.bass as bass
from concourse import mybir

ALU = mybir.AluOpType
ACT = mybir.ActivationFunctionType
F32 = mybir.dt.float32
AX_X = mybir.AxisListType.X

P = 128
D_MODEL, SEQ, CTX_LEN, DEPTH, GRID_W = 1024, 1024, 256, 2, 64
EPS = 1e-6
TOK = SEQ + CTX_LEN
KD = D_MODEL // P
NT, CT = TOK // P, CTX_LEN // P
LT = NT - CT
A_HEADS, A_KV, A_DIM = 8, 2, 64
B_HEADS, B_DIM = 4, 128
C_HEADS, C_NOPE, C_ROPE, C_V = 16, 64, 32, 64
C_QK = C_NOPE + C_ROPE
QR, KVR = 384, 256
FFN = 2816
FB = FFN // P
AB_IN = 2832
NEG = -1e30
ALL_CHUNKS = ((0, 512), (512, 512), (1024, 256))
LAT_CHUNKS = ((256, 512), (768, 512))
LEVELS = 7
MATS = (["ident", "ones", "swap", "dup0", "dup1", "dupswap0", "dupswap1", "kpe_place", "kpe_swap", "q_swap",
         "cum0", "cum1", "decay_mask0", "decay_mask1"]
        + [f"level{d}_{l}" for d in range(2) for l in range(LEVELS)])
ROWS_A = (("mod_b", 96), ("c", KD), ("c_ctx", KD), ("q_norm", 3), ("kv_norm", 2), ("out_norm", 1))
ROWS_B = (("norm_gains", 64), ("conv", 36))


def give(eng, sems, n=1):
    for s in sems:
        eng.sem_inc(s, n)


class Stage:
    used_semaphores = []

    def __init__(self, nc, name):
        self.nc, self.name, self.stack = nc, name, ExitStack()

    @classmethod
    def recycle(cls, nc):
        nc.clear_and_free_semaphores(cls.used_semaphores)
        cls.used_semaphores = []
        nc.all_engine_barrier()

    def __enter__(self):
        self.stack.__enter__()
        return self

    def __exit__(self, *a):
        return self.stack.__exit__(*a)

    def sb(self, name, *shape):
        return self.stack.enter_context(self.nc.sbuf_tensor(f"{self.name}_{name}", list(shape), F32))

    def sb_r(self, name, *shape):
        return self.stack.enter_context(self.nc.sbuf_tensor(f"{self.name}_{name}", list(shape), mybir.dt.float32r))

    def ps(self, name, *shape):
        return self.stack.enter_context(self.nc.psum_tensor(f"{self.name}_{name}", list(shape), F32))

    def sem(self, name, n=None):
        sems = [self.nc.alloc_semaphore(f"{self.name}_{name}{i}") for i in range(n or 1)]
        Stage.used_semaphores += sems
        return sems if n else sems[0]


def rows_at(spec, name):
    at = 0
    for n, k in spec:
        if n == name:
            return at, at + k
        at += k
    raise KeyError(name)


def load_constants(nc, a, sb):
    with Stage(nc, "const") as st:
        rows = [st.sb("rows_a", P, P), st.sb("rows_b", P, P)]
        turned = [st.ps("turned_a", P, P), st.ps("turned_b", P, P)]
        loaded, cleared, transposed, columns = st.sem("loaded"), st.sem("cleared"), st.sem("transposed"), st.sem("columns")
        srcs = {
            "mod_b": a["mod_b"].rearrange("l (b p) -> (l b) p", p=P),
            "c": a["c"].rearrange("o (b p) -> (o b) p", p=P),
            "c_ctx": a["c_ctx"].rearrange("(b p) -> b p", p=P),
            "q_norm": a["mla_q_norm"].rearrange("o (b p) -> (o b) p", p=P),
            "kv_norm": a["mla_kv_norm"].rearrange("o (b p) -> (o b) p", p=P),
            "out_norm": a["ab_out_norm"],
            "norm_gains": a["norm_gains"].rearrange("l g (b p) -> (l g b) p", p=P),
            "conv": a["ab_conv"].rearrange("o j (b p) -> (o j b) p", p=P),
        }
        with nc.Block() as block:
            @block.vector
            def _(dve):
                for r in rows:
                    dve.memset(r[:, :], 0.0).then_inc(cleared, 1)
                dve.wait_ge(transposed, 2).then_inc(transposed, -2)
                dve.tensor_copy(sb["cols_a"][:, :], turned[0][:, :]).then_inc(columns, 1)
                dve.tensor_copy(sb["cols_b"][:, :], turned[1][:, :]).then_inc(columns, 1)

            @block.sync
            def _(sp):
                sp.dma_start(sb["ident"][:, :], a["mats"][MATS.index("ident")]).then_inc(loaded, 16)
                sp.dma_start(sb["ones"][:, :], a["mats"][MATS.index("ones")]).then_inc(loaded, 16)
                sp.wait_ge(cleared, 2)
                for spec, r in ((ROWS_A, rows[0]), (ROWS_B, rows[1])):
                    for name, _k in spec:
                        lo, hi = rows_at(spec, name)
                        sp.dma_start(r[lo:hi, :], srcs[name]).then_inc(loaded, 16)

            @block.tensor
            def _(pe):
                pe.wait_ge(loaded, 16 * (2 + len(ROWS_A) + len(ROWS_B)))
                for r, t in zip(rows, turned):
                    pe.transpose(t[:, :], r[:, :], sb["ident"][:, :]).then_inc(transposed, 1)

            @block.scalar
            def _(act):
                act.wait_ge(columns, 2)
                lo, _hi = rows_at(ROWS_A, "c")
                act.activation(sb["silu_c"][:, :, :], sb["cols_a"][:, lo:lo + 2 * KD].rearrange("p (c k) -> p k c", c=2),
                               ACT.Silu)


def adaln(nc, a, sb):
    NG, NS, W = 12, 4, 512
    with Stage(nc, "adaln") as st:
        w = [st.sb(f"w{s}", P, KD, W) for s in range(NS)]
        out = [st.ps(f"out{s}", 2, W) for s in range(NS)]
        rows = st.sb("rows", 2, DEPTH, 6 * D_MODEL)
        cols = st.ps("cols", P, DEPTH, 48, 2)
        mod = st.sb("mod", P, DEPTH, 2, 48)
        w_in, out_full, out_free = st.sem("w_in", NS), st.sem("out_full", NS), st.sem("out_free", NS)
        rows_full, rows_done, cols_full, mod_done, coef_step = (st.sem(n) for n in ("rows_full", "rows_done", "cols_full", "mod_done", "coef_step"))
        b_lo, _ = rows_at(ROWS_A, "mod_b")
        g_lo, _ = rows_at(ROWS_B, "norm_gains")
        with nc.Block() as block:
            @block.sync
            def _(sp):
                for layer in range(DEPTH):
                    w_v = a["mod_w"][layer].rearrange("(k p) n -> p k n", p=P)
                    with sp.Fori(0, NG // NS) as i:
                        for s in range(NS):
                            sp.wait_ge(out_free[s], 1).then_inc(out_free[s], -1)
                            sp.dma_start(w[s][:, :, :], w_v[:, :, bass.ds((i * NS + s) * W, W)]).then_inc(w_in[s], 16)

            @block.tensor
            def _(pe):
                for layer in range(DEPTH):
                    with pe.Fori(0, NG // NS) as i:
                        for s in range(NS):
                            pe.wait_ge(w_in[s], 16).then_inc(w_in[s], -16)
                            for k in range(KD):
                                mm = pe.matmul(out[s][:, :], sb["silu_c"][:, k, :], w[s][:, k, :], start=(k == 0), stop=(k == KD - 1))
                            mm.then_inc(out_full[s], 1)
                pe.wait_ge(rows_full, 1).then_inc(rows_full, -1)
                for layer in range(DEPTH):
                    for b in range(48):
                        mm = pe.transpose(cols[:, layer, b, :], rows[:, layer, b * P:(b + 1) * P], sb["ident"][0:2, 0:2])
                mm.then_inc(cols_full, 1)

            @block.vector
            def _(dve):
                give(dve, out_free)
                for layer in range(DEPTH):
                    with dve.Fori(0, NG // NS) as i:
                        for s in range(NS):
                            dve.wait_ge(out_full[s], 1).then_inc(out_full[s], -1)
                            dve.tensor_copy(rows[:, layer, bass.ds((i * NS + s) * W, W)], out[s][:, :]).then_inc(rows_done, 1)
                            dve.wait_ge(rows_done, 1).then_inc(rows_done, -1)
                            dve.sem_inc(out_free[s], 1)
                dve.sem_inc(rows_full, 1)
                dve.wait_ge(cols_full, 1).then_inc(cols_full, -1)
                for layer in range(DEPTH):
                    for cond in range(2):
                        dve.tensor_tensor(mod[:, layer, cond, :], cols[:, layer, :, cond],
                                          sb["cols_a"][:, b_lo + layer * 48:b_lo + (layer + 1) * 48], ALU.add).then_inc(mod_done, 1)
                dve.wait_ge(mod_done, 4).then_inc(mod_done, -4)
                for layer in range(DEPTH):
                    for half in range(2):
                        for cond in range(2):
                            m = [mod[:, layer, cond, (3 * half + j) * KD:(3 * half + j + 1) * KD] for j in range(3)]
                            g = [sb["cols_b"][:, g_lo + (layer * 4 + 2 * half + j) * KD:g_lo + (layer * 4 + 2 * half + j + 1) * KD]
                                 for j in range(2)]
                            c = sb["coef"]
                            dve.tensor_copy(c[:, layer, half, cond, 0, :], m[0])
                            dve.scalar_tensor_tensor(out=c[:, layer, half, cond, 1, :], in0=m[1], scalar=1.0, in1=g[0],
                                                     op0=ALU.add, op1=ALU.mult)
                            dve.tensor_tensor(c[:, layer, half, cond, 2, :], m[2], g[1], ALU.mult)


def norms(nc, a, sb, name, segs, layer_y=None, y=None, layer_u=None, u=None):
    with Stage(nc, name) as st:
        h = [st.sb(f"h{s}", P, D_MODEL) for s in range(2)]
        sq = st.sb("sq", P, D_MODEL)
        stat = st.sb("stat", P, 2, 2, 4)
        eps = st.sb("eps", P, 1)
        h_in, h_free, h_out = st.sem("h_in", 2), st.sem("h_free", 2), st.sem("h_out", 2)
        h_new, h_new_act, h_new_dma = st.sem("h_new"), st.sem("h_new_act"), st.sem("h_new_dma", 2)
        act_step, root, sub, eps_set = st.sem("act_step"), st.sem("root"), st.sem("sub"), st.sem("eps_set")
        if y is not None:
            y_slot = [st.sb(f"y{s}", P, KD, P) for s in range(2)]
            y_tok = [st.ps(f"ytok{s}", P, D_MODEL) for s in range(2)]
            gate = st.sb("gate", P, 2, D_MODEL)
            tmp = st.sb("tmp", P, D_MODEL)
            y_in, y_free, y_full, y_read = st.sem("y_in", 2), st.sem("y_free", 2), st.sem("y_full", 2), st.sem("y_read", 2)
            gate_full, gate_read, gate_set = st.sem("gate_full"), st.sem("gate_read"), st.sem("gate_set")
        if u is not None:
            hn = [st.sb(f"hn{s}", P, D_MODEL) for s in range(2)]
            u_ps = [st.ps(f"ups{s}", P, D_MODEL) for s in range(2)]
            hn_full, hn_free, u_full, u_free = st.sem("hn_full", 2), st.sem("hn_free", 2), st.sem("u_full", 2), st.sem("u_free", 2)
            h_read = st.sem("h_read", 2)
        conds = [s[0] for s in segs]
        with nc.Block() as block:
            @block.sync
            def _(sp):
                for cond, t0, n, src, dst in segs:
                    with sp.Fori(0, n // 2) as i:
                        for s in range(2):
                            sp.wait_ge(h_free[s], 1).then_inc(h_free[s], -1)
                            sp.dma_start(h[s][:, :], src[bass.ds((2 * i + s) * P, P), :]).then_inc(h_in[s], 16)
                            if y is not None:
                                sp.wait_ge(y_free[s], 1).then_inc(y_free[s], -1)
                                sp.dma_start(y_slot[s][:, :, :], y[:, :, bass.ds((2 * i + s + t0) * P, P)]).then_inc(y_in[s], 16)

            @block.tensor
            def _(pe):
                if y is not None:
                    for cond in conds:
                        pe.wait_ge(gate_read, 1).then_inc(gate_read, -1)
                        for k in range(KD):
                            col = sb["coef"][:, layer_y[0], layer_y[1], cond, 2, k:k + 1]
                            mm = pe.matmul(y_tok[0][:, k * P:(k + 1) * P], col.to_broadcast([P, P]), sb["ident"][:, :],
                                           start=True, stop=True)
                        mm.then_inc(gate_full, 1)
                    pe.wait_ge(gate_read, 1).then_inc(gate_read, -1)
                for cond, t0, n, src, dst in segs:
                    with pe.Fori(0, n // 2) as i:
                        if y is not None:
                            for s in range(2):
                                pe.wait_ge(y_in[s], 16).then_inc(y_in[s], -16)
                                pe.wait_ge(y_read[s], 1).then_inc(y_read[s], -1)
                                for k in range(KD):
                                    mm = pe.transpose(y_tok[s][:, k * P:(k + 1) * P], y_slot[s][:, k, :], sb["ident"][:, :])
                                mm.then_inc(y_full[s], 1)
                        if u is not None:
                            for s in range(2):
                                pe.wait_ge(hn_full[s], 1).then_inc(hn_full[s], -1)
                                pe.wait_ge(u_free[s], 1).then_inc(u_free[s], -1)
                                for k in range(KD):
                                    mm = pe.transpose(u_ps[s][:, k * P:(k + 1) * P], hn[s][:, k * P:(k + 1) * P], sb["ident"][:, :])
                                mm.then_inc(u_full[s], 1)

            def root_mean_square(act, src, to):
                act.activation(sq[:, :], src, ACT.Square, accum_out=to[:, 0:1]).then_inc(act_step, 1)
                act.wait_ge(act_step, 1).then_inc(act_step, -1)
                act.activation(to[:, 1:2], to[:, 0:1], ACT.Sqrt, scale=1.0 / D_MODEL, bias=eps[:, :]).then_inc(root, 1)

            @block.scalar
            def _(act):
                act.wait_ge(eps_set, 1)
                for cond, t0, n, src, dst in segs:
                    with act.Fori(0, n // 2) as i:
                        for s in range(2):
                            if y is not None:
                                act.wait_ge(y_full[s], 1).then_inc(y_full[s], -1)
                                act.sem_inc(y_free[s], 1)
                                root_mean_square(act, y_tok[s][:, :], stat[:, s, 0, :])
                        for s in range(2):
                            if y is None:
                                act.wait_ge(h_in[s], 16).then_inc(h_in[s], -16)
                            else:
                                act.wait_ge(h_new_act, 1).then_inc(h_new_act, -1)
                            if u is not None:
                                root_mean_square(act, h[s][:, :], stat[:, s, 1, :])
                            if dst is not None:
                                act.dma_start(dst[bass.ds((2 * i + s) * P, P), :], h[s][:, :]).then_inc(h_out[s], 16)
                        if u is not None:
                            for s in range(2):
                                act.wait_ge(u_full[s], 1).then_inc(u_full[s], -1)
                                act.sem_inc(hn_free[s], 1)
                                c = sb["coef"]
                                for k in range(KD):
                                    act.activation(u[:, k, bass.ds((2 * i + s + t0) * P, P)], u_ps[s][:, k * P:(k + 1) * P],
                                                   ACT.Identity, scale=c[:, layer_u[0], layer_u[1], cond, 1, k:k + 1],
                                                   bias=c[:, layer_u[0], layer_u[1], cond, 0, k:k + 1]).then_inc(act_step, 1)
                                act.wait_ge(act_step, KD).then_inc(act_step, -KD)
                                act.sem_inc(u_free[s], 1)

            @block.vector
            def _(dve):
                dve.memset(eps[:, :], EPS).then_inc(eps_set, 1)
                give(dve, h_free)
                if y is not None:
                    give(dve, y_free)
                    give(dve, y_read)
                    give(dve, [gate_read])
                    for cond in conds:
                        dve.wait_ge(gate_full, 1).then_inc(gate_full, -1)
                        dve.tensor_copy(gate[:, cond, :], y_tok[0][:, :]).then_inc(gate_set, 1)
                        dve.wait_ge(gate_set, 1).then_inc(gate_set, -1)
                        dve.sem_inc(gate_read, 1)
                if u is not None:
                    give(dve, hn_free)
                    give(dve, u_free)
                for cond, t0, n, src, dst in segs:
                    with dve.Fori(0, n // 2) as i:
                        for s in range(2):
                            if y is not None:
                                r = stat[:, s, 0, 2:3]
                                dve.wait_ge(root, 1).then_inc(root, -1)
                                dve.reciprocal(r, stat[:, s, 0, 1:2]).then_inc(sub, 1)
                                dve.wait_ge(sub, 1).then_inc(sub, -1)
                                dve.scalar_tensor_tensor(out=tmp[:, :], in0=y_tok[s][:, :], scalar=r, in1=gate[:, cond, :],
                                                         op0=ALU.mult, op1=ALU.mult).then_inc(sub, 1)
                                dve.wait_ge(sub, 1).then_inc(sub, -1)
                                dve.sem_inc(y_read[s], 1)
                                dve.wait_ge(h_in[s], 16).then_inc(h_in[s], -16)
                                dve.tensor_tensor(h[s][:, :], h[s][:, :], tmp[:, :], ALU.add).then_inc(sub, 1)
                                dve.wait_ge(sub, 1).then_inc(sub, -1)
                                dve.sem_inc(h_new_act, 1)
                            if y is not None and u is None:
                                dve.wait_ge(h_out[s], 16).then_inc(h_out[s], -16)
                                dve.sem_inc(h_free[s], 1)
                        if u is not None:
                            for s in range(2):
                                r = stat[:, s, 1, 2:3]
                                dve.wait_ge(root, 1).then_inc(root, -1)
                                dve.reciprocal(r, stat[:, s, 1, 1:2]).then_inc(sub, 1)
                                dve.wait_ge(sub, 1).then_inc(sub, -1)
                                dve.wait_ge(hn_free[s], 1).then_inc(hn_free[s], -1)
                                dve.tensor_scalar(hn[s][:, :], h[s][:, :], r, None, ALU.mult).then_inc(sub, 1)
                                dve.wait_ge(sub, 1).then_inc(sub, -1)
                                dve.sem_inc(hn_full[s], 1)
                                if dst is not None:
                                    dve.wait_ge(h_out[s], 16).then_inc(h_out[s], -16)
                                dve.sem_inc(h_free[s], 1)


def project(nc, name, segs, x, k_tiles, chunks):
    nch = len(chunks)
    with Stage(nc, name) as st:
        w_slot = [st.sb(f"w{s}", P, k_tiles, P) for s in range(2)]
        acc = [[st.ps(f"acc{s}{j}", P, 512) for j in range(nch)] for s in range(2)]
        w_in, w_free = st.sem("w_in", 2), st.sem("w_free", 2)
        acc_full = [st.sem(f"acc_full{s}", nch) for s in range(2)]
        acc_free = [st.sem(f"acc_free{s}", nch) for s in range(2)]
        copied = st.sem("copied")

        def over_blocks(eng, nblk, body):
            if nblk > 1:
                with eng.Fori(0, nblk // 2) as i:
                    for s in range(2):
                        body(s, 2 * i + s)
            if nblk % 2:
                body(0, nblk - 1)

        with nc.Block() as block:
            @block.sync
            def _(sp):
                for w, col0, m, nblk, dst, blk0 in segs:
                    w_v = w.rearrange("(k p) n -> p k n", p=P)

                    def load(s, b):
                        sp.wait_ge(w_free[s], 1).then_inc(w_free[s], -1)
                        sp.dma_start(w_slot[s][:, :, 0:m], w_v[:, :, bass.ds(b * m + col0, m)]).then_inc(w_in[s], 16)
                    over_blocks(sp, nblk, load)

            @block.tensor
            def _(pe):
                for w, col0, m, nblk, dst, blk0 in segs:
                    def products(s, b):
                        pe.wait_ge(w_in[s], 16).then_inc(w_in[s], -16)
                        for j, (t0, n) in enumerate(chunks):
                            pe.wait_ge(acc_free[s][j], 1).then_inc(acc_free[s][j], -1)
                            for k in range(k_tiles):
                                mm = pe.matmul(acc[s][j][0:m, 0:n], w_slot[s][:, k, 0:m], x[:, k, t0:t0 + n],
                                               start=(k == 0), stop=(k == k_tiles - 1))
                            mm.then_inc(acc_full[s][j], 1)
                    over_blocks(pe, nblk, products)

            @block.vector
            def _(dve):
                give(dve, w_free)
                for s in range(2):
                    give(dve, acc_free[s])
                for w, col0, m, nblk, dst, blk0 in segs:
                    def copy_out(s, b):
                        for j, (t0, n) in enumerate(chunks):
                            dve.wait_ge(acc_full[s][j], 1).then_inc(acc_full[s][j], -1)
                            if j == nch - 1:
                                dve.sem_inc(w_free[s], 1)
                            dve.tensor_copy(dst[0:m, bass.ds(b + blk0, 1), t0:t0 + n], acc[s][j][0:m, 0:n].rearrange("p (o n) -> p o n", o=1)).then_inc(copied, 1)
                            dve.wait_ge(copied, 1).then_inc(copied, -1)
                            dve.sem_inc(acc_free[s][j], 1)
                    over_blocks(dve, nblk, copy_out)


def ffn(nc, name, w_gate, w_up, w_down, u, chunks):
    F32R = mybir.dt.float32r
    nch = len(chunks)
    lo_tok, n_tok = chunks[0][0], TOK - chunks[0][0]
    PAIRS = ((0, 0), (1, 0), (0, 1))
    NO = 4
    with Stage(nc, name) as st:
        raw = [st.sb(f"raw_{n}", P, D_MODEL) for n in ("gate", "up", "down")]
        u_part = [st.sb_r(f"u_part{x}", P, KD, n_tok) for x in range(2)]
        gu_part = [[[st.sb_r(f"gu{s}{g}{x}", P, KD * P) for x in range(2)] for g in range(2)] for s in range(2)]
        down_part = [st.sb_r(f"down{x}", P, D_MODEL) for x in range(2)]
        silu, hid = st.sb("silu", P, 512), [st.sb(f"hid{r}", P, 512) for r in range(2)]
        hid_part = [[st.sb_r(f"hid_part{r}{x}", P, 512) for x in range(2)] for r in range(2)]
        acc = [[st.ps(f"acc{r}{g}", P, 512) for g in range(2)] for r in range(2)]
        out = [st.ps(f"out{r}", P, 512) for r in range(NO)]
        raw_in, raw_free = st.sem("raw_in", 3), st.sem("raw_free", 3)
        weight_hi, gu_clear, gu_free = st.sem("weight_hi"), st.sem("gu_clear", 2), st.sem("gu_free", 2)
        down_ready, down_free = st.sem("down_ready"), st.sem("down_free")
        u_hi, u_split, u_clear = st.sem("u_hi"), st.sem("u_split"), st.sem("u_clear")
        gate_full, up_full, pair_free = st.sem("gate_full", 2), st.sem("up_full", 2), st.sem("pair_free", 2)
        silu_full, hid_full, hid_hi = st.sem("silu_full"), st.sem("hid_full"), st.sem("hid_hi")
        hid_ready, hid_free = st.sem("hid_ready", 2), st.sem("hid_free", 2)
        out_full, out_free, step = st.sem("out_full", NO), st.sem("out_free", NO), st.sem("step")

        def over_blocks(eng, start, unit, prepare_down, prepare_gu):
            prepare_gu(0)
            prepare_down()
            prepare_gu(1)
            start()

            def pair_of_blocks(last):
                units = [(s, j, (s * nch + j) % 2) for s in range(2) for j in range(nch)]
                for n, (s, j, r) in enumerate(units):
                    end = last and n == len(units) - 1
                    unit((s, j, r), None if end else units[(n + 1) % len(units)])
                    if j == nch - 1 and not (last and s == 1):
                        prepare_down()
                    if j == nch - 1 and not last:
                        prepare_gu(s)
            with eng.Fori(0, FB // 2 - 1) as i:
                pair_of_blocks(False)
            pair_of_blocks(True)

        with nc.Block() as block:
            @block.sync
            def _(sp):
                gu_v = [w.rearrange("(k p) n -> p k n", p=P) for w in (w_gate, w_up)]
                down_v = w_down.rearrange("(f p) n -> p f n", p=P)

                def load_gu(f):
                    for g in range(2):
                        sp.wait_ge(raw_free[g], 1).then_inc(raw_free[g], -1)
                        sp.dma_start(raw[g][:, :].rearrange("p (k n) -> p k n", k=KD), gu_v[g][:, :, bass.ds(f * P, P)]).then_inc(raw_in[g], 16)

                def load_down(f):
                    sp.wait_ge(raw_free[2], 1).then_inc(raw_free[2], -1)
                    sp.dma_start(raw[2][:, :].rearrange("p (o n) -> p o n", o=1), down_v[:, bass.ds(f, 1), :]).then_inc(raw_in[2], 16)
                load_gu(0)
                load_down(0)
                load_gu(1)
                with sp.Fori(0, FB - 2) as f:
                    load_down(f + 1)
                    load_gu(f + 2)
                load_down(FB - 1)

            @block.tensor
            def _(pe):
                def gate_up(s, j, r):
                    t0, n = chunks[j]
                    if j == 0:
                        pe.wait_ge(gu_clear[s], 2).then_inc(gu_clear[s], -2)
                    pe.wait_ge(pair_free[r], 1).then_inc(pair_free[r], -1)
                    for g, full in ((0, gate_full), (1, up_full)):
                        for k in range(KD):
                            for w_, x_ in PAIRS:
                                mm = pe.matmul(acc[r][g][:, 0:n], gu_part[s][g][w_][:, k * P:(k + 1) * P], u_part[x_][:, k, t0 - lo_tok:t0 - lo_tok + n],
                                               start=(k == 0 and w_ + x_ == 0), stop=(k == KD - 1 and x_ == 1))
                        mm.then_inc(full[r], 1)
                    if j == nch - 1:
                        pe.drain().then_inc(gu_free[s], 1)

                def down(s, j, r):
                    t0, n = chunks[j]
                    if j == 0:
                        pe.wait_ge(down_ready, 1).then_inc(down_ready, -1)
                    pe.wait_ge(hid_ready[r], 1).then_inc(hid_ready[r], -1)
                    for b in range(KD):
                        o = b % NO
                        pe.wait_ge(out_free[o], 1).then_inc(out_free[o], -1)
                        for w_, x_ in PAIRS:
                            mm = pe.matmul(out[o][:, 0:n], down_part[w_][:, b * P:(b + 1) * P], hid_part[r][x_][:, 0:n],
                                           start=(w_ + x_ == 0), stop=(x_ == 1))
                        mm.then_inc(out_full[o], 1)
                    pe.drain().then_inc(hid_free[r], 1)
                    if j == nch - 1:
                        pe.sem_inc(down_free, 1)

                def unit(this, nxt):
                    if nxt is not None:
                        gate_up(*nxt)
                    down(*this)
                over_blocks(pe, lambda: gate_up(0, 0, 0), unit, lambda: None, lambda s: None)

            @block.scalar
            def _(act):
                def hidden(s, j, r):
                    t0, n = chunks[j]
                    act.wait_ge(gate_full[r], 1).then_inc(gate_full[r], -1)
                    act.activation(silu[:, 0:n], acc[r][0][:, 0:n], ACT.Silu).then_inc(silu_full, 1)
                    act.wait_ge(hid_full, 1).then_inc(hid_full, -1)
                    act.wait_ge(hid_free[r], 1).then_inc(hid_free[r], -1)
                    act.activation(hid_part[r][0][:, 0:n], hid[r][:, 0:n], ACT.Copy).then_inc(hid_hi, 1)

                def prepare_gu(s):
                    act.wait_ge(gu_free[s], 1).then_inc(gu_free[s], -1)
                    for g in range(2):
                        act.wait_ge(raw_in[g], 16).then_inc(raw_in[g], -16)
                        act.activation(gu_part[s][g][0][:, :], raw[g][:, :], ACT.Copy).then_inc(weight_hi, 1)

                def prepare_down():
                    act.wait_ge(down_free, 1).then_inc(down_free, -1)
                    act.wait_ge(raw_in[2], 16).then_inc(raw_in[2], -16)
                    act.activation(down_part[0][:, :], raw[2][:, :], ACT.Copy).then_inc(weight_hi, 1)

                def unit(this, nxt):
                    if nxt is not None:
                        hidden(*nxt)

                give(act, gu_free)
                give(act, hid_free)
                give(act, [down_free])
                for k in range(KD):
                    act.activation(u_part[0][:, k, :], u[:, k, lo_tok:], ACT.Copy).then_inc(u_hi, 1)
                over_blocks(act, lambda: hidden(0, 0, 0), unit, prepare_down, prepare_gu)

            @block.gpsimd
            def _(pool):
                for k in range(KD):
                    pool.wait_ge(u_split, 1).then_inc(u_split, -1)
                    pool.memset(u[:, k, lo_tok:], 0.0).then_inc(u_clear, 1)
                pool.wait_ge(u_clear, KD).then_inc(u_clear, -KD)
                give(pool, out_free)

            @block.vector
            def _(dve):
                def done(ins, *to):
                    ins.then_inc(step, 1)
                    dve.wait_ge(step, 1).then_inc(step, -1)
                    for x_ in to:
                        dve.sem_inc(x_, 1)

                def hidden(s, j, r):
                    t0, n = chunks[j]
                    dve.wait_ge(silu_full, 1).then_inc(silu_full, -1)
                    dve.wait_ge(up_full[r], 1).then_inc(up_full[r], -1)
                    done(dve.tensor_tensor(hid[r][:, 0:n], acc[r][1][:, 0:n], silu[:, 0:n], ALU.mult), hid_full, pair_free[r])

                def hidden_low(s, j, r):
                    t0, n = chunks[j]
                    dve.wait_ge(hid_hi, 1).then_inc(hid_hi, -1)
                    dve.tensor_tensor(hid_part[r][1][:, 0:n], hid[r][:, 0:n], hid_part[r][0][:, 0:n].bitcast(F32), ALU.subtract).then_inc(hid_ready[r], 1)

                def low_part(parts, g, ready):
                    dve.wait_ge(weight_hi, 1).then_inc(weight_hi, -1)
                    done(dve.tensor_tensor(parts[1][:, :], raw[g][:, :], parts[0][:, :].bitcast(F32), ALU.subtract), ready, raw_free[g])

                def prepare_gu(s):
                    for g in range(2):
                        low_part(gu_part[s][g], g, gu_clear[s])

                def prepare_down():
                    low_part(down_part, 2, down_ready)

                def unit(this, nxt):
                    if nxt is not None:
                        hidden(*nxt)
                    s, j, r = this
                    t0, n = chunks[j]
                    for b in range(KD):
                        o = b % NO
                        dve.wait_ge(out_full[o], 1).then_inc(out_full[o], -1)
                        dve.tensor_tensor(u[:, b, t0:t0 + n], u[:, b, t0:t0 + n], out[o][:, 0:n], ALU.add).then_inc(out_free[o], 1)
                        if b == 1 and nxt is not None:
                            hidden_low(*nxt)

                for g in (raw_free, pair_free):
                    give(dve, g)
                for k in range(KD):
                    dve.wait_ge(u_hi, 1).then_inc(u_hi, -1)
                    dve.tensor_tensor(u_part[1][:, k, :], u[:, k, lo_tok:], u_part[0][:, k, :].bitcast(F32), ALU.subtract).then_inc(u_split, 1)
                over_blocks(dve, lambda: (hidden(0, 0, 0), hidden_low(0, 0, 0)), unit, prepare_down, prepare_gu)


def decay_columns(nc, a, sb, u, cols):
    w_col = AB_IN - 4 * B_HEADS
    nh = 2 * B_HEADS
    with Stage(nc, "decay") as st:
        w = st.sb("w", P, KD, 2 * nh)
        alog, dtb = st.sb("alog", P, nh), st.sb("dtb", P, nh)
        cum = [st.sb(f"cum{d}", P, P) for d in range(2)]
        x, e, sp_, total = (st.sb(n, P, NT, nh) for n in ("x", "e", "sp", "total"))
        raw = st.ps("raw", P, NT, 2 * nh)
        sums = st.ps("sums", P, 2, NT, nh)
        loaded, raw_full, step, act_step = st.sem("loaded"), st.sem("raw_full"), st.sem("step"), st.sem("act_step")
        go_act, go_dve, ld_full, sums_full = st.sem("go_act"), st.sem("go_dve"), st.sem("ld_full"), st.sem("sums_full")

        def kind(k, d):
            return cols[:, :, d, k, :]

        def heads(t, d):
            return t[:, :, d * B_HEADS:(d + 1) * B_HEADS]

        with nc.Block() as block:
            @block.sync
            def _(sp):
                sp.dma_start(w[:, :, :], a["ab_w_in"][0].rearrange("(k p) n -> p k n", p=P)[:, :, w_col:AB_IN]).then_inc(loaded, 16)
                sp.dma_start(alog[:, :], a["ab_a_log"].rearrange("o d h -> o (d h)").to_broadcast([P, nh])).then_inc(loaded, 16)
                sp.dma_start(dtb[:, :], a["ab_dt_bias"].rearrange("o d h -> o (d h)").to_broadcast([P, nh])).then_inc(loaded, 16)
                for d in range(2):
                    sp.dma_start(cum[d][:, :], a["mats"][MATS.index(f"cum{d}")]).then_inc(loaded, 16)

            @block.tensor
            def _(pe):
                pe.wait_ge(loaded, 80)
                for t in range(NT):
                    for k in range(KD):
                        mm = pe.matmul(raw[:, t, :], u[:, k, t * P:(t + 1) * P], w[:, k, :], start=(k == 0), stop=(k == KD - 1))
                mm.then_inc(raw_full, 1)
                pe.wait_ge(ld_full, 1).then_inc(ld_full, -1)
                for d in range(2):
                    ld = sp_[:, :, d * B_HEADS:(d + 1) * B_HEADS]
                    pe.matmul(sums[:, 0, :, d * B_HEADS:(d + 1) * B_HEADS], cum[d][:, :], ld, start=True, stop=True)
                    mm = pe.matmul(sums[:, 1, :, d * B_HEADS:(d + 1) * B_HEADS], sb["ones"][:, :], ld, start=True, stop=True)
                mm.then_inc(sums_full, 1)

            @block.vector
            def _(dve):
                def done(ins, n=1):
                    ins.then_inc(step, 1)
                    dve.wait_ge(step, 1).then_inc(step, -1)

                dve.wait_ge(loaded, 80)
                dve.wait_ge(raw_full, 1).then_inc(raw_full, -1)
                done(dve.tensor_tensor(x[:, :, :], raw[:, :, 0:nh], dtb[:, :].rearrange("p (o n) -> p o n", o=1).to_broadcast([P, NT, nh]), ALU.add))
                done(dve.tensor_copy(total[:, :, :], raw[:, :, nh:2 * nh]))
                dve.sem_inc(go_act, 1)
                dve.wait_ge(go_dve, 1).then_inc(go_dve, -1)
                done(dve.tensor_scalar(e[:, :, :], e[:, :, :], 1.0, None, ALU.add))
                done(dve.reciprocal(e[:, :, :], e[:, :, :]))
                for d in range(2):
                    dve.tensor_copy(kind(2, d), heads(e, d))
                done(dve.tensor_scalar(x[:, :, :], x[:, :, :], 0.0, None, ALU.max))
                done(dve.tensor_tensor(x[:, :, :], x[:, :, :], sp_[:, :, :], ALU.add))
                done(dve.scalar_tensor_tensor(out=sp_[:, :, :], in0=x[:, :, :], scalar=-1.0,
                                              in1=alog[:, :].rearrange("p (o n) -> p o n", o=1).to_broadcast([P, NT, nh]), op0=ALU.mult, op1=ALU.mult))
                dve.sem_inc(ld_full, 1)
                for d in range(2):
                    dve.tensor_copy(kind(0, d), heads(sp_, d))
                dve.wait_ge(sums_full, 1).then_inc(sums_full, -1)
                done(dve.tensor_copy(x[:, :, :], sums[:, 0, :, :]))
                done(dve.tensor_copy(total[:, :, :], sums[:, 1, :, :]))
                for d in range(2):
                    dve.tensor_copy(kind(1, d), heads(x, d))
                done(dve.tensor_tensor(sp_[:, :, :], total[:, :, :], x[:, :, :], ALU.subtract))
                dve.sem_inc(go_act, 1)
                dve.wait_ge(go_dve, 1).then_inc(go_dve, -1)
                done(dve.tensor_tensor(sp_[:, :, :], sp_[:, :, :], e[:, :, :], ALU.mult))
                for d in range(2):
                    dve.tensor_scalar(kind(3, d), heads(x, d), -1.0, None, ALU.mult)
                    dve.tensor_copy(kind(4, d), heads(sp_, d))
                    dve.tensor_copy(kind(5, d), heads(total, d))

            @block.scalar
            def _(act):
                def done(ins):
                    ins.then_inc(act_step, 1)
                    act.wait_ge(act_step, 1).then_inc(act_step, -1)

                act.wait_ge(go_act, 1).then_inc(go_act, -1)
                done(act.activation(e[:, :, :], total[:, :, :], ACT.Exp, scale=-1.0))
                done(act.activation(alog[:, :], alog[:, :], ACT.Exp))
                done(act.activation(sp_[:, :, :], x[:, :, :], ACT.Abs))
                done(act.activation(sp_[:, :, :], sp_[:, :, :], ACT.Exp, scale=-1.0))
                done(act.activation(sp_[:, :, :], sp_[:, :, :], ACT.Ln, bias=1.0))
                act.sem_inc(go_dve, 1)
                act.wait_ge(go_act, 1).then_inc(go_act, -1)
                done(act.activation(x[:, :, :], x[:, :, :], ACT.Exp))
                done(act.activation(sp_[:, :, :], sp_[:, :, :], ACT.Exp))
                done(act.activation(total[:, :, :], total[:, :, :], ACT.Exp))
                act.sem_inc(go_dve, 1)


def conv_qkv(nc, a, sb, pb, qkv_dram):
    c_lo, _ = rows_at(ROWS_B, "conv")
    with Stage(nc, "conv") as st:
        y = [st.sb(f"y{s}", P, TOK) for s in range(2)]
        z = [st.sb(f"z{s}", P, TOK) for s in range(2)]
        sq = [st.sb(f"sq{s}", P, TOK) for s in range(2)]
        eps = st.sb("eps", P, 1)
        norm = [[st.ps(f"norm{s}{j}", P, 512) for j in range(3)] for s in range(2)]
        eps_set, step, act_step = st.sem("eps_set"), st.sem("step"), st.sem("act_step")
        y_full, z_full, sq_full, norm_full, root_full = (st.sem(n, 2) for n in ("y_full", "z_full", "sq_full", "norm_full", "root_full"))
        out_ready, stored = st.sem("out_ready", 2), st.sem("stored", 2)
        groups = ((0, float(B_DIM) ** -0.5), (4, 1.0), (8, None))
        with nc.Block() as block:
            @block.vector
            def _(dve):
                dve.memset(eps[:, :], EPS).then_inc(eps_set, 1)
                give(dve, stored, 16)
                for b0, scale in groups:
                    with dve.Fori(0, 2) as i:
                        for s in range(2):
                            b = 2 * i + s + b0
                            taps = [sb["cols_b"][:, bass.ds(b + c_lo + 12 * j, 1)] for j in range(3)]
                            dve.wait_ge(stored[s], 16).then_inc(stored[s], -16)
                            dve.tensor_scalar(y[s][:, :].rearrange("p (o n) -> p o n", o=1), pb[:, bass.ds(b, 1), :], taps[1], None, ALU.mult).then_inc(step, 1)
                            dve.wait_ge(step, 1).then_inc(step, -1)
                            for j, (src, dst) in ((0, (0, 1)), (2, (1, 0))):
                                for lo, n in ((0, CTX_LEN), (CTX_LEN, SEQ)):
                                    o = y[s][:, lo + dst:lo + dst + n - 1].rearrange("p (o n) -> p o n", o=1)
                                    dve.scalar_tensor_tensor(out=o, in0=pb[:, bass.ds(b, 1), lo + src:lo + src + n - 1],
                                                             scalar=taps[j], in1=o, op0=ALU.mult, op1=ALU.add).then_inc(step, 1)
                                dve.wait_ge(step, 2).then_inc(step, -2)
                            dve.sem_inc(y_full[s], 1)
                        if scale is not None:
                            for s in range(2):
                                dve.wait_ge(root_full[s], 1).then_inc(root_full[s], -1)
                                dve.reciprocal(y[s][:, :], y[s][:, :]).then_inc(step, 1)
                                dve.wait_ge(step, 1).then_inc(step, -1)
                                dve.scalar_tensor_tensor(out=z[s][:, :], in0=y[s][:, :], scalar=scale, in1=z[s][:, :],
                                                         op0=ALU.mult, op1=ALU.mult).then_inc(out_ready[s], 1)

            @block.scalar
            def _(act):
                act.wait_ge(eps_set, 1)
                for b0, scale in groups:
                    with act.Fori(0, 2) as i:
                        for s in range(2):
                            act.wait_ge(y_full[s], 1).then_inc(y_full[s], -1)
                            ins = act.activation(z[s][:, :], y[s][:, :], ACT.Silu)
                            if scale is None:
                                ins.then_inc(out_ready[s], 1)
                                continue
                            ins.then_inc(act_step, 1)
                            act.wait_ge(act_step, 1).then_inc(act_step, -1)
                            act.activation(sq[s][:, :], z[s][:, :], ACT.Square).then_inc(sq_full[s], 1)
                        if scale is not None:
                            for s in range(2):
                                act.wait_ge(norm_full[s], 1).then_inc(norm_full[s], -1)
                                for j, (t0, n) in enumerate(ALL_CHUNKS):
                                    act.activation(y[s][:, t0:t0 + n], norm[s][j][:, 0:n], ACT.Sqrt, bias=eps[:, :]).then_inc(act_step, 1)
                                act.wait_ge(act_step, 3).then_inc(act_step, -3)
                                act.sem_inc(root_full[s], 1)

            @block.tensor
            def _(pe):
                for b0, scale in groups:
                    if scale is None:
                        continue
                    with pe.Fori(0, 2) as i:
                        for s in range(2):
                            pe.wait_ge(sq_full[s], 1).then_inc(sq_full[s], -1)
                            for j, (t0, n) in enumerate(ALL_CHUNKS):
                                mm = pe.matmul(norm[s][j][:, 0:n], sb["ones"][:, :], sq[s][:, t0:t0 + n], start=True, stop=True)
                            mm.then_inc(norm_full[s], 1)

            @block.sync
            def _(sp):
                for b0, scale in groups:
                    with sp.Fori(0, 2) as i:
                        for s in range(2):
                            sp.wait_ge(out_ready[s], 1).then_inc(out_ready[s], -1)
                            sp.dma_start(qkv_dram[bass.ds(2 * i + s + b0, 1), :, :].rearrange("o p n -> p o n"),
                                         z[s][:, :].rearrange("p (o n) -> p o n", o=1)).then_inc(stored[s], 16)
                for s in range(2):
                    sp.wait_ge(stored[s], 16)


def window_prepare(nc, a, sb, pa, k_dup, v_tok):
    with Stage(nc, "wprep") as st:
        names = ("swap", "dup0", "dup1", "dupswap0", "dupswap1")
        m = {n: st.sb(n, P, P) for n in names}
        cos, sin = st.sb("cos", P, TOK), st.sb("sin", P, TOK)
        tmp = [st.sb(f"tmp{i}", P, 512) for i in range(2)]
        rot = [st.ps(f"rot{j}", P, 512) for j in range(4)]
        vt = [st.ps(f"vt{j}", P, 512) for j in range(3)]
        loaded, full, free, step, v_full = st.sem("loaded"), st.sem("full", 4), st.sem("free", 4), st.sem("step"), st.sem("v_full")
        q_free = st.sem("q_free")
        with nc.Block() as block:
            @block.sync
            def _(sp):
                for n in names:
                    sp.dma_start(m[n][:, :], a["mats"][MATS.index(n)]).then_inc(loaded, 16)
                sp.dma_start(cos[:, :], a["rope_a"][0]).then_inc(loaded, 16)
                sp.dma_start(sin[:, :], a["rope_a"][1]).then_inc(loaded, 16)

            @block.tensor
            def _(pe):
                pe.wait_ge(loaded, 112)
                with pe.Fori(0, 4) as b:
                    for j, (t0, n) in enumerate(ALL_CHUNKS):
                        pe.wait_ge(free[j], 1).then_inc(free[j], -1)
                        pe.matmul(rot[j][:, 0:n], m["swap"][:, :], pa[:, bass.ds(b, 1), t0:t0 + n].rearrange("p o n -> p (o n)"), start=True, stop=True).then_inc(full[j], 1)
                for kv in range(2):
                    for j, (t0, n) in enumerate(ALL_CHUNKS):
                        for h, name in enumerate((f"dup{kv}", f"dupswap{kv}")):
                            r = (2 * j + h) % 4
                            pe.wait_ge(free[r], 1).then_inc(free[r], -1)
                            pe.matmul(rot[r][:, 0:n], m[name][:, :], pa[:, 4, t0:t0 + n], start=True, stop=True).then_inc(full[r], 1)
                for t in range(NT):
                    mm = pe.transpose(vt[t // 4][:, t % 4 * P:(t % 4 + 1) * P], pa[:, 5, t * P:(t + 1) * P], sb["ident"][:, :])
                mm.then_inc(v_full, 1)

            @block.vector
            def _(dve):
                def done(ins, n=1):
                    ins.then_inc(step, 1)
                    dve.wait_ge(step, 1).then_inc(step, -1)

                give(dve, free)
                dve.wait_ge(loaded, 112)
                with dve.Fori(0, 4) as b:
                    for j, (t0, n) in enumerate(ALL_CHUNKS):
                        q = pa[:, bass.ds(b, 1), t0:t0 + n]
                        w = lambda ap: ap.rearrange("p (o n) -> p o n", o=1)
                        dve.wait_ge(full[j], 1).then_inc(full[j], -1)
                        done(dve.tensor_tensor(tmp[0][:, 0:n], rot[j][:, 0:n], sin[:, t0:t0 + n], ALU.mult))
                        done(dve.tensor_tensor(q, q, w(cos[:, t0:t0 + n]), ALU.mult))
                        done(dve.tensor_tensor(q, q, w(tmp[0][:, 0:n]), ALU.add))
                        dve.sem_inc(free[j], 1)
                for kv in range(2):
                    dve.memset(k_dup[:, kv, 0:P], 0.0)
                    dve.memset(k_dup[:, kv, P + TOK:], 0.0)
                    for j, (t0, n) in enumerate(ALL_CHUNKS):
                        r = (2 * j) % 4
                        dve.wait_ge(full[r], 1).then_inc(full[r], -1)
                        done(dve.tensor_tensor(tmp[0][:, 0:n], rot[r][:, 0:n], cos[:, t0:t0 + n], ALU.mult))
                        dve.sem_inc(free[r], 1)
                        dve.wait_ge(full[r + 1], 1).then_inc(full[r + 1], -1)
                        done(dve.tensor_tensor(tmp[1][:, 0:n], rot[r + 1][:, 0:n], sin[:, t0:t0 + n], ALU.mult))
                        dve.sem_inc(free[r + 1], 1)
                        done(dve.tensor_tensor(k_dup[:, kv, P + t0:P + t0 + n], tmp[0][:, 0:n], tmp[1][:, 0:n], ALU.add))
                dve.memset(v_tok[:, 0, :], 0.0)
                dve.memset(v_tok[:, NT + 1, :], 0.0)
                dve.wait_ge(v_full, 1).then_inc(v_full, -1)
                for j, (t0, n) in enumerate(ALL_CHUNKS):
                    dve.tensor_copy(v_tok[:, 1 + 4 * j:1 + 4 * j + n // P, :], vt[j][:, 0:n].rearrange("p (t d) -> p t d", d=P))


def window_attention(nc, a, sb, pa, k_dup, v_tok, x):
    W = 3 * P
    scale = float(A_DIM) ** -0.5
    PAIRS = NT // 2
    with Stage(nc, "watt") as st:
        q = [st.sb(f"q{s}", P, 4, P) for s in range(2)]
        k = [st.sb(f"k{s}", P, A_KV, W) for s in range(2)]
        mask = [st.sb(f"mask{s}", P, W) for s in range(2)]
        sink, neg_sink, sink_arg = st.sb("sink", P, A_HEADS), st.sb("neg_sink", P, A_HEADS), st.sb("sink_arg", P, 2, A_HEADS)
        prob = [st.sb(f"prob{r}", P, CTX_LEN + W) for r in range(2)]
        prob_t = st.sb("prob_t", P, CTX_LEN + W)
        top, neg_top, total, sink_exp = (st.sb(n, P, 2, A_HEADS) for n in ("top", "neg_top", "total", "sink_exp"))
        o_tok = [st.sb(f"o{s}", P, 4 * P) for s in range(2)]
        C0 = 512 - CTX_LEN
        s_ps = [st.ps(f"sps{r}", P, 1024) for r in range(2)]
        t_ps = st.ps("tps", P, 1024)
        o_ps = [st.ps(f"ops{s}", P, 512) for s in range(2)]
        q_in, q_free, mask_free = st.sem("q_in", 2), st.sem("q_free", 2), st.sem("mask_free", 2)
        mask_in, sink_in = st.sem("mask_in", 2), st.sem("sink_in")
        s_full, s_free, neg_ready = st.sem("s_full", 2), st.sem("s_free", 2), st.sem("neg_ready", 2)
        p_full, p_free, t_full, pt_full = st.sem("p_full", 2), st.sem("p_free", 2), st.sem("t_full"), st.sem("pt_full")
        o_full, o_free, o_done, ot_full = st.sem("o_full", 2), st.sem("o_free", 2), st.sem("o_done", 2), st.sem("ot_full", 2)
        arg_ready, sink_done, step, act_step = st.sem("arg_ready"), st.sem("sink_done"), st.sem("step"), st.sem("act_step")

        def over_pairs(eng, body):
            body(0, False, True)
            with eng.Fori(1, PAIRS - 1) as i:
                body(i, True, True)
            body(PAIRS - 1, True, None)

        def unit_at(n, window, nxt):
            if n >= 2 * A_HEADS:
                return None if nxt is None else (0, n - 2 * A_HEADS, nxt)
            return n // A_HEADS, n % A_HEADS, window

        with nc.Block() as block:
            @block.sync
            def _(sp):
                sp.dma_start(sink[:, :], a["ab_sink"].to_broadcast([P, A_HEADS])).then_inc(sink_in, 16)

                def body(i, window, nxt):
                    for s in range(2):
                        t = 2 * i + s
                        sp.wait_ge(q_free[s], 1).then_inc(q_free[s], -1)
                        sp.dma_start(q[s][:, :, :], pa[:, 0:4, bass.ds(t * P, P)]).then_inc(q_in[s], 16)
                        if window:
                            sp.dma_start(k[s][:, :, :], k_dup[:, :, bass.ds(t * P, W)]).then_inc(q_in[s], 16)
                            sp.wait_ge(mask_free[s], 1).then_inc(mask_free[s], -1)
                            sp.dma_start(mask[s][:, :], a["window"][bass.ds(t, 1), :, :].rearrange("o p n -> p (o n)")).then_inc(mask_in[s], 16)
                over_pairs(sp, body)

            @block.tensor
            def _(pe):
                def scores(s, h, window):
                    r, kv, lo = h % 2, h // (A_HEADS // A_KV), (h % 2) * A_DIM
                    if h == 0 and window:
                        pe.wait_ge(q_in[s], 32).then_inc(q_in[s], -32)
                    if h == 0 and not window:
                        pe.wait_ge(q_in[s], 16).then_inc(q_in[s], -16)
                    pe.wait_ge(s_free[r], 1).then_inc(s_free[r], -1)
                    qh = q[s][lo:lo + A_DIM, h // 2, :]
                    mm = pe.matmul(s_ps[r][:, C0:512], qh, k_dup[lo:lo + A_DIM, kv, P:P + CTX_LEN], start=True, stop=True)
                    if window:
                        mm = pe.matmul(s_ps[r][:, 512:512 + W], qh, k[s][lo:lo + A_DIM, kv, :], start=True, stop=True)
                    mm.then_inc(s_full[r], 1)
                    if h == A_HEADS - 1:
                        pe.drain().then_inc(q_free[s], 1)

                def turned(h, blocks):
                    r = h % 2
                    pe.wait_ge(p_full[r], 1).then_inc(p_full[r], -1)
                    for j in range(blocks):
                        mm = pe.transpose(t_ps[:, j * P:(j + 1) * P], prob[r][:, j * P:(j + 1) * P], sb["ident"][:, :])
                    mm.then_inc(t_full, 1)
                    pe.drain().then_inc(p_free[r], 1)

                def values(s, h, t, blocks):
                    kv = h // (A_HEADS // A_KV)
                    pe.wait_ge(pt_full, 1).then_inc(pt_full, -1)
                    if h == 0:
                        pe.wait_ge(o_free[s], 1).then_inc(o_free[s], -1)
                    for j in range(blocks):
                        v = (v_tok[:, 1 + j, kv * A_DIM:(kv + 1) * A_DIM] if j < CT
                             else v_tok[:, bass.ds(t + (j - CT), 1), kv * A_DIM:(kv + 1) * A_DIM].rearrange("p o n -> p (o n)"))
                        mm = pe.matmul(o_ps[s][:, h * A_DIM:(h + 1) * A_DIM], prob_t[:, j * P:(j + 1) * P], v, start=(j == 0), stop=(j == blocks - 1))
                    if h == A_HEADS - 1:
                        mm.then_inc(o_full[s], 1)

                def output_turned(s):
                    pe.wait_ge(o_done[s], 1).then_inc(o_done[s], -1)
                    for b in range(4):
                        mm = pe.transpose(o_ps[s][:, b * P:(b + 1) * P], o_tok[s][:, b * P:(b + 1) * P], sb["ident"][:, :])
                    mm.then_inc(ot_full[s], 1)

                def body(i, window, nxt):
                    for n in range(2 * A_HEADS):
                        s, h, _w = unit_at(n, window, nxt)
                        blocks = (CTX_LEN + W if window else CTX_LEN) // P
                        turned(h, blocks)
                        ahead = unit_at(n + 2, window, nxt)
                        if ahead is not None:
                            scores(*ahead)
                        values(s, h, 2 * i + s, blocks)
                        if h == 0 and (s == 1 or window):
                            output_turned(1 - s)
                scores(0, 0, False)
                scores(0, 1, False)
                over_pairs(pe, body)
                output_turned(1)

            @block.vector
            def _(dve):
                def done(ins, *to):
                    ins.then_inc(step, 1)
                    dve.wait_ge(step, 1).then_inc(step, -1)
                    for x_ in to:
                        dve.sem_inc(x_, 1)

                def maximum(s, h, window):
                    r = h % 2
                    dve.wait_ge(s_full[r], 1).then_inc(s_full[r], -1)
                    if window:
                        if h == 0:
                            dve.wait_ge(mask_in[s], 16).then_inc(mask_in[s], -16)
                        done(dve.tensor_tensor(s_ps[r][:, 512:512 + W], s_ps[r][:, 512:512 + W], mask[s][:, :], ALU.add))
                        if h == A_HEADS - 1:
                            dve.sem_inc(mask_free[s], 1)
                    done(dve.tensor_reduce(top[:, s, h:h + 1], s_ps[r][:, C0:C0 + CTX_LEN + (W if window else 0)], AX_X, ALU.max))
                    done(dve.tensor_scalar(neg_top[:, s, h:h + 1], top[:, s, h:h + 1], -scale, neg_sink[:, h:h + 1], ALU.mult, ALU.min), neg_ready[r])
                    if h == A_HEADS - 1:
                        dve.tensor_tensor(sink_arg[:, s, :], sink[:, :], neg_top[:, s, :], ALU.add).then_inc(arg_ready, 1)

                def divided(s):
                    dve.wait_ge(sink_done, 1).then_inc(sink_done, -1)
                    done(dve.tensor_tensor(total[:, s, :], total[:, s, :], sink_exp[:, s, :], ALU.add))
                    done(dve.reciprocal(total[:, s, :], total[:, s, :]))
                    dve.wait_ge(o_full[s], 1).then_inc(o_full[s], -1)
                    dve.tensor_tensor(o_tok[s][:, :].rearrange("p (h d) -> p h d", h=A_HEADS), o_ps[s][:, :].rearrange("p (h d) -> p h d", h=A_HEADS),
                                      total[:, s, :].rearrange("p (h o) -> p h o", o=1).to_broadcast([P, A_HEADS, A_DIM]), ALU.mult).then_inc(o_done[s], 1)

                def output(s, t):
                    dve.wait_ge(ot_full[s], 1).then_inc(ot_full[s], -1)
                    dve.tensor_copy(x[:, 0:4, bass.ds(t * P, P)], o_ps[s][:, :].rearrange("p (b n) -> p b n", b=4)).then_inc(o_free[s], 1)

                def body(i, window, nxt):
                    for n in range(2 * A_HEADS):
                        s, h, _w = unit_at(n, window, nxt)
                        ahead = unit_at(n + 2, window, nxt)
                        if ahead is not None:
                            maximum(*ahead)
                        if h == A_HEADS - 1:
                            divided(s)
                        if h == 0 and (s == 1 or window):
                            output(1 - s, 2 * i + s - 1)

                for g in (q_free, mask_free, o_free):
                    give(dve, g)
                dve.wait_ge(sink_in, 16)
                done(dve.tensor_scalar(neg_sink[:, :], sink[:, :], -1.0, None, ALU.mult))
                maximum(0, 0, False)
                maximum(0, 1, False)
                over_pairs(dve, body)
                output(1, NT - 1)

            @block.scalar
            def _(act):
                def exponent(s, h, window):
                    r = h % 2
                    act.wait_ge(neg_ready[r], 1).then_inc(neg_ready[r], -1)
                    act.wait_ge(p_free[r], 1).then_inc(p_free[r], -1)
                    keys = CTX_LEN + (W if window else 0)
                    act.activation(prob[r][:, 0:keys], s_ps[r][:, C0:C0 + keys], ACT.Exp, scale=scale, bias=neg_top[:, s, h:h + 1],
                                   accum_out=total[:, s, h:h + 1]).then_inc(act_step, 1)
                    act.wait_ge(act_step, 1).then_inc(act_step, -1)
                    act.sem_inc(s_free[r], 1)
                    act.sem_inc(p_full[r], 1)
                    if h == A_HEADS - 1:
                        act.wait_ge(arg_ready, 1).then_inc(arg_ready, -1)
                        act.activation(sink_exp[:, s, :], sink_arg[:, s, :], ACT.Exp).then_inc(sink_done, 1)

                def body(i, window, nxt):
                    for n in range(2 * A_HEADS):
                        keys = CTX_LEN + (W if window else 0)
                        act.wait_ge(t_full, 1).then_inc(t_full, -1)
                        act.activation(prob_t[:, 0:keys], t_ps[:, 0:keys], ACT.Copy).then_inc(pt_full, 1)
                        ahead = unit_at(n + 1, window, nxt)
                        if ahead is not None:
                            exponent(*ahead)

                give(act, s_free)
                give(act, p_free)
                exponent(0, 0, False)
                over_pairs(act, body)


def delta_rule(nc, a, sb, qkv_dram, cols, o_dirs):
    HP = [P, B_HEADS, P]
    with Stage(nc, "delta") as st:
        levels = [[st.sb(f"level{d}{l}", P, P) for l in range(LEVELS)] for d in range(2)]
        cum = [st.sb(f"cum{d}", P, P) for d in range(2)]
        dmask = [st.sb(f"dmask{d}", P, P) for d in range(2)]
        qkv = [[st.sb(f"qkv{d}{s}", P, 12, P) for s in range(2)] for d in range(2)]
        names = ("ld", "col", "dec", "egrow", "b", "aqk", "uu", "vv", "ww", "ktok", "vtok", "vn", "vt", "state")
        t = [{n: st.sb(f"{n}{d}", P, 6, B_HEADS) if n == "col" else st.sb(f"{n}{d}", *HP) for n in names} for d in range(2)]
        bank = [[st.ps(f"bank{d}{j}", *HP) for j in range(4)] for d in range(2)]
        E = lambda n: st.sem(n, 2)
        loaded = st.sem("loaded")
        qkv_in = [st.sem(f"qkv_in{d}", 2) for d in range(2)]
        qkv_free = [st.sem(f"qkv_free{d}", 2) for d in range(2)]
        ld_full, ld_free, col_full, col_free, pool_step = E("ld_full"), E("ld_free"), E("col_full"), E("col_free"), st.sem("pool_step")
        grow_full, grow_read, decay_raw, decay_full, egrow_full = E("grow_full"), E("grow_read"), E("decay_raw"), E("decay_full"), E("egrow_full")
        tok_copied, kk_full, kq_full, tok_full, tok_read, vtok_full = E("tok_copied"), E("kk_full"), E("kq_full"), E("tok_full"), E("tok_read"), E("vtok_full")
        b_full, w_psum, w_full, v_psum, u_psum, uv_full = E("b_full"), E("w_psum"), E("w_full"), E("v_psum"), E("u_psum"), E("uv_full")
        ks_full, r_full, vn_psum, vn_full = E("ks_full"), E("r_full"), E("vn_psum"), E("vn_full")
        o_full, o_read, s_psum, s_full = E("o_full"), E("o_read"), E("s_psum"), E("s_full")
        step, act_step = st.sem("step"), st.sem("act_step")

        def bc(m):
            return m[:, :].rearrange("p (o n) -> p o n", o=1).to_broadcast(HP)

        def per_head(d, kind):
            return t[d]["col"][:, kind, :].rearrange("p (h o) -> p h o", o=1).to_broadcast(HP)

        def over_chunks(eng, body):
            for s in range(CT):
                body(s, (s, CT - 1 - s))
            with eng.Fori(0, LT // 2) as i:
                for s in range(2):
                    body(s, (2 * i + s + CT, NT - 1 - s - 2 * i))

        with nc.Block() as block:
            @block.sync
            def _(sp):
                for d in range(2):
                    for l in range(LEVELS):
                        sp.dma_start(levels[d][l][:, :], a["mats"][MATS.index(f"level{d}_{l}")]).then_inc(loaded, 16)
                    sp.dma_start(cum[d][:, :], a["mats"][MATS.index(f"cum{d}")]).then_inc(loaded, 16)
                    sp.dma_start(dmask[d][:, :], a["mats"][MATS.index(f"decay_mask{d}")]).then_inc(loaded, 16)

                def load(s, tiles):
                    for d in range(2):
                        sp.wait_ge(qkv_free[d][s], 1).then_inc(qkv_free[d][s], -1)
                        sp.dma_start(qkv[d][s][:, :, :], qkv_dram.rearrange("b p n -> p b n")[:, :, bass.ds(tiles[d] * P, P)]).then_inc(qkv_in[d][s], 16)
                over_chunks(sp, load)

            @block.gpsimd
            def _(pool):
                def spread(s, tiles):
                    for d in range(2):
                        pool.wait_ge(col_free[d], 1).then_inc(col_free[d], -1)
                        pool.tensor_copy(t[d]["col"][:, :, :].rearrange("p k h -> p (k h)"),
                                         cols[:, bass.ds(tiles[d], 1), d, :, :].rearrange("p o k h -> p (o k h)")).then_inc(pool_step, 1)
                        pool.wait_ge(pool_step, 1).then_inc(pool_step, -1)
                        pool.sem_inc(col_full[d], 1)
                        pool.wait_ge(ld_free[d], 1).then_inc(ld_free[d], -1)
                        pool.tensor_copy(t[d]["ld"][:, :, :], per_head(d, 0)).then_inc(ld_full[d], 1)
                over_chunks(pool, spread)

            @block.tensor
            def _(pe):
                pe.wait_ge(loaded, 16 * 2 * (LEVELS + 2))

                def heads4(d, j, lhs, rhs, start=True, stop=True):
                    for h in range(B_HEADS):
                        mm = pe.matmul(bank[d][j][:, h, :], lhs(h), rhs(h), start=start, stop=stop)
                    return mm

                def chunk(s, tiles):
                    T = lambda d, n: (lambda h: t[d][n][:, h, :])
                    Q = lambda d: (lambda h: qkv[d][s][:, h, :])
                    K = lambda d: (lambda h: qkv[d][s][:, B_HEADS + h, :])
                    ident = lambda h: sb["ident"][:, :]
                    for d in range(2):
                        pe.wait_ge(ld_full[d], 1).then_inc(ld_full[d], -1)
                        pe.wait_ge(o_read[d], 1).then_inc(o_read[d], -1)
                        heads4(d, 0, T(d, "ld"), lambda h: cum[d][:, :]).then_inc(grow_full[d], 1)
                    for d in range(2):
                        pe.wait_ge(qkv_in[d][s], 16).then_inc(qkv_in[d][s], -16)
                        heads4(d, 1, K(d), K(d)).then_inc(kk_full[d], 1)
                        heads4(d, 2, K(d), Q(d)).then_inc(kq_full[d], 1)
                        pe.wait_ge(s_full[d], 1).then_inc(s_full[d], -1)
                        for h in range(B_HEADS):
                            pe.transpose(bank[d][3][:, h, :], K(d)(h), sb["ident"][:, :])
                        pe.wait_ge(grow_read[d], 1).then_inc(grow_read[d], -1)
                        for h in range(B_HEADS):
                            mm = pe.transpose(bank[d][0][:, h, :], qkv[d][s][:, 2 * B_HEADS + h, :], sb["ident"][:, :])
                        mm.then_inc(tok_full[d], 1)
                    for d in range(2):
                        pe.wait_ge(b_full[d], 1).then_inc(b_full[d], -1)
                        heads4(d, 1, T(d, "b"), ident).then_inc(w_psum[d], 1)
                    for l in range(1, LEVELS):
                        for d in range(2):
                            pe.wait_ge(uv_full[d], 1).then_inc(uv_full[d], -1)
                            if l == 1:
                                pe.wait_ge(tok_read[d], 1).then_inc(tok_read[d], -1)
                            heads4(d, 2, T(d, "b"), T(d, "vv")).then_inc(w_psum[d], 1)
                        for d in range(2):
                            pe.wait_ge(w_full[d], 1).then_inc(w_full[d], -1)
                            if l == 1:
                                pe.wait_ge(tok_copied[d], 1).then_inc(tok_copied[d], -1)
                            if l < LEVELS - 1:
                                heads4(d, 1, T(d, "uu"), T(d, "ww")).then_inc(v_psum[d], 1)
                            heads4(d, 3, T(d, "ww"), T(d, "uu")).then_inc(u_psum[d], 1)
                    for d in range(2):
                        heads4(d, 1, K(d), T(d, "state")).then_inc(ks_full[d], 1)
                    for d in range(2):
                        pe.wait_ge(r_full[d], 1).then_inc(r_full[d], -1)
                        heads4(d, 2, T(d, "uu"), T(d, "vv")).then_inc(vn_psum[d], 1)
                    for d in range(2):
                        pe.wait_ge(vn_full[d], 1).then_inc(vn_full[d], -1)
                        for h in range(B_HEADS):
                            pe.matmul(bank[d][0][:, h, :], t[d]["state"][:, h, :], t[d]["egrow"][:, h, :], start=True, stop=False)
                            mm = pe.matmul(bank[d][0][:, h, :], t[d]["vn"][:, h, :], t[d]["aqk"][:, h, :], start=False, stop=True)
                        mm.then_inc(o_full[d], 1)
                        heads4(d, 3, T(d, "ktok"), T(d, "vt")).then_inc(s_psum[d], 1)
                over_chunks(pe, chunk)

            @block.vector
            def _(dve):
                def done(ins, *to):
                    ins.then_inc(step, 1)
                    dve.wait_ge(step, 1).then_inc(step, -1)
                    for x in to:
                        dve.sem_inc(x, 1)

                dve.wait_ge(loaded, 16 * 2 * (LEVELS + 2))
                for d in range(2):
                    give(dve, qkv_free[d])
                    dve.memset(t[d]["state"][:, :, :], 0.0).then_inc(step, 1)
                dve.wait_ge(step, 2).then_inc(step, -2)
                for g in (col_free, ld_free, o_read, s_full):
                    give(dve, g)

                def chunk(s, tiles):
                    for d in range(2):
                        x = t[d]
                        dve.wait_ge(col_full[d], 1).then_inc(col_full[d], -1)
                        dve.wait_ge(grow_full[d], 1).then_inc(grow_full[d], -1)
                        dve.sem_inc(ld_free[d], 1)
                        for h in range(B_HEADS):
                            dve.scalar_tensor_tensor(out=x["dec"][:, h, :], in0=bank[d][0][:, h, :], scalar=x["col"][:, 1, h:h + 1],
                                                     in1=dmask[d][:, :], op0=ALU.subtract, op1=ALU.add).then_inc(step, 1)
                        dve.wait_ge(step, B_HEADS).then_inc(step, -B_HEADS)
                        dve.sem_inc(decay_raw[d], 1)
                    for d in range(2):
                        x = t[d]
                        dve.wait_ge(kk_full[d], 1).then_inc(kk_full[d], -1)
                        dve.wait_ge(decay_full[d], 1).then_inc(decay_full[d], -1)
                        for h in range(B_HEADS):
                            dve.scalar_tensor_tensor(out=x["b"][:, h, :], in0=bank[d][1][:, h, :], scalar=x["col"][:, 2, h:h + 1],
                                                     in1=x["dec"][:, h, :], op0=ALU.mult, op1=ALU.mult).then_inc(step, 1)
                        dve.wait_ge(step, B_HEADS).then_inc(step, -B_HEADS)
                        dve.sem_inc(b_full[d], 1)
                        done(dve.tensor_tensor(x["uu"][:, :, :], x["b"][:, :, :], bc(levels[1 - d][0]), ALU.mult))
                        done(dve.scalar_tensor_tensor(out=x["uu"][:, :, :], in0=x["uu"][:, :, :], scalar=-1.0, in1=bc(sb["ident"]), op0=ALU.mult, op1=ALU.add))
                    for d in range(2):
                        x = t[d]
                        dve.wait_ge(w_psum[d], 1).then_inc(w_psum[d], -1)
                        done(dve.tensor_tensor(x["vv"][:, :, :], bank[d][1][:, :, :], bc(levels[d][0]), ALU.mult))
                        done(dve.scalar_tensor_tensor(out=x["vv"][:, :, :], in0=x["vv"][:, :, :], scalar=-1.0, in1=bc(sb["ident"]), op0=ALU.mult, op1=ALU.add), uv_full[d])
                    for d in range(2):
                        x = t[d]
                        dve.wait_ge(kq_full[d], 1).then_inc(kq_full[d], -1)
                        done(dve.tensor_tensor(x["aqk"][:, :, :], bank[d][2][:, :, :], x["dec"][:, :, :], ALU.mult), tok_read[d])
                        dve.wait_ge(egrow_full[d], 1).then_inc(egrow_full[d], -1)
                        done(dve.tensor_tensor(x["egrow"][:, :, :], qkv[d][s][:, 0:B_HEADS, :], x["egrow"][:, :, :], ALU.mult))
                    for l in range(1, LEVELS):
                        for d in range(2):
                            dve.wait_ge(w_psum[d], 1).then_inc(w_psum[d], -1)
                            done(dve.tensor_tensor(t[d]["ww"][:, :, :], bank[d][2][:, :, :], bc(levels[d][l]), ALU.mult), w_full[d])
                        for d in range(2):
                            x = t[d]
                            if l < LEVELS - 1:
                                dve.wait_ge(v_psum[d], 1).then_inc(v_psum[d], -1)
                                done(dve.tensor_tensor(x["vv"][:, :, :], x["vv"][:, :, :], bank[d][1][:, :, :], ALU.subtract))
                            dve.wait_ge(u_psum[d], 1).then_inc(u_psum[d], -1)
                            done(dve.tensor_tensor(x["uu"][:, :, :], x["uu"][:, :, :], bank[d][3][:, :, :], ALU.subtract))
                            if l < LEVELS - 1:
                                dve.sem_inc(uv_full[d], 1)
                    for d in range(2):
                        x = t[d]
                        dve.wait_ge(ks_full[d], 1).then_inc(ks_full[d], -1)
                        dve.wait_ge(vtok_full[d], 1).then_inc(vtok_full[d], -1)
                        dve.sem_inc(qkv_free[d][s], 1)
                        for h in range(B_HEADS):
                            dve.scalar_tensor_tensor(out=x["vv"][:, h, :], in0=bank[d][1][:, h, :], scalar=x["col"][:, 3, h:h + 1],
                                                     in1=x["vtok"][:, h, :], op0=ALU.mult, op1=ALU.add).then_inc(step, 1)
                        dve.wait_ge(step, B_HEADS).then_inc(step, -B_HEADS)
                        dve.sem_inc(r_full[d], 1)
                    for d in range(2):
                        x = t[d]
                        dve.wait_ge(vn_psum[d], 1).then_inc(vn_psum[d], -1)
                        done(dve.tensor_tensor(x["vn"][:, :, :], bank[d][2][:, :, :], per_head(d, 2), ALU.mult))
                        done(dve.tensor_tensor(x["vt"][:, :, :], bank[d][2][:, :, :], per_head(d, 4), ALU.mult), vn_full[d])
                    for d in range(2):
                        x = t[d]
                        dve.wait_ge(s_psum[d], 1).then_inc(s_psum[d], -1)
                        for h in range(B_HEADS):
                            dve.scalar_tensor_tensor(out=x["state"][:, h, :], in0=x["state"][:, h, :], scalar=x["col"][:, 5, h:h + 1],
                                                     in1=bank[d][3][:, h, :], op0=ALU.mult, op1=ALU.add).then_inc(step, 1)
                        dve.wait_ge(step, B_HEADS).then_inc(step, -B_HEADS)
                        dve.sem_inc(s_full[d], 1)
                        dve.sem_inc(col_free[d], 1)
                over_chunks(dve, chunk)

            @block.scalar
            def _(act):
                def done(ins, *to):
                    ins.then_inc(act_step, 1)
                    act.wait_ge(act_step, 1).then_inc(act_step, -1)
                    for x in to:
                        act.sem_inc(x, 1)

                def chunk(s, tiles):
                    for d in range(2):
                        x = t[d]
                        act.wait_ge(decay_raw[d], 1).then_inc(decay_raw[d], -1)
                        done(act.activation(x["egrow"][:, :, :], bank[d][0][:, :, :], ACT.Exp), grow_read[d], egrow_full[d])
                        done(act.activation(x["dec"][:, :, :], x["dec"][:, :, :], ACT.Exp), decay_full[d])
                    for d in range(2):
                        x = t[d]
                        act.wait_ge(tok_full[d], 1).then_inc(tok_full[d], -1)
                        act.activation(x["ktok"][:, :, :], bank[d][3][:, :, :], ACT.Copy).then_inc(act_step, 1)
                        act.activation(x["vtok"][:, :, :], bank[d][0][:, :, :], ACT.Copy).then_inc(act_step, 1)
                        act.wait_ge(act_step, 2).then_inc(act_step, -2)
                        act.sem_inc(vtok_full[d], 1)
                        act.sem_inc(tok_copied[d], 1)
                    for d in range(2):
                        act.wait_ge(o_full[d], 1).then_inc(o_full[d], -1)
                        done(act.activation(o_dirs[d][:, :, bass.ds(tiles[d] * P, P)], bank[d][0][:, :, :], ACT.Copy), o_read[d])
                over_chunks(act, chunk)


def head_norm(nc, a, sb, o_f, o_b, gate):
    g_lo, _ = rows_at(ROWS_A, "out_norm")
    with Stage(nc, "hnorm") as st:
        sq = [st.sb(f"sq{s}", P, TOK) for s in range(2)]
        rt, sg = ([st.sb(f"{n}{h}", P, TOK) for h in range(B_HEADS)] for n in ("rt", "sg"))
        eps = st.sb("eps", P, 1)
        ss = [[st.ps(f"ss{s}{j}", P, 512) for j in range(3)] for s in range(2)]
        eps_set, sum_full, sq_full, ss_full, rt_full, sg_full, step = (st.sem(n) for n in
            ("eps_set", "sum_full", "sq_full", "ss_full", "rt_full", "sg_full", "step"))
        act_step = st.sem("act_step")
        with nc.Block() as block:
            @block.vector
            def _(dve):
                dve.memset(eps[:, :], EPS).then_inc(eps_set, 1)
                for h in range(B_HEADS):
                    dve.tensor_tensor(o_f[:, h, :], o_f[:, h, :], o_b[:, h, :], ALU.add).then_inc(sum_full, 1)
                for h in range(B_HEADS):
                    dve.wait_ge(rt_full, 1).then_inc(rt_full, -1)
                    dve.reciprocal(rt[h][:, :], rt[h][:, :]).then_inc(step, 1)
                    dve.wait_ge(step, 1).then_inc(step, -1)
                    dve.scalar_tensor_tensor(out=o_f[:, h, :], in0=o_f[:, h, :], scalar=sb["cols_a"][:, g_lo:g_lo + 1],
                                             in1=rt[h][:, :], op0=ALU.mult, op1=ALU.mult).then_inc(step, 1)
                    dve.wait_ge(step, 1).then_inc(step, -1)
                    dve.wait_ge(sg_full, 1).then_inc(sg_full, -1)
                    dve.tensor_tensor(o_f[:, h, :], o_f[:, h, :], sg[h][:, :], ALU.mult).then_inc(step, 1)
                    dve.wait_ge(step, 1).then_inc(step, -1)

            @block.scalar
            def _(act):
                act.wait_ge(eps_set, 1)
                for h in range(B_HEADS):
                    s = h % 2
                    act.wait_ge(sum_full, h + 1)
                    act.activation(sq[s][:, :], o_f[:, h, :], ACT.Square).then_inc(sq_full, 1)
                    act.wait_ge(ss_full, h + 1)
                    for j, (t0, n) in enumerate(ALL_CHUNKS):
                        act.activation(rt[h][:, t0:t0 + n], ss[s][j][:, 0:n], ACT.Sqrt, scale=1.0 / B_DIM, bias=eps[:, :]).then_inc(act_step, 1)
                    act.wait_ge(act_step, 3).then_inc(act_step, -3)
                    act.sem_inc(rt_full, 1)
                for h in range(B_HEADS):
                    act.activation(sg[h][:, :], gate[:, h, :], ACT.Silu).then_inc(sg_full, 1)

            @block.tensor
            def _(pe):
                for h in range(B_HEADS):
                    s = h % 2
                    pe.wait_ge(sq_full, h + 1)
                    for j, (t0, n) in enumerate(ALL_CHUNKS):
                        mm = pe.matmul(ss[s][j][:, 0:n], sb["ones"][:, :], sq[s][:, t0:t0 + n], start=True, stop=True)
                    mm.then_inc(ss_full, 1)


def latent_norms(nc, a, sb, c5, kpe, kpe_rot):
    q_lo, _ = rows_at(ROWS_A, "q_norm")
    with Stage(nc, "lnorm") as st:
        sq = [st.sb(f"sq{b}", P, TOK) for b in range(5)]
        rt = st.sb("rt", P, 2, TOK)
        place, swap = st.sb("place", P, P), st.sb("swap", P, P)
        cos, sin = st.sb("cos", P, TOK), st.sb("sin", P, TOK)
        tmp = [st.sb(f"tmp{i}", P, 512) for i in range(2)]
        eps = st.sb("eps", P, 1)
        ss = [[st.ps(f"ss{g}{j}", P, 512) for j in range(3)] for g in range(2)]
        rot = [st.ps(f"rot{i}", P, 512) for i in range(2)]
        loaded, eps_set, sq_full, ss_full, act_step, rt_full, step, rot_full, rot_free = (st.sem(n) for n in
            ("loaded", "eps_set", "sq_full", "ss_full", "act_step", "rt_full", "step", "rot_full", "rot_free"))
        groups = ((range(0, 3), QR, LAT_CHUNKS), (range(3, 5), KVR, ALL_CHUNKS))
        rr = slice(C_NOPE, C_QK)
        with nc.Block() as block:
            @block.sync
            def _(sp):
                sp.dma_start(place[:, :], a["mats"][MATS.index("kpe_place")]).then_inc(loaded, 16)
                sp.dma_start(swap[:, :], a["mats"][MATS.index("kpe_swap")]).then_inc(loaded, 16)
                sp.dma_start(cos[:, :], a["rope_c"][0]).then_inc(loaded, 16)
                sp.dma_start(sin[:, :], a["rope_c"][1]).then_inc(loaded, 16)

            @block.scalar
            def _(act):
                act.wait_ge(eps_set, 1)
                for b in range(5):
                    lo = CTX_LEN if b < 3 else 0
                    act.activation(sq[b][:, lo:], c5[:, b, lo:], ACT.Square).then_inc(sq_full, 1)
                for g, (blocks, rank, chunks) in enumerate(groups):
                    for j, (t0, n) in enumerate(chunks):
                        act.wait_ge(ss_full, 1).then_inc(ss_full, -1)
                        act.activation(rt[:, g, t0:t0 + n], ss[g][j][:, 0:n], ACT.Sqrt, scale=1.0 / rank, bias=eps[:, :]).then_inc(rt_full, 1)

            @block.tensor
            def _(pe):
                for g, (blocks, rank, chunks) in enumerate(groups):
                    pe.wait_ge(sq_full, blocks[-1] + 1)
                    for j, (t0, n) in enumerate(chunks):
                        for b in blocks:
                            mm = pe.matmul(ss[g][j][:, 0:n], sb["ones"][:, :], sq[b][:, t0:t0 + n], start=(b == blocks[0]), stop=(b == blocks[-1]))
                        mm.then_inc(ss_full, 1)
                pe.wait_ge(loaded, 64)
                for j, (t0, n) in enumerate(ALL_CHUNKS):
                    pe.wait_ge(rot_free, 1).then_inc(rot_free, -1)
                    pe.matmul(rot[0][:, 0:n], place[0:C_ROPE, :], kpe[:, 0, t0:t0 + n], start=True, stop=True)
                    pe.matmul(rot[1][:, 0:n], swap[0:C_ROPE, :], kpe[:, 0, t0:t0 + n], start=True, stop=True).then_inc(rot_full, 1)

            @block.vector
            def _(dve):
                def done(ins, n=1):
                    ins.then_inc(step, 1)
                    dve.wait_ge(step, 1).then_inc(step, -1)

                dve.memset(eps[:, :], EPS).then_inc(eps_set, 1)
                dve.wait_ge(loaded, 64)
                give(dve, [rot_free])
                for g, (blocks, rank, chunks) in enumerate(groups):
                    dve.wait_ge(rt_full, len(chunks)).then_inc(rt_full, -len(chunks))
                    lo = chunks[0][0]
                    done(dve.reciprocal(rt[:, g, lo:], rt[:, g, lo:]))
                    for b in blocks:
                        dve.scalar_tensor_tensor(out=c5[:, b, lo:], in0=c5[:, b, lo:], scalar=sb["cols_a"][:, q_lo + b:q_lo + b + 1],
                                                 in1=rt[:, g, lo:], op0=ALU.mult, op1=ALU.mult)
                for j, (t0, n) in enumerate(ALL_CHUNKS):
                    dve.wait_ge(rot_full, 1).then_inc(rot_full, -1)
                    dve.tensor_tensor(tmp[0][rr, 0:n], rot[0][rr, 0:n], cos[rr, t0:t0 + n], ALU.mult).then_inc(step, 1)
                    dve.tensor_tensor(tmp[1][rr, 0:n], rot[1][rr, 0:n], sin[rr, t0:t0 + n], ALU.mult).then_inc(step, 1)
                    dve.wait_ge(step, 2).then_inc(step, -2)
                    dve.sem_inc(rot_free, 1)
                    done(dve.tensor_tensor(kpe_rot[rr, t0:t0 + n], tmp[0][rr, 0:n], tmp[1][rr, 0:n], ALU.add))


def latent_attention(nc, a, sb, c5, kpe_rot, x):
    scale = float(C_QK) ** -0.5
    NQ = LT
    AUG = C_QK + 1
    rr = slice(C_NOPE, C_QK)
    row = slice(C_QK, AUG)
    units = [(kt, half) for kt in range(NT) for half in range(2)]
    NS, NR = 3, 3
    NPT, LAG = 4, 2
    with Stage(nc, "latt") as st:
        wq = [st.sb(f"wq{s}", P, 3, C_QK) for s in range(2)]
        wkv = [st.sb(f"wkv{s}", P, 2, C_NOPE + C_V) for s in range(2)]
        q_swap = st.sb("q_swap", P, P)
        cos, sin = st.sb("cos", P, SEQ), st.sb("sin", P, SEQ)
        kt, qt = st.sb("kt", P, TOK), st.sb("qt", P, SEQ)
        kt_part = [[st.sb_r(f"kt{s}{x}", P, TOK) for x in range(2)] for s in range(2)]
        qt_part = [[st.sb_r(f"qt{s}{x}", P, SEQ) for x in range(2)] for s in range(2)]
        vt = [st.sb(f"vt{s}", P, NT, C_V + 1) for s in range(2)]
        prob = [st.sb(f"prob{r}", P, 512) for r in range(NPT)]
        tmp = st.sb("tmp", P, 512)
        o_tok = st.sb("o_tok", P, NQ, 2 * C_V)
        part_max = st.sb("part_max", P, NQ, 3)
        neg_max = st.sb("neg_max", P, NQ)
        rec = st.sb("rec", P, 2, 4)
        s_ps = [st.ps(f"s{r}", P, 512) for r in range(NS)]
        ring = [st.ps(f"ring{r}", P, 512) for r in range(NR)]
        o_ps = [st.ps(f"o{half}", P, 4, P) for half in range(2)]
        w_in, w_free = st.sem("w_in", 2), st.sem("w_free", 2)
        loaded, ones_set = st.sem("loaded"), st.sem("ones_set")
        ring_full, ring_free, q_copied = st.sem("ring_full", NR), st.sem("ring_free", NR), st.sem("q_copied")
        r_ready, neg_ready, head_ready = st.sem("r_ready"), st.sem("neg_ready"), st.sem("head_ready")
        rounded, hi_ready = st.sem("rounded"), st.sem("hi_ready")
        s_full, s_free = st.sem("s_full", NS), st.sem("s_free", NS)
        p_full, p_free = st.sem("p_full", NPT), st.sem("p_free", NPT)
        o_full, o_free, step, act_step = st.sem("o_full"), st.sem("o_free"), st.sem("step"), st.sem("act_step")
        pair_done = st.sem("pair_done")
        q_fixed, k_copied = st.sem("q_fixed"), st.sem("k_copied")
        n_units = len(units)

        def turns():
            n = 0
            while True:
                yield n % NR
                n += 1

        def over_heads(eng, prepare, main, pair):
            for piece in prepare(0):
                piece()
            main(0, prepare(1))
            main(1, prepare(0))
            with eng.Fori(1, C_HEADS // 2 - 1) as i:
                main(0, prepare(1, pair(i - 1)))
                main(1, prepare(0))
            main(0, prepare(1, pair(C_HEADS // 2 - 2)))
            main(1, [])
            for piece in pair(C_HEADS // 2 - 1):
                piece()

        with nc.Block() as block:
            @block.sync
            def _(sp):
                sp.dma_start(q_swap[:, :], a["mats"][MATS.index("q_swap")]).then_inc(loaded, 16)
                sp.dma_start(cos[:, :], a["rope_c"][0, :, CTX_LEN:]).then_inc(loaded, 16)
                sp.dma_start(sin[:, :], a["rope_c"][1, :, CTX_LEN:]).then_inc(loaded, 16)
                wq_v = a["mla_w_qb"][0].rearrange("(k p) n -> p k n", p=P)
                wkv_v = a["mla_w_kvb"][0].rearrange("(k p) n -> p k n", p=P)
                with sp.Fori(0, C_HEADS // 2) as i:
                    for s in range(2):
                        sp.wait_ge(w_free[s], 1).then_inc(w_free[s], -1)
                        sp.dma_start(wq[s][:, :, :], wq_v[:, :, bass.ds((2 * i + s) * C_QK, C_QK)]).then_inc(w_in[s], 16)
                        sp.dma_start(wkv[s][:, :, :], wkv_v[:, :, bass.ds((2 * i + s) * (C_NOPE + C_V), C_NOPE + C_V)]).then_inc(w_in[s], 16)

            @block.tensor
            def _(pe):
                turn = turns()
                pe.wait_ge(loaded, 48)
                pe.wait_ge(ones_set, 1)

                def prepare(s, after=()):
                    def query(j):
                        t0, n = LAT_CHUNKS[j]
                        if j == 0:
                            pe.wait_ge(w_in[s], 32).then_inc(w_in[s], -32)
                        r = next(turn)
                        pe.wait_ge(ring_free[r], 1).then_inc(ring_free[r], -1)
                        for k in range(3):
                            mm = pe.matmul(ring[r][0:C_QK, 0:n], wq[s][:, k, :], c5[:, k, t0:t0 + n], start=(k == 0), stop=(k == 2))
                        mm.then_inc(ring_full[r], 1)

                    def rotate(j):
                        pe.wait_ge(q_copied, 1).then_inc(q_copied, -1)
                        r = next(turn)
                        pe.wait_ge(ring_free[r], 1).then_inc(ring_free[r], -1)
                        pe.matmul(ring[r][:, :], q_swap[0:C_QK, :], qt[0:C_QK, j * 512:(j + 1) * 512], start=True, stop=True).then_inc(ring_full[r], 1)

                    def key(j):
                        t0, n = ALL_CHUNKS[j]
                        r = next(turn)
                        pe.wait_ge(ring_free[r], 1).then_inc(ring_free[r], -1)
                        for k in range(2):
                            mm = pe.matmul(ring[r][0:C_NOPE, 0:n], wkv[s][:, k, 0:C_NOPE], c5[:, 3 + k, t0:t0 + n], start=(k == 0), stop=(k == 1))
                        mm.then_inc(ring_full[r], 1)

                    def value(t0, t1):
                        r = next(turn)
                        pe.wait_ge(ring_free[r], 1).then_inc(ring_free[r], -1)
                        for t in range(t0, t1):
                            for k in range(2):
                                mm = pe.matmul(ring[r][:, (t - t0) * C_V:(t - t0 + 1) * C_V], c5[:, 3 + k, t * P:(t + 1) * P], wkv[s][:, k, C_NOPE:], start=(k == 0), stop=(k == 1))
                        mm.then_inc(ring_full[r], 1)

                    def maxima(qb, j):
                        if qb == 0 and j == 0:
                            pe.wait_ge(r_ready, 1).then_inc(r_ready, -1)
                        t0, n = ALL_CHUNKS[j]
                        r = next(turn)
                        pe.wait_ge(ring_free[r], 1).then_inc(ring_free[r], -1)
                        pe.matmul(ring[r][:, 0:n], qt_part[s][0][0:C_QK, qb * P:(qb + 1) * P], kt_part[s][0][0:C_QK, t0:t0 + n], start=True, stop=True).then_inc(ring_full[r], 1)

                    def negated(j):
                        if j == 0:
                            pe.wait_ge(neg_ready, 1).then_inc(neg_ready, -1)
                        r = next(turn)
                        pe.wait_ge(ring_free[r], 1).then_inc(ring_free[r], -1)
                        for q in range(4):
                            mm = pe.matmul(ring[r][C_QK:AUG, q * P:(q + 1) * P], neg_max[:, 4 * j + q:4 * j + q + 1], sb["ident"][:, :], start=True, stop=True)
                        mm.then_inc(ring_full[r], 1)

                    return ([lambda j=j: query(j) for j in range(2)] + [lambda: key(0), lambda: rotate(0), lambda: key(1), lambda: rotate(1), lambda: key(2)]
                            + [lambda: value(0, 8), lambda: value(8, NT)] + list(after) + [lambda: None] * (4 - len(after))
                            + [lambda q=q, j=j: maxima(q, j) for q in range(NQ) for j in range(3)]
                            + [lambda: None] * 3 + [lambda: negated(0), lambda: negated(1)])

                def scores(s, n):
                    t, half = units[n]
                    r = n % NS
                    pe.wait_ge(s_free[r], 1).then_inc(s_free[r], -1)
                    for k_, q_ in ((0, 0), (1, 0), (0, 1)):
                        mm = pe.matmul(s_ps[r][:, :], kt_part[s][k_][0:AUG, t * P:(t + 1) * P], qt_part[s][q_][0:AUG, half * 512:(half + 1) * 512],
                                       start=(k_ + q_ == 0), stop=(q_ == 1))
                    mm.then_inc(s_full[r], 1)

                def values(s, n):
                    t, half = units[n]
                    r = n % NPT
                    if n == 0:
                        pe.wait_ge(o_free, 1).then_inc(o_free, -1)
                    pe.wait_ge(p_full[r], 1).then_inc(p_full[r], -1)
                    for q in range(4):
                        mm = pe.matmul(o_ps[half][:, q, 0:C_V + 1], prob[r][:, q * P:(q + 1) * P], vt[s][:, t, :],
                                       start=(t == 0 and q == 0), stop=(t == NT - 1), skip_group_check=True)
                    mm.then_inc(p_free[r], 1)

                def main(s, pieces):
                    pieces = list(pieces)
                    pe.wait_ge(head_ready, 1).then_inc(head_ready, -1)
                    for n in range(n_units + LAG):
                        if n < n_units:
                            scores(s, n)
                        if pieces:
                            pieces.pop(0)()
                        if n >= LAG:
                            values(s, n - LAG)
                        for _ in range(1 if n < n_units // 3 else 2):
                            if pieces:
                                pieces.pop(0)()
                    assert not pieces
                    pe.drain().then_inc(o_full, 1)

                def pair(i):
                    def turned(j):
                        if j == 0:
                            pe.wait_ge(pair_done, 1).then_inc(pair_done, -1)
                        r = next(turn)
                        pe.wait_ge(ring_free[r], 1).then_inc(ring_free[r], -1)
                        for q in range(4):
                            mm = pe.transpose(ring[r][:, q * P:(q + 1) * P], o_tok[:, 4 * j + q, :], sb["ident"][:, :])
                        mm.then_inc(ring_full[r], 1)
                    return [lambda j=j: turned(j) for j in range(2)]
                over_heads(pe, prepare, main, pair)

            @block.vector
            def _(dve):
                turn = turns()
                def done(ins, *to):
                    ins.then_inc(step, 1)
                    dve.wait_ge(step, 1).then_inc(step, -1)
                    for x_ in to:
                        dve.sem_inc(x_, 1)

                dve.wait_ge(loaded, 48)
                for g in (w_free, ring_free):
                    give(dve, g)
                give(dve, [o_free])
                for s in range(2):
                    hi, lo = kt_part[s]
                    dve.memset(vt[s][:, :, C_V:], 1.0)
                    done(dve.memset(kt[row, :], 1.0))
                    done(dve.tensor_copy(hi[rr, :], kpe_rot[rr, :]))
                    done(dve.tensor_tensor(lo[rr, :], kpe_rot[rr, :], hi[rr, :].bitcast(F32), ALU.subtract))
                    done(dve.tensor_copy(hi[row, :], kt[row, :]))
                    done(dve.tensor_tensor(lo[row, :], kt[row, :], kt[row, :], ALU.subtract))
                dve.sem_inc(ones_set, 1)

                def prepare(s, after=()):
                    def query(j):
                        r = next(turn)
                        dve.wait_ge(ring_full[r], 1).then_inc(ring_full[r], -1)
                        done(dve.tensor_copy(qt[0:C_QK, j * 512:(j + 1) * 512], ring[r][0:C_QK, :]), ring_free[r], q_copied)

                    def rotate(j):
                        c = slice(j * 512, (j + 1) * 512)
                        r = next(turn)
                        dve.wait_ge(ring_full[r], 1).then_inc(ring_full[r], -1)
                        done(dve.tensor_tensor(tmp[rr, :], ring[r][rr, :], sin[rr, c], ALU.mult), ring_free[r])
                        done(dve.tensor_tensor(qt[rr, c], qt[rr, c], cos[rr, c], ALU.mult))
                        done(dve.tensor_tensor(qt[rr, c], qt[rr, c], tmp[rr, :], ALU.add))
                        if j == 1:
                            dve.sem_inc(q_fixed, 1)

                    def key(j):
                        t0, n = ALL_CHUNKS[j]
                        r = next(turn)
                        dve.wait_ge(ring_full[r], 1).then_inc(ring_full[r], -1)
                        done(dve.tensor_copy(kt[0:C_NOPE, t0:t0 + n], ring[r][0:C_NOPE, 0:n]), ring_free[r])
                        if j == 2:
                            dve.sem_inc(k_copied, 1)

                    def value(t0, t1):
                        r = next(turn)
                        dve.wait_ge(ring_full[r], 1).then_inc(ring_full[r], -1)
                        if t1 == NT:
                            dve.sem_inc(w_free[s], 1)
                        done(dve.tensor_copy(vt[s][:, t0:t1, 0:C_V], ring[r][:, 0:(t1 - t0) * C_V].rearrange("p (t d) -> p t d", d=C_V)), ring_free[r])

                    def maxima(qb, j):
                        t0, n = ALL_CHUNKS[j]
                        r = next(turn)
                        dve.wait_ge(ring_full[r], 1).then_inc(ring_full[r], -1)
                        top = dve.tensor_reduce(part_max[:, qb, j:j + 1], ring[r][:, 0:n], AX_X, ALU.max)
                        if qb < NQ - 1:
                            top.then_inc(ring_free[r], 1)
                        else:
                            done(top, ring_free[r])
                        if qb == NQ - 1 and j == 2:
                            done(dve.tensor_reduce(neg_max[:, :], part_max[:, :, :], AX_X, ALU.max))
                            done(dve.tensor_scalar(neg_max[:, :], neg_max[:, :], -1.0, None, ALU.mult), neg_ready)

                    def low_part(x, parts, rows, c):
                        dve.wait_ge(hi_ready, 1).then_inc(hi_ready, -1)
                        done(dve.tensor_tensor(parts[1][rows, c], x[rows, c], parts[0][rows, c].bitcast(F32), ALU.subtract))

                    def negated(j):
                        r = next(turn)
                        dve.wait_ge(ring_full[r], 1).then_inc(ring_full[r], -1)
                        hi, lo = (x_[row, j * 512:(j + 1) * 512] for x_ in qt_part[s])
                        done(dve.tensor_copy(hi, ring[r][row, :]))
                        done(dve.tensor_tensor(lo, ring[r][row, :], hi.bitcast(F32), ALU.subtract), ring_free[r])
                        if j == 1:
                            dve.sem_inc(head_ready, 1)

                    lows = ([lambda j=j: low_part(qt, qt_part[s], slice(0, C_QK), slice(j * 512, (j + 1) * 512)) for j in range(2)]
                            + [lambda t0=t0, n=n: low_part(kt, kt_part[s], slice(0, C_NOPE), slice(t0, t0 + n)) for t0, n in ALL_CHUNKS])
                    return ([lambda j=j: query(j) for j in range(2)] + [lambda: key(0), lambda: rotate(0), lambda: key(1), lambda: rotate(1), lambda: key(2)]
                            + [lambda: value(0, 8), lambda: value(8, NT)] + list(after) + [lambda: None] * (4 - len(after))
                            + [piece for q in range(NQ) for piece in [lambda j=j, q=q: maxima(q, j) for j in range(3)] + lows[q:q + 1]]
                            + [lambda j=j: negated(j) for j in range(2)])

                def main(s, pieces):
                    for piece in pieces:
                        piece()
                    dve.wait_ge(o_full, 1).then_inc(o_full, -1)
                    for half in range(2):
                        done(dve.reciprocal(rec[:, half, :], o_ps[half][:, :, C_V]))
                        done(dve.tensor_tensor(o_tok[:, 4 * half:4 * half + 4, s * C_V:(s + 1) * C_V], o_ps[half][:, :, 0:C_V],
                                               rec[:, half, :].rearrange("p (q o) -> p q o", o=1).to_broadcast([P, 4, C_V]), ALU.mult))
                    dve.sem_inc(o_free, 1)
                    if s == 1:
                        dve.sem_inc(pair_done, 1)

                def pair(i):
                    def output(j):
                        r = next(turn)
                        dve.wait_ge(ring_full[r], 1).then_inc(ring_full[r], -1)
                        done(dve.tensor_copy(x[:, bass.ds(i, 1), CTX_LEN + j * 512:CTX_LEN + (j + 1) * 512], ring[r][:, :].rearrange("p (o n) -> p o n", o=1)), ring_free[r])
                    return [lambda j=j: output(j) for j in range(2)]
                over_heads(dve, prepare, main, pair)

            @block.scalar
            def _(act):
                give(act, s_free)

                def prepare(s, after=()):
                    def round_query(j):
                        c = slice(j * 512, (j + 1) * 512)
                        if j == 0:
                            act.wait_ge(q_fixed, 1).then_inc(q_fixed, -1)
                        act.activation(qt_part[s][0][0:C_QK, c], qt[0:C_QK, c], ACT.Copy).then_inc(rounded, 1)

                    def round_key(j):
                        t0, n = ALL_CHUNKS[j]
                        if j == 0:
                            act.wait_ge(k_copied, 1).then_inc(k_copied, -1)
                        act.activation(kt_part[s][0][0:C_NOPE, t0:t0 + n], kt[0:C_NOPE, t0:t0 + n], ACT.Copy).then_inc(rounded, 1)
                        if j == 2:
                            act.wait_ge(rounded, 5).then_inc(rounded, -5)
                            act.sem_inc(r_ready, 1)
                            act.sem_inc(hi_ready, 5)
                    return [lambda j=j: round_query(j) for j in range(2)] + [lambda j=j: round_key(j) for j in range(3)]

                def main(s, pieces):
                    pieces = list(pieces)
                    for n in range(n_units):
                        r, b = n % NS, n % NPT
                        act.wait_ge(s_full[r], 1).then_inc(s_full[r], -1)
                        act.wait_ge(p_free[b], 1).then_inc(p_free[b], -1)
                        act.activation(prob[b][:, :], s_ps[r][:, :], ACT.Exp, scale=scale).then_inc(act_step, 1)
                        act.wait_ge(act_step, 1).then_inc(act_step, -1)
                        act.sem_inc(s_free[r], 1)
                        act.sem_inc(p_full[b], 1)
                        for _ in range(2 if n >= 3 else 0):
                            if pieces:
                                pieces.pop(0)()
                for r in range(NPT):
                    act.sem_inc(p_free[r], 1)
                over_heads(act, prepare, main, lambda i: ())


def program(nc, a, out):
    Stage.used_semaphores = []
    with ExitStack() as ctx:
        def sbt(name, *shape):
            return ctx.enter_context(nc.sbuf_tensor(name, list(shape), F32))

        sb = {
            "ident": sbt("ident", P, P), "ones": sbt("ones", P, P),
            "cols_a": sbt("cols_a", P, P), "cols_b": sbt("cols_b", P, P),
            "silu_c": sbt("silu_c", P, KD, 2),
            "coef": sbt("coef", P, DEPTH, 2, 2, 3, KD),
        }
        h_ctx = nc.dram_tensor("h_ctx", (CTX_LEN, D_MODEL), F32, kind="Internal").ap()
        h_lat = nc.dram_tensor("h_lat", (SEQ, D_MODEL), F32, kind="Internal").ap()
        x, cx = a["x"][0], a["ctx"][0]
        u = sbt("u", P, KD, TOK)
        load_constants(nc, a, sb)
        adaln(nc, a, sb)
        norms(nc, a, sb, "norm_ab", [(1, 0, CT, cx, None), (0, CT, LT, x, None)], layer_u=(0, 0), u=u)
        x_mix = u
        qkv_dram = nc.dram_tensor("qkv_dram", (12, P, TOK), F32, kind="Internal").ap()
        cols = sbt("cols", P, NT, 2, 6, B_HEADS)
        with Stage(nc, "layer0") as l0:
            pa = l0.sb("pa", P, 10, TOK)
            decay_columns(nc, a, sb, u, cols)
            with Stage(nc, "layer0b") as l0b:
                pb = l0b.sb("pb", P, 12, TOK)
                w = a["ab_w_in"][0]
                project(nc, "in_ab", [(w, 0, P, 6, pa, 0), (w, 2304, P, 4, pa, 6), (w, 768, P, 12, pb, 0)], u, KD, ALL_CHUNKS)
                conv_qkv(nc, a, sb, pb, qkv_dram)
            with Stage(nc, "layer0c") as l0c:
                k_dup = l0c.sb("k_dup", P, A_KV, (NT + 2) * P)
                v_tok = l0c.sb("v_tok", P, NT + 2, P)
                window_prepare(nc, a, sb, pa, k_dup, v_tok)
                window_attention(nc, a, sb, pa, k_dup, v_tok, x_mix)
            Stage.recycle(nc)
            delta_rule(nc, a, sb, qkv_dram, cols, (x_mix[:, 4:8, :], pa[:, 0:4, :]))
            head_norm(nc, a, sb, x_mix[:, 4:8, :], pa[:, 0:4, :], pa[:, 6:10, :])
        Stage.recycle(nc)
        cond_tiles = ((1, 0, CT), (0, CT, LT))
        with Stage(nc, "out0") as st:
            y = st.sb("y", P, KD, TOK)
            project(nc, "out_ab", [(a["ab_w_out"][0], 0, P, KD, y, 0)], x_mix, KD, ALL_CHUNKS)
            norms(nc, a, sb, "res_ab", [(*cond_tiles[0], cx, h_ctx), (*cond_tiles[1], x, h_lat)],
                  layer_y=(0, 0), y=y, layer_u=(0, 1), u=u)

        def ffn_of(layer, chunks):
            ffn(nc, f"ffn{layer}", a["ffn_w_gate"][layer], a["ffn_w_up"][layer], a["ffn_w_down"][layer], u, chunks)

        ffn_of(0, ALL_CHUNKS)
        norms(nc, a, sb, "res_ffn0", [(*cond_tiles[0], h_ctx, None), (*cond_tiles[1], h_lat, h_lat)],
              layer_y=(0, 1), y=u, layer_u=(1, 0), u=u)
        Stage.recycle(nc)

        with Stage(nc, "layer1") as l1:
            c5, kpe, kpe_rot = l1.sb("c5", P, 5, TOK), l1.sb("kpe", C_ROPE, 1, TOK), l1.sb("kpe_rot", P, TOK)
            w = a["mla_w_in"][0]
            project(nc, "in_mla", [(w, 0, P, 5, c5, 0), (w, QR + KVR, C_ROPE, 1, kpe, 0)], u, KD, ALL_CHUNKS)
            latent_norms(nc, a, sb, c5, kpe, kpe_rot)
            latent_attention(nc, a, sb, c5, kpe_rot, u)
        with Stage(nc, "out1") as st:
            y = st.sb("y", P, KD, TOK)
            project(nc, "out_mla", [(a["mla_w_out"][0], 0, P, KD, y, 0)], u, KD, LAT_CHUNKS)
            Stage.recycle(nc)
            norms(nc, a, sb, "res_mla", [(*cond_tiles[1], h_lat, h_lat)], layer_y=(1, 0), y=y, layer_u=(1, 1), u=u)
        ffn_of(1, LAT_CHUNKS)
        norms(nc, a, sb, "res_ffn1", [(*cond_tiles[1], h_lat, out[0])], layer_y=(1, 1), y=u)


def tables():
    i = np.arange(P)
    eye = np.eye(P, dtype=np.float32)

    def pick(src, rows=P):
        m = np.zeros((P, P), np.float32)
        for out, s in enumerate(src):
            if s is not None:
                m[s, out] = 1.0
        return m

    half = A_DIM // 2
    mats = {"ident": eye, "ones": np.ones((P, P), np.float32)}
    swap = [(m // A_DIM) * A_DIM + (m % A_DIM + half) % A_DIM for m in i]
    mats["swap"] = pick(swap)
    for kv in range(2):
        mats[f"dup{kv}"] = pick([kv * A_DIM + m % A_DIM for m in i])
        mats[f"dupswap{kv}"] = pick([kv * A_DIM + (m % A_DIM + half) % A_DIM for m in i])
    hr = C_ROPE // 2
    mats["kpe_place"] = pick([m - C_NOPE if C_NOPE <= m < C_QK else None for m in i])
    mats["kpe_swap"] = pick([(m - C_NOPE + hr) % C_ROPE if C_NOPE <= m < C_QK else None for m in i])
    mats["q_swap"] = pick([C_NOPE + (m - C_NOPE + hr) % C_ROPE if C_NOPE <= m < C_QK else None for m in i])
    upto = (i[:, None] <= i[None, :])
    mats["cum0"], mats["cum1"] = upto.astype(np.float32), upto.T.astype(np.float32)
    mats["decay_mask0"] = np.where(upto, 0, NEG).astype(np.float32)
    mats["decay_mask1"] = np.where(upto.T, 0, NEG).astype(np.float32)
    for l in range(LEVELS):
        b = i >> l
        m = ((b[:, None] >> 1) == (b[None, :] >> 1)) & (b[:, None] % 2 == 1) & (b[None, :] % 2 == 0)
        mats[f"level0_{l}"], mats[f"level1_{l}"] = m.astype(np.float32), m.T.astype(np.float32)

    def rope(dim):
        n = dim // 4
        inv = (np.float32(10000.0) ** (-np.arange(n, dtype=np.float32) / n)).astype(np.float32)
        t = np.arange(SEQ)
        ang = np.concatenate([(t // GRID_W)[None, :] * inv[:, None], (t % GRID_W)[None, :] * inv[:, None]], 0).astype(np.float32)
        c, s = np.cos(ang), np.sin(ang)
        cos = np.ones((dim, TOK), np.float32)
        sin = np.zeros((dim, TOK), np.float32)
        cos[:, CTX_LEN:] = np.concatenate([c, c], 0)
        sin[:, CTX_LEN:] = np.concatenate([-s, s], 0)
        return cos, sin

    rope_a = np.stack([np.tile(x, (2, 1)) for x in rope(A_DIM)])
    rope_c = np.zeros((2, P, TOK), np.float32)
    rope_c[:, C_NOPE:C_QK] = np.stack(rope(C_ROPE))
    rel = np.arange(3 * P)[None, :] - P - i[:, None]
    window = np.full((NT, P, 3 * P), NEG, np.float32)
    for t in range(CT, NT):
        key = (t - CT) * P - P + np.arange(3 * P)
        window[t] = np.where((np.abs(rel) <= 128) & ((key >= 0) & (key < SEQ))[None, :], 0, NEG)
    return {"mats": np.stack([mats[m] for m in MATS]), "rope_a": rope_a.astype(np.float32),
            "rope_c": rope_c, "window": window}


INPUTS = ["x", "c", "ctx", "c_ctx", "mod_w", "mod_b", "norm_gains", "ffn_w_gate", "ffn_w_up", "ffn_w_down",
          "ab_w_in", "ab_sink", "ab_conv", "ab_a_log", "ab_dt_bias", "ab_out_norm", "ab_w_out",
          "mla_w_in", "mla_q_norm", "mla_kv_norm", "mla_w_qb", "mla_w_kvb", "mla_w_out"]


def kernel(**inputs):
    import concourse.bacc as bacc
    from concourse.bass_utils import run_bass_kernel_spmd

    nc = bacc.Bacc("TRN2", target_bir_lowering=False, num_devices=1)
    arrays = {n: np.ascontiguousarray(inputs[n]) for n in INPUTS}
    arrays.update(tables())
    aps = {n: nc.dram_tensor(f"in_{n}", v.shape, F32, kind="ExternalInput").ap() for n, v in arrays.items()}
    out = nc.dram_tensor("out", (1, SEQ, D_MODEL), F32, kind="ExternalOutput").ap()
    program(nc, aps, out)
    r = run_bass_kernel_spmd(nc, [{f"in_{n}": v for n, v in arrays.items()}], core_ids=[0])
    return r.results[0]["out"]
```

```python
from contextlib import ExitStack

import numpy as np
import concourse.bass as bass
from concourse import mybir

ALU = mybir.AluOpType
ACT = mybir.ActivationFunctionType
F32 = mybir.dt.float32
AX_X = mybir.AxisListType.X

P = 128
D_MODEL, SEQ, CTX_LEN, DEPTH, GRID_W = 1024, 1024, 256, 2, 64
EPS = 1e-6
TOK = SEQ + CTX_LEN
KD = D_MODEL // P
NT, CT = TOK // P, CTX_LEN // P
LT = NT - CT
A_HEADS, A_KV, A_DIM = 8, 2, 64
B_HEADS, B_DIM = 4, 128
C_HEADS, C_NOPE, C_ROPE, C_V = 16, 64, 32, 64
C_QK = C_NOPE + C_ROPE
QR, KVR = 384, 256
FFN = 2816
FB = FFN // P
AB_IN = 2832
NEG = -1e30
ALL_CHUNKS = ((0, 512), (512, 512), (1024, 256))
LAT_CHUNKS = ((256, 512), (768, 512))
LEVELS = 7
MATS = (["ident", "ones", "swap", "dup0", "dup1", "dupswap0", "dupswap1", "kpe_place", "kpe_swap", "q_swap",
         "cum0", "cum1", "decay_mask0", "decay_mask1"]
        + [f"level{d}_{l}" for d in range(2) for l in range(LEVELS)])
ROWS_A = (("mod_b", 96), ("c", KD), ("c_ctx", KD), ("q_norm", 3), ("kv_norm", 2), ("out_norm", 1))
ROWS_B = (("norm_gains", 64), ("conv", 36))


def give(eng, sems, n=1):
    for s in sems:
        eng.sem_inc(s, n)


class Stage:
    used_semaphores = []

    def __init__(self, nc, name):
        self.nc, self.name, self.stack = nc, name, ExitStack()

    @classmethod
    def recycle(cls, nc):
        nc.clear_and_free_semaphores(cls.used_semaphores)
        cls.used_semaphores = []
        nc.all_engine_barrier()

    def __enter__(self):
        self.stack.__enter__()
        return self

    def __exit__(self, *a):
        return self.stack.__exit__(*a)

    def sb(self, name, *shape):
        return self.stack.enter_context(self.nc.sbuf_tensor(f"{self.name}_{name}", list(shape), F32))

    def sb_r(self, name, *shape):
        return self.stack.enter_context(self.nc.sbuf_tensor(f"{self.name}_{name}", list(shape), mybir.dt.float32r))

    def ps(self, name, *shape):
        return self.stack.enter_context(self.nc.psum_tensor(f"{self.name}_{name}", list(shape), F32))

    def sem(self, name, n=None):
        sems = [self.nc.alloc_semaphore(f"{self.name}_{name}{i}") for i in range(n or 1)]
        Stage.used_semaphores += sems
        return sems if n else sems[0]


def rows_at(spec, name):
    at = 0
    for n, k in spec:
        if n == name:
            return at, at + k
        at += k
    raise KeyError(name)


def load_constants(nc, a, sb):
    with Stage(nc, "const") as st:
        rows = [st.sb("rows_a", P, P), st.sb("rows_b", P, P)]
        turned = [st.ps("turned_a", P, P), st.ps("turned_b", P, P)]
        loaded, cleared, transposed, columns = st.sem("loaded"), st.sem("cleared"), st.sem("transposed"), st.sem("columns")
        srcs = {
            "mod_b": a["mod_b"].rearrange("l (b p) -> (l b) p", p=P),
            "c": a["c"].rearrange("o (b p) -> (o b) p", p=P),
            "c_ctx": a["c_ctx"].rearrange("(b p) -> b p", p=P),
            "q_norm": a["mla_q_norm"].rearrange("o (b p) -> (o b) p", p=P),
            "kv_norm": a["mla_kv_norm"].rearrange("o (b p) -> (o b) p", p=P),
            "out_norm": a["ab_out_norm"],
            "norm_gains": a["norm_gains"].rearrange("l g (b p) -> (l g b) p", p=P),
            "conv": a["ab_conv"].rearrange("o j (b p) -> (o j b) p", p=P),
        }
        with nc.Block() as block:
            @block.vector
            def _(dve):
                for r in rows:
                    dve.memset(r[:, :], 0.0).then_inc(cleared, 1)
                dve.wait_ge(transposed, 2).then_inc(transposed, -2)
                dve.tensor_copy(sb["cols_a"][:, :], turned[0][:, :]).then_inc(columns, 1)
                dve.tensor_copy(sb["cols_b"][:, :], turned[1][:, :]).then_inc(columns, 1)

            @block.sync
            def _(sp):
                sp.dma_start(sb["ident"][:, :], a["mats"][MATS.index("ident")]).then_inc(loaded, 16)
                sp.dma_start(sb["ones"][:, :], a["mats"][MATS.index("ones")]).then_inc(loaded, 16)
                sp.wait_ge(cleared, 2)
                for spec, r in ((ROWS_A, rows[0]), (ROWS_B, rows[1])):
                    for name, _k in spec:
                        lo, hi = rows_at(spec, name)
                        sp.dma_start(r[lo:hi, :], srcs[name]).then_inc(loaded, 16)

            @block.tensor
            def _(pe):
                pe.wait_ge(loaded, 16 * (2 + len(ROWS_A) + len(ROWS_B)))
                for r, t in zip(rows, turned):
                    pe.transpose(t[:, :], r[:, :], sb["ident"][:, :]).then_inc(transposed, 1)

            @block.scalar
            def _(act):
                act.wait_ge(columns, 2)
                lo, _hi = rows_at(ROWS_A, "c")
                act.activation(sb["silu_c"][:, :, :], sb["cols_a"][:, lo:lo + 2 * KD].rearrange("p (c k) -> p k c", c=2),
                               ACT.Silu)


def adaln(nc, a, sb):
    NG, NS, W = 12, 4, 512
    with Stage(nc, "adaln") as st:
        w = [st.sb(f"w{s}", P, KD, W) for s in range(NS)]
        out = [st.ps(f"out{s}", 2, W) for s in range(NS)]
        rows = st.sb("rows", 2, DEPTH, 6 * D_MODEL)
        cols = st.ps("cols", P, DEPTH, 48, 2)
        mod = st.sb("mod", P, DEPTH, 2, 48)
        w_in, out_full, out_free = st.sem("w_in", NS), st.sem("out_full", NS), st.sem("out_free", NS)
        rows_full, rows_done, cols_full, mod_done, coef_step = (st.sem(n) for n in ("rows_full", "rows_done", "cols_full", "mod_done", "coef_step"))
        b_lo, _ = rows_at(ROWS_A, "mod_b")
        g_lo, _ = rows_at(ROWS_B, "norm_gains")
        with nc.Block() as block:
            @block.sync
            def _(sp):
                for layer in range(DEPTH):
                    w_v = a["mod_w"][layer].rearrange("(k p) n -> p k n", p=P)
                    with sp.Fori(0, NG // NS) as i:
                        for s in range(NS):
                            sp.wait_ge(out_free[s], 1).then_inc(out_free[s], -1)
                            sp.dma_start(w[s][:, :, :], w_v[:, :, bass.ds((i * NS + s) * W, W)]).then_inc(w_in[s], 16)

            @block.tensor
            def _(pe):
                for layer in range(DEPTH):
                    with pe.Fori(0, NG // NS) as i:
                        for s in range(NS):
                            pe.wait_ge(w_in[s], 16).then_inc(w_in[s], -16)
                            for k in range(KD):
                                mm = pe.matmul(out[s][:, :], sb["silu_c"][:, k, :], w[s][:, k, :], start=(k == 0), stop=(k == KD - 1))
                            mm.then_inc(out_full[s], 1)
                pe.wait_ge(rows_full, 1).then_inc(rows_full, -1)
                for layer in range(DEPTH):
                    for b in range(48):
                        mm = pe.transpose(cols[:, layer, b, :], rows[:, layer, b * P:(b + 1) * P], sb["ident"][0:2, 0:2])
                mm.then_inc(cols_full, 1)

            @block.vector
            def _(dve):
                give(dve, out_free)
                for layer in range(DEPTH):
                    with dve.Fori(0, NG // NS) as i:
                        for s in range(NS):
                            dve.wait_ge(out_full[s], 1).then_inc(out_full[s], -1)
                            dve.tensor_copy(rows[:, layer, bass.ds((i * NS + s) * W, W)], out[s][:, :]).then_inc(rows_done, 1)
                            dve.wait_ge(rows_done, 1).then_inc(rows_done, -1)
                            dve.sem_inc(out_free[s], 1)
                dve.sem_inc(rows_full, 1)
                dve.wait_ge(cols_full, 1).then_inc(cols_full, -1)
                for layer in range(DEPTH):
                    for cond in range(2):
                        dve.tensor_tensor(mod[:, layer, cond, :], cols[:, layer, :, cond],
                                          sb["cols_a"][:, b_lo + layer * 48:b_lo + (layer + 1) * 48], ALU.add).then_inc(mod_done, 1)
                dve.wait_ge(mod_done, 4).then_inc(mod_done, -4)
                for layer in range(DEPTH):
                    for half in range(2):
                        for cond in range(2):
                            m = [mod[:, layer, cond, (3 * half + j) * KD:(3 * half + j + 1) * KD] for j in range(3)]
                            g = [sb["cols_b"][:, g_lo + (layer * 4 + 2 * half + j) * KD:g_lo + (layer * 4 + 2 * half + j + 1) * KD]
                                 for j in range(2)]
                            c = sb["coef"]
                            dve.tensor_copy(c[:, layer, half, cond, 0, :], m[0])
                            dve.scalar_tensor_tensor(out=c[:, layer, half, cond, 1, :], in0=m[1], scalar=1.0, in1=g[0],
                                                     op0=ALU.add, op1=ALU.mult)
                            dve.tensor_tensor(c[:, layer, half, cond, 2, :], m[2], g[1], ALU.mult)


def norms(nc, a, sb, name, segs, layer_y=None, y=None, layer_u=None, u=None):
    with Stage(nc, name) as st:
        h_old = [st.sb(f"h_old{s}", P, D_MODEL) for s in range(2)]
        sq = st.sb("sq", P, D_MODEL)
        stat = st.sb("stat", P, 2, 2, 4)
        eps = st.sb("eps", P, 1)
        h_in, h_free, h_out = st.sem("h_in", 2), st.sem("h_free", 2), st.sem("h_out", 2)
        h_full, root_y, root_h = st.sem("h_full"), st.sem("root_y"), st.sem("root_h")
        act_step, step, eps_set = st.sem("act_step"), st.sem("step"), st.sem("eps_set")
        h = h_old
        if y is not None:
            h = [st.sb(f"h{s}", P, D_MODEL) for s in range(2)]
            y_slot = [st.sb(f"y{s}", P, KD, P) for s in range(2)]
            y_tok = [st.ps(f"ytok{s}", P, D_MODEL) for s in range(2)]
            gate = st.sb("gate", P, 2, D_MODEL)
            residual = [st.sb(f"residual{s}", P, D_MODEL) for s in range(2)]
            residual_full, residual_free, pool_step = st.sem("residual_full", 2), st.sem("residual_free", 2), st.sem("pool_step")
            y_in, y_free, y_full, y_read = st.sem("y_in", 2), st.sem("y_free", 2), st.sem("y_full", 2), st.sem("y_read", 2)
            gate_full, gate_read = st.sem("gate_full"), st.sem("gate_read")
        if u is not None:
            hn = [st.sb(f"hn{s}", P, D_MODEL) for s in range(2)]
            u_ps = [st.ps(f"ups{s}", P, D_MODEL) for s in range(2)]
            hn_full, hn_free, u_free = st.sem("hn_full", 2), st.sem("hn_free", 2), st.sem("u_free", 2)
            u_full, u_full_act = st.sem("u_full", 2), st.sem("u_full_act", 2)
        conds = [s[0] for s in segs]
        HALF = KD // 2
        n_tiles = sum(s[2] for s in segs)
        before_last = n_tiles - segs[-1][2]

        def tile_at(p):
            if not isinstance(p, int) or p >= before_last:
                return segs[-1], p - before_last
            for seg in segs:
                if p < seg[2]:
                    return seg, p
                p -= seg[2]

        def over_tiles(eng, add, normalise, modulate):
            def one(p, s):
                if not isinstance(p, int) or p + 1 < n_tiles:
                    add(1 - s, *tile_at(p + 1))
                normalise(s, *tile_at(p))
                if not isinstance(p, int) or p > 0:
                    modulate(1 - s, *tile_at(p - 1))
            add(0, *tile_at(0))
            lead = before_last + 1
            for p in range(lead):
                one(p, p % 2)
            with eng.Fori(0, (n_tiles - 1 - lead) // 2) as i:
                for j in range(2):
                    one(2 * i + (lead + j), (lead + j) % 2)
            one(n_tiles - 1, (n_tiles - 1) % 2)
            modulate((n_tiles - 1) % 2, *tile_at(n_tiles - 1))

        def modulated(eng, emit, s, seg, i, blocks, sem):
            cond, t0 = seg[:2]
            c = sb["coef"]
            for k in blocks:
                emit(u[:, k, bass.ds((i + t0) * P, P)], u_ps[s][:, k * P:(k + 1) * P],
                     c[:, layer_u[0], layer_u[1], cond, 1, k:k + 1], c[:, layer_u[0], layer_u[1], cond, 0, k:k + 1]).then_inc(sem, 1)

        with nc.Block() as block:
            @block.sync
            def _(sp):
                for cond, t0, n, src, dst in segs:
                    with sp.Fori(0, n // 2) as i:
                        for s in range(2):
                            if y is not None:
                                sp.wait_ge(y_free[s], 1).then_inc(y_free[s], -1)
                                sp.dma_start(y_slot[s][:, :, :], y[:, :, bass.ds((2 * i + s + t0) * P, P)]).then_inc(y_in[s], 16)
                            sp.wait_ge(h_free[s], 1).then_inc(h_free[s], -1)
                            sp.dma_start(h_old[s][:, :], src[bass.ds((2 * i + s) * P, P), :]).then_inc(h_in[s], 16)

            @block.tensor
            def _(pe):
                if y is not None:
                    for cond in conds:
                        pe.wait_ge(gate_read, 1).then_inc(gate_read, -1)
                        for k in range(KD):
                            col = sb["coef"][:, layer_y[0], layer_y[1], cond, 2, k:k + 1]
                            mm = pe.matmul(y_tok[0][:, k * P:(k + 1) * P], col.to_broadcast([P, P]), sb["ident"][:, :],
                                           start=True, stop=True)
                        mm.then_inc(gate_full, 1)
                    pe.wait_ge(gate_read, 1).then_inc(gate_read, -1)

                def add(s, seg, i):
                    if y is not None:
                        pe.wait_ge(y_in[s], 16).then_inc(y_in[s], -16)
                        pe.wait_ge(y_read[s], 1).then_inc(y_read[s], -1)
                        for k in range(KD):
                            mm = pe.transpose(y_tok[s][:, k * P:(k + 1) * P], y_slot[s][:, k, :], sb["ident"][:, :])
                        mm.then_inc(y_full[s], 1)

                def modulate(s, seg, i):
                    if u is not None:
                        pe.wait_ge(hn_full[s], 1).then_inc(hn_full[s], -1)
                        pe.wait_ge(u_free[s], 2).then_inc(u_free[s], -2)
                        for k in range(KD):
                            mm = pe.transpose(u_ps[s][:, k * P:(k + 1) * P], hn[s][:, k * P:(k + 1) * P], sb["ident"][:, :])
                        mm.then_inc(u_full[s], 1)
                        pe.drain().then_inc(u_full_act[s], 1)
                over_tiles(pe, add, lambda s, seg, i: None, modulate)

            @block.scalar
            def _(act):
                act.wait_ge(eps_set, 1)

                def root_mean_square(src, to, root):
                    act.activation(sq[:, :], src, ACT.Square, accum_out=to[:, 0:1]).then_inc(act_step, 1)
                    act.wait_ge(act_step, 1).then_inc(act_step, -1)
                    act.activation(to[:, 1:2], to[:, 0:1], ACT.Sqrt, scale=1.0 / D_MODEL, bias=eps[:, :]).then_inc(root, 1)

                def add(s, seg, i):
                    if y is not None:
                        act.wait_ge(y_full[s], 1).then_inc(y_full[s], -1)
                        act.sem_inc(y_free[s], 1)
                        root_mean_square(y_tok[s][:, :], stat[:, s, 0, :], root_y)

                def normalise(s, seg, i):
                    if y is None:
                        act.wait_ge(h_in[s], 16).then_inc(h_in[s], -16)
                    else:
                        act.wait_ge(h_full, 1).then_inc(h_full, -1)
                    if seg[4] is not None:
                        act.dma_start(seg[4][bass.ds(i * P, P), :], h[s][:, :]).then_inc(h_out[s], 16)
                    elif y is not None:
                        act.sem_inc(h_out[s], 16)
                    if u is not None:
                        root_mean_square(h[s][:, :], stat[:, s, 1, :], root_h)

                def modulate(s, seg, i):
                    if u is not None:
                        act.wait_ge(u_full_act[s], 1).then_inc(u_full_act[s], -1)
                        modulated(act, lambda out, in_, scale, shift: act.activation(out, in_, ACT.Identity, scale=scale, bias=shift),
                                  s, seg, i, range(HALF), act_step)
                        act.wait_ge(act_step, HALF).then_inc(act_step, -HALF)
                        act.sem_inc(u_free[s], 1)
                over_tiles(act, add, normalise, modulate)

            @block.vector
            def _(dve):
                def done(ins, *to):
                    ins.then_inc(step, 1)
                    dve.wait_ge(step, 1).then_inc(step, -1)
                    for x_ in to:
                        dve.sem_inc(x_, 1)

                dve.memset(eps[:, :], EPS).then_inc(eps_set, 1)
                give(dve, h_free)
                if y is not None:
                    give(dve, y_free)
                    give(dve, y_read)
                    give(dve, residual_free)
                    give(dve, [gate_read])
                    for cond in conds:
                        dve.wait_ge(gate_full, 1).then_inc(gate_full, -1)
                        done(dve.tensor_copy(gate[:, cond, :], y_tok[0][:, :]), gate_read)
                if u is not None:
                    give(dve, hn_free)
                    give(dve, u_free, 2)

                def add(s, seg, i):
                    if y is not None:
                        r = stat[:, s, 0, 2:3]
                        dve.wait_ge(root_y, 1).then_inc(root_y, -1)
                        done(dve.reciprocal(r, stat[:, s, 0, 1:2]))
                        dve.wait_ge(residual_free[s], 1).then_inc(residual_free[s], -1)
                        done(dve.scalar_tensor_tensor(out=residual[s][:, :], in0=y_tok[s][:, :], scalar=r, in1=gate[:, seg[0], :],
                                                      op0=ALU.mult, op1=ALU.mult), y_read[s], residual_full[s])

                def normalise(s, seg, i):
                    if u is not None:
                        r = stat[:, s, 1, 2:3]
                        dve.wait_ge(root_h, 1).then_inc(root_h, -1)
                        done(dve.reciprocal(r, stat[:, s, 1, 1:2]))
                        dve.wait_ge(hn_free[s], 1).then_inc(hn_free[s], -1)
                        ins = dve.tensor_scalar(hn[s][:, :], h[s][:, :], r, None, ALU.mult)
                        if y is None:
                            done(ins, hn_full[s], h_free[s])
                        else:
                            done(ins, hn_full[s])

                def modulate(s, seg, i):
                    if u is not None:
                        dve.wait_ge(u_full[s], 1).then_inc(u_full[s], -1)
                        dve.sem_inc(hn_free[s], 1)
                        modulated(dve, lambda out, in_, scale, shift: dve.tensor_scalar(out, in_, scale, shift, ALU.mult, ALU.add),
                                  s, seg, i, range(HALF, KD), step)
                        dve.wait_ge(step, HALF).then_inc(step, -HALF)
                        dve.sem_inc(u_free[s], 1)
                over_tiles(dve, add, normalise, modulate)

            @block.gpsimd
            def _(pool):
                if y is None:
                    return
                give(pool, h_out, 16)

                def add(s, seg, i):
                    pool.wait_ge(residual_full[s], 1).then_inc(residual_full[s], -1)
                    pool.wait_ge(h_in[s], 16).then_inc(h_in[s], -16)
                    pool.wait_ge(h_out[s], 16).then_inc(h_out[s], -16)
                    pool.tensor_tensor(h[s][:, :], h_old[s][:, :], residual[s][:, :], ALU.add).then_inc(pool_step, 1)
                    pool.wait_ge(pool_step, 1).then_inc(pool_step, -1)
                    for x_ in (h_full, h_free[s], residual_free[s]):
                        pool.sem_inc(x_, 1)
                over_tiles(pool, add, lambda s, seg, i: None, lambda s, seg, i: None)
                for s in range(2):
                    pool.wait_ge(h_out[s], 16).then_inc(h_out[s], -16)


def project(nc, name, segs, x, k_tiles, chunks):
    nch = len(chunks)
    with Stage(nc, name) as st:
        w_slot = [st.sb(f"w{s}", P, k_tiles, P) for s in range(2)]
        acc = [[st.ps(f"acc{s}{j}", P, 512) for j in range(nch)] for s in range(2)]
        w_in, w_free = st.sem("w_in", 2), st.sem("w_free", 2)
        acc_full = [st.sem(f"acc_full{s}", nch) for s in range(2)]
        acc_free = [st.sem(f"acc_free{s}", nch) for s in range(2)]
        copied = st.sem("copied")

        def over_blocks(eng, nblk, body):
            if nblk > 1:
                with eng.Fori(0, nblk // 2) as i:
                    for s in range(2):
                        body(s, 2 * i + s)
            if nblk % 2:
                body(0, nblk - 1)

        with nc.Block() as block:
            @block.sync
            def _(sp):
                for w, col0, m, nblk, dst, blk0 in segs:
                    w_v = w.rearrange("(k p) n -> p k n", p=P)

                    def load(s, b):
                        sp.wait_ge(w_free[s], 1).then_inc(w_free[s], -1)
                        sp.dma_start(w_slot[s][:, :, 0:m], w_v[:, :, bass.ds(b * m + col0, m)]).then_inc(w_in[s], 16)
                    over_blocks(sp, nblk, load)

            @block.tensor
            def _(pe):
                for w, col0, m, nblk, dst, blk0 in segs:
                    def products(s, b):
                        pe.wait_ge(w_in[s], 16).then_inc(w_in[s], -16)
                        for j, (t0, n) in enumerate(chunks):
                            pe.wait_ge(acc_free[s][j], 1).then_inc(acc_free[s][j], -1)
                            for k in range(k_tiles):
                                mm = pe.matmul(acc[s][j][0:m, 0:n], w_slot[s][:, k, 0:m], x[:, k, t0:t0 + n],
                                               start=(k == 0), stop=(k == k_tiles - 1))
                            mm.then_inc(acc_full[s][j], 1)
                    over_blocks(pe, nblk, products)

            @block.vector
            def _(dve):
                give(dve, w_free)
                for s in range(2):
                    give(dve, acc_free[s])
                for w, col0, m, nblk, dst, blk0 in segs:
                    def copy_out(s, b):
                        for j, (t0, n) in enumerate(chunks):
                            dve.wait_ge(acc_full[s][j], 1).then_inc(acc_full[s][j], -1)
                            if j == nch - 1:
                                dve.sem_inc(w_free[s], 1)
                            dve.tensor_copy(dst[0:m, bass.ds(b + blk0, 1), t0:t0 + n], acc[s][j][0:m, 0:n].rearrange("p (o n) -> p o n", o=1)).then_inc(copied, 1)
                            dve.wait_ge(copied, 1).then_inc(copied, -1)
                            dve.sem_inc(acc_free[s][j], 1)
                    over_blocks(dve, nblk, copy_out)


def project_split(nc, name, w, col0, nblk, dst, x, k_tiles, chunks, tail=None):
    nch = len(chunks)
    lo_tok, n_tok = chunks[0][0], TOK - chunks[0][0]
    PAIRS = ((0, 0), (1, 0), (0, 1))
    total = nblk + (tail is not None)
    with Stage(nc, name) as st:
        raw = [st.sb(f"raw{s}", P, k_tiles, P) for s in range(2)]
        part = [[st.sb_r(f"w{s}{h}", P, k_tiles, P) for h in range(2)] for s in range(2)]
        x_part = [st.sb_r(f"x{h}", P, k_tiles, n_tok) for h in range(2)]
        acc = [[st.ps(f"acc{s}{j}", P, 512) for j in range(nch)] for s in range(2)]
        raw_in, raw_free, part_free, part_ready = st.sem("raw_in", 2), st.sem("raw_free", 2), st.sem("part_free", 2), st.sem("part_ready", 2)
        weight_hi, x_hi, x_ready, step = st.sem("weight_hi"), st.sem("x_hi"), st.sem("x_ready"), st.sem("step")
        acc_full = [st.sem(f"acc_full{s}", nch) for s in range(2)]
        acc_free = [st.sem(f"acc_free{s}", nch) for s in range(2)]

        def block_at(b):
            if isinstance(b, int) and b == nblk:
                return tail[0], tail[1], tail[2][0:tail[1], 0:1, :]
            return b * P + col0, P, dst[:, bass.ds(b, 1), :]

        def over_blocks(eng, body):
            pairs = (nblk - 2) // 2
            with eng.Fori(0, pairs) as i:
                for s in range(2):
                    body(s, 2 * i + s, True)
            for b in range(2 * pairs, total):
                body(b % 2, b, b + 2 < total)

        with nc.Block() as block:
            @block.sync
            def _(sp):
                w_v = w.rearrange("(k p) n -> p k n", p=P)

                def load(s, b, _more):
                    col, m, _dst = block_at(b)
                    sp.wait_ge(raw_free[s], 1).then_inc(raw_free[s], -1)
                    sp.dma_start(raw[s][:, :, 0:m], w_v[:, :, bass.ds(col, m)]).then_inc(raw_in[s], 16)
                over_blocks(sp, load)

            @block.tensor
            def _(pe):
                def products(s, b, _more):
                    m = block_at(b)[1]
                    pe.wait_ge(part_ready[s], 1).then_inc(part_ready[s], -1)
                    for j, (t0, n) in enumerate(chunks):
                        pe.wait_ge(acc_free[s][j], 1).then_inc(acc_free[s][j], -1)
                        for k in range(k_tiles):
                            for w_, x_ in PAIRS:
                                mm = pe.matmul(acc[s][j][0:m, 0:n], part[s][w_][:, k, 0:m], x_part[x_][:, k, t0 - lo_tok:t0 - lo_tok + n],
                                               start=(k == 0 and w_ + x_ == 0), stop=(k == k_tiles - 1 and x_ == 1))
                        mm.then_inc(acc_full[s][j], 1)
                over_blocks(pe, products)

            @block.scalar
            def _(act):
                def high_part(s, b, _more):
                    m = block_at(b)[1]
                    act.wait_ge(part_free[s], 1).then_inc(part_free[s], -1)
                    act.wait_ge(raw_in[s], 16).then_inc(raw_in[s], -16)
                    act.activation(part[s][0][:, :, 0:m], raw[s][:, :, 0:m], ACT.Copy).then_inc(weight_hi, 1)

                give(act, part_free)
                for t0, n in chunks:
                    for k in range(k_tiles):
                        act.activation(x_part[0][:, k, t0 - lo_tok:t0 - lo_tok + n], x[:, k, t0:t0 + n], ACT.Copy).then_inc(x_hi, 1)
                over_blocks(act, high_part)

            @block.vector
            def _(dve):
                def low_part(s, m):
                    dve.wait_ge(weight_hi, 1).then_inc(weight_hi, -1)
                    dve.tensor_tensor(part[s][1][:, :, 0:m], raw[s][:, :, 0:m], part[s][0][:, :, 0:m].bitcast(F32), ALU.subtract).then_inc(step, 1)
                    dve.wait_ge(step, 1).then_inc(step, -1)
                    dve.sem_inc(part_ready[s], 1)
                    dve.sem_inc(raw_free[s], 1)

                def copy_out(s, b, more):
                    _col, m, to = block_at(b)
                    for j, (t0, n) in enumerate(chunks):
                        dve.wait_ge(acc_full[s][j], 1).then_inc(acc_full[s][j], -1)
                        if j == nch - 1:
                            dve.sem_inc(part_free[s], 1)
                        dve.tensor_copy(to[:, :, t0:t0 + n], acc[s][j][0:m, 0:n].rearrange("p (o n) -> p o n", o=1)).then_inc(acc_free[s][j], 1)
                    if more:
                        low_part(s, block_at(b + 2)[1])

                give(dve, raw_free)
                for s in range(2):
                    give(dve, acc_free[s])
                for t0, n in chunks:
                    for k in range(k_tiles):
                        dve.wait_ge(x_hi, 1).then_inc(x_hi, -1)
                        dve.tensor_tensor(x_part[1][:, k, t0 - lo_tok:t0 - lo_tok + n], x[:, k, t0:t0 + n],
                                          x_part[0][:, k, t0 - lo_tok:t0 - lo_tok + n].bitcast(F32), ALU.subtract).then_inc(x_ready, 1)
                dve.wait_ge(x_ready, k_tiles * nch).then_inc(x_ready, -k_tiles * nch)
                low_part(0, P)
                low_part(1, P)
                over_blocks(dve, copy_out)


def ffn(nc, name, w_gate, w_up, w_down, u, chunks):
    F32R = mybir.dt.float32r
    nch = len(chunks)
    lo_tok, n_tok = chunks[0][0], TOK - chunks[0][0]
    PAIRS = ((0, 0), (1, 0), (0, 1))
    NO = 4
    with Stage(nc, name) as st:
        raw = [st.sb(f"raw_{n}", P, D_MODEL) for n in ("gate", "up", "down")]
        u_part = [st.sb_r(f"u_part{x}", P, KD, n_tok) for x in range(2)]
        gu_part = [[[st.sb_r(f"gu{s}{g}{x}", P, KD * P) for x in range(2)] for g in range(2)] for s in range(2)]
        down_part = [st.sb_r(f"down{x}", P, D_MODEL) for x in range(2)]
        silu, hid = st.sb("silu", P, 512), [st.sb(f"hid{r}", P, 512) for r in range(2)]
        hid_part = [[st.sb_r(f"hid_part{r}{x}", P, 512) for x in range(2)] for r in range(2)]
        acc = [[st.ps(f"acc{r}{g}", P, 512) for g in range(2)] for r in range(2)]
        out = [st.ps(f"out{r}", P, 512) for r in range(NO)]
        raw_in, raw_free = st.sem("raw_in", 3), st.sem("raw_free", 3)
        weight_hi, gu_ready = st.sem("weight_hi"), st.sem("gu_ready", 2)
        down_ready, down_free = st.sem("down_ready"), st.sem("down_free")
        u_hi, u_split, u_rest, u_clear = st.sem("u_hi"), st.sem("u_split"), st.sem("u_rest"), st.sem("u_clear")
        gate_full, up_full, pair_free = st.sem("gate_full", 2), st.sem("up_full", 2), st.sem("pair_free", 2)
        silu_full, hid_full, hid_hi = st.sem("silu_full"), st.sem("hid_full"), st.sem("hid_hi")
        hid_ready = st.sem("hid_ready", 2)
        out_full, out_free, step = st.sem("out_full", NO), st.sem("out_free", NO), st.sem("step")

        def over_blocks(eng, split, start, unit, prepare_down, prepare_gu):
            split(chunks[:1])
            prepare_gu(0)
            split(chunks[1:])
            prepare_down()
            prepare_gu(1)
            start()

            def pair_of_blocks(last):
                units = [(s, j, (s * nch + j) % 2) for s in range(2) for j in range(nch)]
                for n, (s, j, r) in enumerate(units):
                    end = last and n == len(units) - 1
                    unit((s, j, r), None if end else units[(n + 1) % len(units)])
                    if j == nch - 1 and not (last and s == 1):
                        prepare_down()
                    if j == nch - 1 and not last:
                        prepare_gu(s)
            with eng.Fori(0, FB // 2 - 1) as i:
                pair_of_blocks(False)
            pair_of_blocks(True)

        with nc.Block() as block:
            @block.sync
            def _(sp):
                gu_v = [w.rearrange("(k p) n -> p k n", p=P) for w in (w_gate, w_up)]
                down_v = w_down.rearrange("(f p) n -> p f n", p=P)

                def load_gu(f):
                    for g in range(2):
                        sp.wait_ge(raw_free[g], 1).then_inc(raw_free[g], -1)
                        sp.dma_start(raw[g][:, :].rearrange("p (k n) -> p k n", k=KD), gu_v[g][:, :, bass.ds(f * P, P)]).then_inc(raw_in[g], 16)

                def load_down(f):
                    sp.wait_ge(raw_free[2], 1).then_inc(raw_free[2], -1)
                    sp.dma_start(raw[2][:, :].rearrange("p (o n) -> p o n", o=1), down_v[:, bass.ds(f, 1), :]).then_inc(raw_in[2], 16)
                load_gu(0)
                load_down(0)
                load_gu(1)
                with sp.Fori(0, FB - 2) as f:
                    load_down(f + 1)
                    load_gu(f + 2)
                load_down(FB - 1)

            @block.tensor
            def _(pe):
                def gate_up(s, j, r):
                    t0, n = chunks[j]
                    if j == 0:
                        pe.wait_ge(gu_ready[s], 2).then_inc(gu_ready[s], -2)
                    pe.wait_ge(pair_free[r], 1).then_inc(pair_free[r], -1)
                    for g, full in ((0, gate_full), (1, up_full)):
                        for k in range(KD):
                            for w_, x_ in PAIRS:
                                mm = pe.matmul(acc[r][g][:, 0:n], gu_part[s][g][w_][:, k * P:(k + 1) * P], u_part[x_][:, k, t0 - lo_tok:t0 - lo_tok + n],
                                               start=(k == 0 and w_ + x_ == 0), stop=(k == KD - 1 and x_ == 1))
                        mm.then_inc(full[r], 1)

                def down(s, j, r):
                    t0, n = chunks[j]
                    if j == 0:
                        pe.wait_ge(down_ready, 1).then_inc(down_ready, -1)
                    pe.wait_ge(hid_ready[r], 1).then_inc(hid_ready[r], -1)
                    for b in range(KD):
                        o = b % NO
                        pe.wait_ge(out_free[o], 1).then_inc(out_free[o], -1)
                        for w_, x_ in PAIRS:
                            mm = pe.matmul(out[o][:, 0:n], down_part[w_][:, b * P:(b + 1) * P], hid_part[r][x_][:, 0:n],
                                           start=(w_ + x_ == 0), stop=(x_ == 1))
                        mm.then_inc(out_full[o], 1)

                def unit(this, nxt):
                    if nxt is not None:
                        gate_up(*nxt)
                    down(*this)

                def start():
                    gate_up(0, 0, 0)
                    pe.wait_ge(u_rest, 1).then_inc(u_rest, -1)
                over_blocks(pe, lambda chunks: None, start, unit, lambda: None, lambda s: None)

            @block.scalar
            def _(act):
                def hidden(s, j, r):
                    t0, n = chunks[j]
                    act.wait_ge(gate_full[r], 1).then_inc(gate_full[r], -1)
                    act.activation(silu[:, 0:n], acc[r][0][:, 0:n], ACT.Silu).then_inc(silu_full, 1)
                    act.wait_ge(hid_full, 1).then_inc(hid_full, -1)
                    act.activation(hid_part[r][0][:, 0:n], hid[r][:, 0:n], ACT.Copy).then_inc(hid_hi, 1)

                def prepare_gu(s):
                    for g in range(2):
                        act.wait_ge(raw_in[g], 16).then_inc(raw_in[g], -16)
                        act.activation(gu_part[s][g][0][:, :], raw[g][:, :], ACT.Copy).then_inc(weight_hi, 1)

                def prepare_down():
                    act.wait_ge(down_free, 1).then_inc(down_free, -1)
                    act.wait_ge(raw_in[2], 16).then_inc(raw_in[2], -16)
                    act.activation(down_part[0][:, :], raw[2][:, :], ACT.Copy).then_inc(weight_hi, 1)

                def unit(this, nxt):
                    if nxt is not None:
                        hidden(*nxt)

                give(act, [down_free])

                def split(chunks):
                    for t0, n in chunks:
                        for k in range(KD):
                            act.activation(u_part[0][:, k, t0 - lo_tok:t0 - lo_tok + n], u[:, k, t0:t0 + n], ACT.Copy).then_inc(u_hi, 1)
                over_blocks(act, split, lambda: hidden(0, 0, 0), unit, prepare_down, prepare_gu)

            @block.gpsimd
            def _(pool):
                pool.wait_ge(u_split, nch * KD).then_inc(u_split, -nch * KD)
                for k in range(KD):
                    pool.memset(u[:, k, lo_tok:], 0.0).then_inc(u_clear, 1)
                pool.wait_ge(u_clear, KD).then_inc(u_clear, -KD)
                give(pool, out_free)

            @block.vector
            def _(dve):
                def done(ins, *to):
                    ins.then_inc(step, 1)
                    dve.wait_ge(step, 1).then_inc(step, -1)
                    for x_ in to:
                        dve.sem_inc(x_, 1)

                def hidden(s, j, r):
                    t0, n = chunks[j]
                    dve.wait_ge(silu_full, 1).then_inc(silu_full, -1)
                    dve.wait_ge(up_full[r], 1).then_inc(up_full[r], -1)
                    done(dve.tensor_tensor(hid[r][:, 0:n], acc[r][1][:, 0:n], silu[:, 0:n], ALU.mult), hid_full, pair_free[r])

                def hidden_low(s, j, r):
                    t0, n = chunks[j]
                    dve.wait_ge(hid_hi, 1).then_inc(hid_hi, -1)
                    dve.tensor_tensor(hid_part[r][1][:, 0:n], hid[r][:, 0:n], hid_part[r][0][:, 0:n].bitcast(F32), ALU.subtract).then_inc(hid_ready[r], 1)

                def low_part(parts, g, ready):
                    dve.wait_ge(weight_hi, 1).then_inc(weight_hi, -1)
                    done(dve.tensor_tensor(parts[1][:, :], raw[g][:, :], parts[0][:, :].bitcast(F32), ALU.subtract), ready, raw_free[g])

                def prepare_gu(s):
                    for g in range(2):
                        low_part(gu_part[s][g], g, gu_ready[s])

                def prepare_down():
                    low_part(down_part, 2, down_ready)

                def unit(this, nxt):
                    if nxt is not None:
                        hidden(*nxt)
                    s, j, r = this
                    t0, n = chunks[j]
                    for b in range(KD):
                        o = b % NO
                        dve.wait_ge(out_full[o], 1).then_inc(out_full[o], -1)
                        if b == KD - 1 and j == nch - 1:
                            dve.sem_inc(down_free, 1)
                        dve.tensor_tensor(u[:, b, t0:t0 + n], u[:, b, t0:t0 + n], out[o][:, 0:n], ALU.add).then_inc(out_free[o], 1)
                        if b == 1 and nxt is not None:
                            hidden_low(*nxt)

                for g in (raw_free, pair_free):
                    give(dve, g)

                def split(chunks):
                    for t0, n in chunks:
                        c = slice(t0 - lo_tok, t0 - lo_tok + n)
                        for k in range(KD):
                            dve.wait_ge(u_hi, 1).then_inc(u_hi, -1)
                            ins = dve.tensor_tensor(u_part[1][:, k, c], u[:, k, t0:t0 + n], u_part[0][:, k, c].bitcast(F32), ALU.subtract)
                            if k < KD - 1:
                                ins.then_inc(u_split, 1)
                            else:
                                done(ins, u_split)
                    if t0 + n == TOK:
                        dve.sem_inc(u_rest, 1)
                over_blocks(dve, split, lambda: (hidden(0, 0, 0), hidden_low(0, 0, 0)), unit, prepare_down, prepare_gu)


def decay_columns(nc, a, sb, u, cols):
    w_col = AB_IN - 4 * B_HEADS
    nh = 2 * B_HEADS
    with Stage(nc, "decay") as st:
        w = st.sb("w", P, KD, 2 * nh)
        alog, dtb = st.sb("alog", P, nh), st.sb("dtb", P, nh)
        cum = [st.sb(f"cum{d}", P, P) for d in range(2)]
        x, e, sp_, total = (st.sb(n, P, NT, nh) for n in ("x", "e", "sp", "total"))
        raw = st.ps("raw", P, NT, 2 * nh)
        sums = st.ps("sums", P, 2, NT, nh)
        loaded, raw_full, step, act_step = st.sem("loaded"), st.sem("raw_full"), st.sem("step"), st.sem("act_step")
        go_act, go_dve, ld_full, sums_full = st.sem("go_act"), st.sem("go_dve"), st.sem("ld_full"), st.sem("sums_full")

        def kind(k, d):
            return cols[:, :, d, k, :]

        def heads(t, d):
            return t[:, :, d * B_HEADS:(d + 1) * B_HEADS]

        with nc.Block() as block:
            @block.sync
            def _(sp):
                sp.dma_start(w[:, :, :], a["ab_w_in"][0].rearrange("(k p) n -> p k n", p=P)[:, :, w_col:AB_IN]).then_inc(loaded, 16)
                sp.dma_start(alog[:, :], a["ab_a_log"].rearrange("o d h -> o (d h)").to_broadcast([P, nh])).then_inc(loaded, 16)
                sp.dma_start(dtb[:, :], a["ab_dt_bias"].rearrange("o d h -> o (d h)").to_broadcast([P, nh])).then_inc(loaded, 16)
                for d in range(2):
                    sp.dma_start(cum[d][:, :], a["mats"][MATS.index(f"cum{d}")]).then_inc(loaded, 16)

            @block.tensor
            def _(pe):
                pe.wait_ge(loaded, 80)
                for t in range(NT):
                    for k in range(KD):
                        mm = pe.matmul(raw[:, t, :], u[:, k, t * P:(t + 1) * P], w[:, k, :], start=(k == 0), stop=(k == KD - 1))
                mm.then_inc(raw_full, 1)
                pe.wait_ge(ld_full, 1).then_inc(ld_full, -1)
                for d in range(2):
                    ld = sp_[:, :, d * B_HEADS:(d + 1) * B_HEADS]
                    pe.matmul(sums[:, 0, :, d * B_HEADS:(d + 1) * B_HEADS], cum[d][:, :], ld, start=True, stop=True)
                    mm = pe.matmul(sums[:, 1, :, d * B_HEADS:(d + 1) * B_HEADS], sb["ones"][:, :], ld, start=True, stop=True)
                mm.then_inc(sums_full, 1)

            @block.vector
            def _(dve):
                def done(ins, n=1):
                    ins.then_inc(step, 1)
                    dve.wait_ge(step, 1).then_inc(step, -1)

                dve.wait_ge(loaded, 80)
                dve.wait_ge(raw_full, 1).then_inc(raw_full, -1)
                done(dve.tensor_tensor(x[:, :, :], raw[:, :, 0:nh], dtb[:, :].rearrange("p (o n) -> p o n", o=1).to_broadcast([P, NT, nh]), ALU.add))
                done(dve.tensor_copy(total[:, :, :], raw[:, :, nh:2 * nh]))
                dve.sem_inc(go_act, 1)
                dve.wait_ge(go_dve, 1).then_inc(go_dve, -1)
                done(dve.tensor_scalar(e[:, :, :], e[:, :, :], 1.0, None, ALU.add))
                done(dve.reciprocal(e[:, :, :], e[:, :, :]))
                for d in range(2):
                    dve.tensor_copy(kind(2, d), heads(e, d))
                done(dve.tensor_scalar(x[:, :, :], x[:, :, :], 0.0, None, ALU.max))
                done(dve.tensor_tensor(x[:, :, :], x[:, :, :], sp_[:, :, :], ALU.add))
                done(dve.scalar_tensor_tensor(out=sp_[:, :, :], in0=x[:, :, :], scalar=-1.0,
                                              in1=alog[:, :].rearrange("p (o n) -> p o n", o=1).to_broadcast([P, NT, nh]), op0=ALU.mult, op1=ALU.mult))
                dve.sem_inc(ld_full, 1)
                for d in range(2):
                    dve.tensor_copy(kind(0, d), heads(sp_, d))
                dve.wait_ge(sums_full, 1).then_inc(sums_full, -1)
                done(dve.tensor_copy(x[:, :, :], sums[:, 0, :, :]))
                done(dve.tensor_copy(total[:, :, :], sums[:, 1, :, :]))
                for d in range(2):
                    dve.tensor_copy(kind(1, d), heads(x, d))
                done(dve.tensor_tensor(sp_[:, :, :], total[:, :, :], x[:, :, :], ALU.subtract))
                dve.sem_inc(go_act, 1)
                dve.wait_ge(go_dve, 1).then_inc(go_dve, -1)
                done(dve.tensor_tensor(sp_[:, :, :], sp_[:, :, :], e[:, :, :], ALU.mult))
                for d in range(2):
                    dve.tensor_scalar(kind(3, d), heads(x, d), -1.0, None, ALU.mult)
                    dve.tensor_copy(kind(4, d), heads(sp_, d))
                    dve.tensor_copy(kind(5, d), heads(total, d))

            @block.scalar
            def _(act):
                def done(ins):
                    ins.then_inc(act_step, 1)
                    act.wait_ge(act_step, 1).then_inc(act_step, -1)

                act.wait_ge(go_act, 1).then_inc(go_act, -1)
                done(act.activation(e[:, :, :], total[:, :, :], ACT.Exp, scale=-1.0))
                done(act.activation(alog[:, :], alog[:, :], ACT.Exp))
                done(act.activation(sp_[:, :, :], x[:, :, :], ACT.Abs))
                done(act.activation(sp_[:, :, :], sp_[:, :, :], ACT.Exp, scale=-1.0))
                done(act.activation(sp_[:, :, :], sp_[:, :, :], ACT.Ln, bias=1.0))
                act.sem_inc(go_dve, 1)
                act.wait_ge(go_act, 1).then_inc(go_act, -1)
                done(act.activation(x[:, :, :], x[:, :, :], ACT.Exp))
                done(act.activation(sp_[:, :, :], sp_[:, :, :], ACT.Exp))
                done(act.activation(total[:, :, :], total[:, :, :], ACT.Exp))
                act.sem_inc(go_dve, 1)


def conv_qkv(nc, a, sb, pb, qkv_dram):
    c_lo, _ = rows_at(ROWS_B, "conv")
    GROUP = 4
    with Stage(nc, "conv") as st:
        y = [st.sb(f"y{s}", P, TOK) for s in range(2)]
        z = [st.sb(f"z{s}", P, TOK) for s in range(GROUP)]
        sq, eps, scales = st.sb("sq", P, TOK), st.sb("eps", P, 1), st.sb("scales", P, 2)
        sums = [st.ps(f"sums{s}", P, NT) for s in range(2)]
        root = [st.sb(f"root{s}", P, NT) for s in range(2)]
        norm = [st.ps(f"norm{s}", P, 3 * 512) for s in range(2)]
        constants, step, act_step = st.sem("constants"), st.sem("step"), st.sem("act_step")
        y_full, y_free, sums_full, root_full, inverse_full, norm_full = (st.sem(n, 2) for n in
            ("y_full", "y_free", "sums_full", "root_full", "inverse_full", "norm_full"))
        sq_full, sq_free = st.sem("sq_full"), st.sem("sq_free")
        out_ready, stored = st.sem("out_ready", GROUP), st.sem("stored", GROUP)

        def over_groups(eng, normalised, plain):
            with eng.Fori(0, 2) as g:
                normalised(g)
            plain(2)

        with nc.Block() as block:
            @block.vector
            def _(dve):
                dve.memset(scales[:, 0:1], float(B_DIM) ** -0.5).then_inc(step, 1)
                dve.memset(scales[:, 1:2], 1.0).then_inc(step, 1)
                dve.wait_ge(step, 2).then_inc(step, -2)
                dve.memset(eps[:, :], EPS).then_inc(constants, 1)
                give(dve, stored, 16)
                give(dve, y_free)
                give(dve, [sq_free])

                def convolved(g, j):
                    b, s = GROUP * g + j, j % 2
                    taps = [sb["cols_b"][:, bass.ds(b + c_lo + 12 * i, 1)] for i in range(3)]
                    dve.wait_ge(y_free[s], 1).then_inc(y_free[s], -1)
                    dve.tensor_scalar(y[s][:, :].rearrange("p (o n) -> p o n", o=1), pb[:, bass.ds(b, 1), :], taps[1], None, ALU.mult).then_inc(step, 1)
                    dve.wait_ge(step, 1).then_inc(step, -1)
                    for i, (src, dst) in ((0, (0, 1)), (2, (1, 0))):
                        for lo, n in ((0, CTX_LEN), (CTX_LEN, SEQ)):
                            o = y[s][:, lo + dst:lo + dst + n - 1].rearrange("p (o n) -> p o n", o=1)
                            dve.scalar_tensor_tensor(out=o, in0=pb[:, bass.ds(b, 1), lo + src:lo + src + n - 1],
                                                     scalar=taps[i], in1=o, op0=ALU.mult, op1=ALU.add).then_inc(step, 1)
                        dve.wait_ge(step, 2).then_inc(step, -2)
                    dve.sem_inc(y_full[s], 1)

                def inverted(j):
                    s = j % 2
                    dve.wait_ge(root_full[s], 1).then_inc(root_full[s], -1)
                    dve.reciprocal(root[s][:, :], root[s][:, :]).then_inc(inverse_full[s], 1)

                def scaled(g, j):
                    s = j % 2
                    dve.wait_ge(norm_full[s], 1).then_inc(norm_full[s], -1)
                    dve.scalar_tensor_tensor(out=z[j][:, :], in0=norm[s][:, 0:TOK], scalar=scales[:, bass.ds(g, 1)], in1=z[j][:, :],
                                             op0=ALU.mult, op1=ALU.mult).then_inc(out_ready[j], 1)

                def normalised(g):
                    for j in range(GROUP + 2):
                        if j < GROUP:
                            convolved(g, j)
                        if 1 <= j <= GROUP:
                            inverted(j - 1)
                        if j >= 2:
                            scaled(g, j - 2)

                def plain(g):
                    for j in range(GROUP):
                        convolved(g, j)
                over_groups(dve, normalised, plain)

            @block.scalar
            def _(act):
                act.wait_ge(constants, 1)

                def silu(j, *to):
                    s = j % 2
                    act.wait_ge(y_full[s], 1).then_inc(y_full[s], -1)
                    act.wait_ge(stored[j], 16).then_inc(stored[j], -16)
                    act.activation(z[j][:, :], y[s][:, :], ACT.Silu).then_inc(act_step, 1)
                    act.wait_ge(act_step, 1).then_inc(act_step, -1)
                    for x_ in (y_free[s], *to):
                        act.sem_inc(x_, 1)

                def rooted(j):
                    s = j % 2
                    act.wait_ge(sums_full[s], 1).then_inc(sums_full[s], -1)
                    act.activation(root[s][:, :], sums[s][:, :], ACT.Sqrt, bias=eps[:, :]).then_inc(root_full[s], 1)

                def normalised(g):
                    for j in range(GROUP + 1):
                        if j < GROUP:
                            silu(j)
                            act.wait_ge(sq_free, 1).then_inc(sq_free, -1)
                            act.activation(sq[:, :], z[j][:, :], ACT.Square).then_inc(sq_full, 1)
                        if j >= 1:
                            rooted(j - 1)

                def plain(g):
                    for j in range(GROUP):
                        silu(j, out_ready[j])
                over_groups(act, normalised, plain)

            @block.tensor
            def _(pe):
                def summed(j):
                    s = j % 2
                    pe.wait_ge(sq_full, 1).then_inc(sq_full, -1)
                    for t in range(NT):
                        mm = pe.matmul(sums[s][:, t:t + 1], sq[:, t * P:(t + 1) * P], sb["ones"][:, 0:1], start=True, stop=True)
                    mm.then_inc(sums_full[s], 1)
                    pe.drain().then_inc(sq_free, 1)

                def spread(j):
                    s = j % 2
                    pe.wait_ge(inverse_full[s], 1).then_inc(inverse_full[s], -1)
                    for t in range(NT):
                        mm = pe.matmul(norm[s][:, t * P:(t + 1) * P], root[s][:, t:t + 1].to_broadcast([P, P]), sb["ident"][:, :], start=True, stop=True)
                    mm.then_inc(norm_full[s], 1)

                def normalised(g):
                    for j in range(GROUP + 1):
                        if j < GROUP:
                            summed(j)
                        if j >= 1:
                            spread(j - 1)
                over_groups(pe, normalised, lambda g: None)

            @block.sync
            def _(sp):
                def store(g):
                    for j in range(GROUP):
                        sp.wait_ge(out_ready[j], 1).then_inc(out_ready[j], -1)
                        sp.dma_start(qkv_dram[bass.ds(GROUP * g + j, 1), :, :].rearrange("o p n -> p o n"),
                                     z[j][:, :].rearrange("p (o n) -> p o n", o=1)).then_inc(stored[j], 16)
                over_groups(sp, store, store)
                for j in range(GROUP):
                    sp.wait_ge(stored[j], 16)


def window_prepare(nc, a, sb, pa, k_dup, v_tok):
    with Stage(nc, "wprep") as st:
        names = ("swap", "dup0", "dup1", "dupswap0", "dupswap1")
        m = {n: st.sb(n, P, P) for n in names}
        cos, sin = st.sb("cos", P, TOK), st.sb("sin", P, TOK)
        tmp = [st.sb(f"tmp{i}", P, 512) for i in range(2)]
        turned = st.sb("turned", P, TOK)
        rot = [st.ps(f"rot{j}", P, 512) for j in range(4)]
        vt = [st.ps(f"vt{j}", P, 512) for j in range(3)]
        loaded, full, free, step, v_full = st.sem("loaded"), st.sem("full", 4), st.sem("free", 4), st.sem("step"), st.sem("v_full")
        q_free = st.sem("q_free")
        with nc.Block() as block:
            @block.sync
            def _(sp):
                for n in names:
                    sp.dma_start(m[n][:, :], a["mats"][MATS.index(n)]).then_inc(loaded, 16)
                sp.dma_start(cos[:, :], a["rope_a"][0]).then_inc(loaded, 16)
                sp.dma_start(sin[:, :], a["rope_a"][1]).then_inc(loaded, 16)

            @block.tensor
            def _(pe):
                pe.wait_ge(loaded, 112)
                with pe.Fori(0, 4) as b:
                    for j, (t0, n) in enumerate(ALL_CHUNKS):
                        pe.wait_ge(free[j], 1).then_inc(free[j], -1)
                        pe.matmul(rot[j][:, 0:n], m["swap"][:, :], pa[:, bass.ds(b, 1), t0:t0 + n].rearrange("p o n -> p (o n)"), start=True, stop=True).then_inc(full[j], 1)
                for kv in range(2):
                    for j, (t0, n) in enumerate(ALL_CHUNKS):
                        for h, name in enumerate((f"dup{kv}", f"dupswap{kv}")):
                            r = (2 * j + h) % 4
                            pe.wait_ge(free[r], 1).then_inc(free[r], -1)
                            pe.matmul(rot[r][:, 0:n], m[name][:, :], pa[:, 4, t0:t0 + n], start=True, stop=True).then_inc(full[r], 1)
                for t in range(NT):
                    mm = pe.transpose(vt[t // 4][:, t % 4 * P:(t % 4 + 1) * P], pa[:, 5, t * P:(t + 1) * P], sb["ident"][:, :])
                mm.then_inc(v_full, 1)

            @block.vector
            def _(dve):
                def done(ins, n=1):
                    ins.then_inc(step, 1)
                    dve.wait_ge(step, 1).then_inc(step, -1)

                give(dve, free)
                dve.wait_ge(loaded, 112)
                with dve.Fori(0, 4) as b:
                    q = pa[:, bass.ds(b, 1), :]
                    w = lambda ap: ap.rearrange("p (o n) -> p o n", o=1)
                    for j, (t0, n) in enumerate(ALL_CHUNKS):
                        dve.wait_ge(full[j], 1).then_inc(full[j], -1)
                        dve.tensor_tensor(turned[:, t0:t0 + n], rot[j][:, 0:n], sin[:, t0:t0 + n], ALU.mult).then_inc(step, 1)
                    dve.tensor_tensor(q, q, w(cos[:, :]), ALU.mult).then_inc(step, 1)
                    dve.wait_ge(step, len(ALL_CHUNKS) + 1).then_inc(step, -len(ALL_CHUNKS) - 1)
                    for j in range(len(ALL_CHUNKS)):
                        dve.sem_inc(free[j], 1)
                    done(dve.tensor_tensor(q, q, w(turned[:, :]), ALU.add))
                for kv in range(2):
                    dve.memset(k_dup[:, kv, 0:P], 0.0)
                    dve.memset(k_dup[:, kv, P + TOK:], 0.0)
                    for j, (t0, n) in enumerate(ALL_CHUNKS):
                        r = (2 * j) % 4
                        dve.wait_ge(full[r], 1).then_inc(full[r], -1)
                        done(dve.tensor_tensor(tmp[0][:, 0:n], rot[r][:, 0:n], cos[:, t0:t0 + n], ALU.mult))
                        dve.sem_inc(free[r], 1)
                        dve.wait_ge(full[r + 1], 1).then_inc(full[r + 1], -1)
                        done(dve.tensor_tensor(tmp[1][:, 0:n], rot[r + 1][:, 0:n], sin[:, t0:t0 + n], ALU.mult))
                        dve.sem_inc(free[r + 1], 1)
                        done(dve.tensor_tensor(k_dup[:, kv, P + t0:P + t0 + n], tmp[0][:, 0:n], tmp[1][:, 0:n], ALU.add))
                dve.memset(v_tok[:, 0, :], 0.0)
                dve.memset(v_tok[:, NT + 1, :], 0.0)
                dve.wait_ge(v_full, 1).then_inc(v_full, -1)
                for j, (t0, n) in enumerate(ALL_CHUNKS):
                    dve.tensor_copy(v_tok[:, 1 + 4 * j:1 + 4 * j + n // P, :], vt[j][:, 0:n].rearrange("p (t d) -> p t d", d=P))


def window_attention(nc, a, sb, pa, k_dup, v_tok, x):
    W = 3 * P
    scale = float(A_DIM) ** -0.5
    PAIRS = NT // 2
    with Stage(nc, "watt") as st:
        q = [st.sb(f"q{s}", P, 4, P) for s in range(2)]
        k = [st.sb(f"k{s}", P, A_KV, W) for s in range(2)]
        mask = [st.sb(f"mask{s}", P, W) for s in range(2)]
        sink, neg_sink, sink_arg = st.sb("sink", P, A_HEADS), st.sb("neg_sink", P, A_HEADS), st.sb("sink_arg", P, 2, A_HEADS)
        prob = [st.sb(f"prob{r}", P, CTX_LEN + W) for r in range(2)]
        prob_t = st.sb("prob_t", P, CTX_LEN + W)
        top, neg_top, total, sink_exp = (st.sb(n, P, 2, A_HEADS) for n in ("top", "neg_top", "total", "sink_exp"))
        o_tok = [st.sb(f"o{s}", P, 4 * P) for s in range(2)]
        C0 = 512 - CTX_LEN
        s_ps = [st.ps(f"sps{r}", P, 1024) for r in range(2)]
        t_ps = st.ps("tps", P, 1024)
        o_ps = [st.ps(f"ops{s}", P, 512) for s in range(2)]
        q_in, q_free, mask_free = st.sem("q_in", 2), st.sem("q_free", 2), st.sem("mask_free", 2)
        mask_in, sink_in = st.sem("mask_in", 2), st.sem("sink_in")
        s_full, s_free, neg_ready = st.sem("s_full", 2), st.sem("s_free", 2), st.sem("neg_ready", 2)
        p_full, t_full, pt_full = st.sem("p_full", 2), st.sem("t_full"), st.sem("pt_full")
        o_full, o_free, o_done, ot_full = st.sem("o_full", 2), st.sem("o_free", 2), st.sem("o_done", 2), st.sem("ot_full", 2)
        arg_ready, sink_done, step, act_step = st.sem("arg_ready"), st.sem("sink_done"), st.sem("step"), st.sem("act_step")

        def over_pairs(eng, body):
            body(0, False, True)
            with eng.Fori(1, PAIRS - 1) as i:
                body(i, True, True)
            body(PAIRS - 1, True, None)

        def unit_at(n, window, nxt):
            if n >= 2 * A_HEADS:
                return None if nxt is None else (0, n - 2 * A_HEADS, nxt)
            return n // A_HEADS, n % A_HEADS, window

        with nc.Block() as block:
            @block.sync
            def _(sp):
                sp.dma_start(sink[:, :], a["ab_sink"].to_broadcast([P, A_HEADS])).then_inc(sink_in, 16)

                def body(i, window, nxt):
                    for s in range(2):
                        t = 2 * i + s
                        sp.wait_ge(q_free[s], 1).then_inc(q_free[s], -1)
                        sp.dma_start(q[s][:, :, :], pa[:, 0:4, bass.ds(t * P, P)]).then_inc(q_in[s], 16)
                        if window:
                            sp.dma_start(k[s][:, :, :], k_dup[:, :, bass.ds(t * P, W)]).then_inc(q_in[s], 16)
                            sp.wait_ge(mask_free[s], 1).then_inc(mask_free[s], -1)
                            sp.dma_start(mask[s][:, :], a["window"][bass.ds(t, 1), :, :].rearrange("o p n -> p (o n)")).then_inc(mask_in[s], 16)
                over_pairs(sp, body)

            @block.tensor
            def _(pe):
                def scores(s, h, window):
                    r, kv, lo = h % 2, h // (A_HEADS // A_KV), (h % 2) * A_DIM
                    if h == 0 and window:
                        pe.wait_ge(q_in[s], 32).then_inc(q_in[s], -32)
                    if h == 0 and not window:
                        pe.wait_ge(q_in[s], 16).then_inc(q_in[s], -16)
                    pe.wait_ge(s_free[r], 1).then_inc(s_free[r], -1)
                    qh = q[s][lo:lo + A_DIM, h // 2, :]
                    mm = pe.matmul(s_ps[r][:, C0:512], qh, k_dup[lo:lo + A_DIM, kv, P:P + CTX_LEN], start=True, stop=True)
                    if window:
                        mm = pe.matmul(s_ps[r][:, 512:512 + W], qh, k[s][lo:lo + A_DIM, kv, :], start=True, stop=True)
                    mm.then_inc(s_full[r], 1)
                    if h == A_HEADS - 1:
                        pe.drain().then_inc(q_free[s], 1)

                def turned(h, blocks):
                    r = h % 2
                    pe.wait_ge(p_full[r], 1).then_inc(p_full[r], -1)
                    for j in range(blocks):
                        mm = pe.transpose(t_ps[:, j * P:(j + 1) * P], prob[r][:, j * P:(j + 1) * P], sb["ident"][:, :])
                    mm.then_inc(t_full, 1)

                def values(s, h, t, blocks):
                    kv = h // (A_HEADS // A_KV)
                    pe.wait_ge(pt_full, 1).then_inc(pt_full, -1)
                    if h == 0:
                        pe.wait_ge(o_free[s], 1).then_inc(o_free[s], -1)
                    for j in range(blocks):
                        v = (v_tok[:, 1 + j, kv * A_DIM:(kv + 1) * A_DIM] if j < CT
                             else v_tok[:, bass.ds(t + (j - CT), 1), kv * A_DIM:(kv + 1) * A_DIM].rearrange("p o n -> p (o n)"))
                        mm = pe.matmul(o_ps[s][:, h * A_DIM:(h + 1) * A_DIM], prob_t[:, j * P:(j + 1) * P], v, start=(j == 0), stop=(j == blocks - 1))
                    if h == A_HEADS - 1:
                        mm.then_inc(o_full[s], 1)

                def output_turned(s):
                    pe.wait_ge(o_done[s], 1).then_inc(o_done[s], -1)
                    for b in range(4):
                        mm = pe.transpose(o_ps[s][:, b * P:(b + 1) * P], o_tok[s][:, b * P:(b + 1) * P], sb["ident"][:, :])
                    mm.then_inc(ot_full[s], 1)

                def body(i, window, nxt):
                    for n in range(2 * A_HEADS):
                        s, h, _w = unit_at(n, window, nxt)
                        blocks = (CTX_LEN + W if window else CTX_LEN) // P
                        turned(h, blocks)
                        ahead = unit_at(n + 2, window, nxt)
                        if ahead is not None:
                            scores(*ahead)
                        values(s, h, 2 * i + s, blocks)
                        if h == 0 and (s == 1 or window):
                            output_turned(1 - s)
                scores(0, 0, False)
                scores(0, 1, False)
                over_pairs(pe, body)
                output_turned(1)

            @block.vector
            def _(dve):
                def done(ins, *to):
                    ins.then_inc(step, 1)
                    dve.wait_ge(step, 1).then_inc(step, -1)
                    for x_ in to:
                        dve.sem_inc(x_, 1)

                def maximum(s, h, window):
                    r = h % 2
                    dve.wait_ge(s_full[r], 1).then_inc(s_full[r], -1)
                    if window:
                        if h == 0:
                            dve.wait_ge(mask_in[s], 16).then_inc(mask_in[s], -16)
                        done(dve.tensor_tensor(s_ps[r][:, 512:512 + W], s_ps[r][:, 512:512 + W], mask[s][:, :], ALU.add))
                        if h == A_HEADS - 1:
                            dve.sem_inc(mask_free[s], 1)
                    done(dve.tensor_reduce(top[:, s, h:h + 1], s_ps[r][:, C0:C0 + CTX_LEN + (W if window else 0)], AX_X, ALU.max))
                    done(dve.tensor_scalar(neg_top[:, s, h:h + 1], top[:, s, h:h + 1], -scale, neg_sink[:, h:h + 1], ALU.mult, ALU.min), neg_ready[r])
                    if h == A_HEADS - 1:
                        dve.tensor_tensor(sink_arg[:, s, :], sink[:, :], neg_top[:, s, :], ALU.add).then_inc(arg_ready, 1)

                def divided(s):
                    dve.wait_ge(sink_done, 1).then_inc(sink_done, -1)
                    done(dve.tensor_tensor(total[:, s, :], total[:, s, :], sink_exp[:, s, :], ALU.add))
                    done(dve.reciprocal(total[:, s, :], total[:, s, :]))
                    dve.wait_ge(o_full[s], 1).then_inc(o_full[s], -1)
                    dve.tensor_tensor(o_tok[s][:, :].rearrange("p (h d) -> p h d", h=A_HEADS), o_ps[s][:, :].rearrange("p (h d) -> p h d", h=A_HEADS),
                                      total[:, s, :].rearrange("p (h o) -> p h o", o=1).to_broadcast([P, A_HEADS, A_DIM]), ALU.mult).then_inc(o_done[s], 1)

                def output(s, t):
                    dve.wait_ge(ot_full[s], 1).then_inc(ot_full[s], -1)
                    dve.tensor_copy(x[:, 0:4, bass.ds(t * P, P)], o_ps[s][:, :].rearrange("p (b n) -> p b n", b=4)).then_inc(o_free[s], 1)

                def body(i, window, nxt):
                    for n in range(2 * A_HEADS):
                        s, h, _w = unit_at(n, window, nxt)
                        ahead = unit_at(n + 2, window, nxt)
                        if ahead is not None:
                            maximum(*ahead)
                        if h == A_HEADS - 1:
                            divided(s)
                        if h == 0 and (s == 1 or window):
                            output(1 - s, 2 * i + s - 1)

                for g in (q_free, mask_free, o_free):
                    give(dve, g)
                dve.wait_ge(sink_in, 16)
                done(dve.tensor_scalar(neg_sink[:, :], sink[:, :], -1.0, None, ALU.mult))
                maximum(0, 0, False)
                maximum(0, 1, False)
                over_pairs(dve, body)
                output(1, NT - 1)

            @block.scalar
            def _(act):
                def exponent(s, h, window):
                    r = h % 2
                    act.wait_ge(neg_ready[r], 1).then_inc(neg_ready[r], -1)
                    keys = CTX_LEN + (W if window else 0)
                    act.activation(prob[r][:, 0:keys], s_ps[r][:, C0:C0 + keys], ACT.Exp, scale=scale, bias=neg_top[:, s, h:h + 1],
                                   accum_out=total[:, s, h:h + 1]).then_inc(act_step, 1)
                    act.wait_ge(act_step, 1).then_inc(act_step, -1)
                    act.sem_inc(s_free[r], 1)
                    act.sem_inc(p_full[r], 1)
                    if h == A_HEADS - 1:
                        act.wait_ge(arg_ready, 1).then_inc(arg_ready, -1)
                        act.activation(sink_exp[:, s, :], sink_arg[:, s, :], ACT.Exp).then_inc(sink_done, 1)

                def body(i, window, nxt):
                    for n in range(2 * A_HEADS):
                        keys = CTX_LEN + (W if window else 0)
                        act.wait_ge(t_full, 1).then_inc(t_full, -1)
                        act.activation(prob_t[:, 0:keys], t_ps[:, 0:keys], ACT.Copy).then_inc(pt_full, 1)
                        ahead = unit_at(n + 1, window, nxt)
                        if ahead is not None:
                            exponent(*ahead)

                give(act, s_free)
                exponent(0, 0, False)
                over_pairs(act, body)


def delta_rule(nc, a, sb, qkv_dram, cols, o_dirs):
    HP = [P, B_HEADS, P]
    with Stage(nc, "delta") as st:
        levels = [[st.sb(f"level{d}{l}", P, P) for l in range(LEVELS)] for d in range(2)]
        cum = [st.sb(f"cum{d}", P, P) for d in range(2)]
        dmask = [st.sb(f"dmask{d}", P, P) for d in range(2)]
        qkv = [[st.sb(f"qkv{d}{s}", P, 12, P) for s in range(2)] for d in range(2)]
        names = ("ld", "col", "dec", "egrow", "b", "aqk", "uu", "vv", "ww", "ktok", "vtok", "vn", "vt", "state")
        t = [{n: st.sb(f"{n}{d}", P, 2, 6, B_HEADS) if n == "col" else st.sb(f"{n}{d}", *HP) for n in names} for d in range(2)]
        bank = [[st.ps(f"bank{d}{j}", *HP) for j in range(4)] for d in range(2)]
        E = lambda n: st.sem(n, 2)
        loaded = st.sem("loaded")
        qkv_in = [st.sem(f"qkv_in{d}", 2) for d in range(2)]
        qkv_free = [st.sem(f"qkv_free{d}", 2) for d in range(2)]
        ld_full, ld_free, col_full, col_free, pool_step = E("ld_full"), E("ld_free"), E("col_full"), E("col_free"), st.sem("pool_step")
        masks_in, qkv_here = st.sem("masks_in"), E("qkv_here")
        b_set, first_uu, eq_full = E("b_set"), E("first_uu"), E("eq_full")
        grow_full, grow_read, decay_raw, decay_full, egrow_full = E("grow_full"), E("grow_read"), E("decay_raw"), E("decay_full"), E("egrow_full")
        tok_copied, kk_full, kq_full, tok_full, tok_read, vtok_full = E("tok_copied"), E("kk_full"), E("kq_full"), E("tok_full"), E("tok_read"), E("vtok_full")
        b_full, w_psum, w_full, v_psum, u_psum, uv_full = E("b_full"), E("w_psum"), E("w_full"), E("v_psum"), E("u_psum"), E("uv_full")
        ks_full, r_full, vn_psum, vn_full = E("ks_full"), E("r_full"), E("vn_psum"), E("vn_full")
        o_full, o_read, s_psum, s_full = E("o_full"), E("o_read"), E("s_psum"), E("s_full")
        step, act_step = st.sem("step"), st.sem("act_step")

        def bc(m):
            return m[:, :].rearrange("p (o n) -> p o n", o=1).to_broadcast(HP)

        def per_head(d, s, kind):
            return t[d]["col"][:, s, kind, :].rearrange("p (h o) -> p h o", o=1).to_broadcast(HP)

        def over_chunks(eng, body):
            for s in range(CT):
                body(s, (s, CT - 1 - s))
            with eng.Fori(0, LT // 2) as i:
                for s in range(2):
                    body(s, (2 * i + s + CT, NT - 1 - s - 2 * i))

        with nc.Block() as block:
            @block.sync
            def _(sp):
                for d in range(2):
                    for l in range(LEVELS):
                        sp.dma_start(levels[d][l][:, :], a["mats"][MATS.index(f"level{d}_{l}")]).then_inc(loaded, 16)
                    sp.dma_start(cum[d][:, :], a["mats"][MATS.index(f"cum{d}")]).then_inc(loaded, 16)
                    sp.dma_start(dmask[d][:, :], a["mats"][MATS.index(f"decay_mask{d}")]).then_inc(loaded, 16)

                def load(s, tiles):
                    for d in range(2):
                        sp.wait_ge(qkv_free[d][s], 1).then_inc(qkv_free[d][s], -1)
                        sp.dma_start(qkv[d][s][:, :, :], qkv_dram.rearrange("b p n -> p b n")[:, :, bass.ds(tiles[d] * P, P)]).then_inc(qkv_in[d][s], 16)
                over_chunks(sp, load)

            @block.gpsimd
            def _(pool):
                def spread(s, tiles):
                    for d in range(2):
                        pool.wait_ge(col_free[d], 1).then_inc(col_free[d], -1)
                        pool.tensor_copy(t[d]["col"][:, s, :, :].rearrange("p k h -> p (k h)"),
                                         cols[:, bass.ds(tiles[d], 1), d, :, :].rearrange("p o k h -> p (o k h)")).then_inc(pool_step, 1)
                        pool.wait_ge(pool_step, 1).then_inc(pool_step, -1)
                        pool.sem_inc(col_full[d], 1)
                        pool.wait_ge(ld_free[d], 1).then_inc(ld_free[d], -1)
                        pool.tensor_copy(t[d]["ld"][:, :, :], per_head(d, s, 0)).then_inc(ld_full[d], 1)

                def done(ins):
                    ins.then_inc(pool_step, 1)
                    pool.wait_ge(pool_step, 1).then_inc(pool_step, -1)

                def first_inverse(s, tiles):
                    for d in range(2):
                        x = t[d]
                        pool.wait_ge(b_set[d], 1).then_inc(b_set[d], -1)
                        done(pool.tensor_tensor(x["uu"][:, :, :], x["b"][:, :, :], bc(levels[1 - d][0]), ALU.mult))
                        pool.tensor_tensor(x["uu"][:, :, :], bc(sb["ident"]), x["uu"][:, :, :], ALU.subtract).then_inc(first_uu[d], 1)
                    for d in range(2):
                        x = t[d]
                        pool.wait_ge(egrow_full[d], 1).then_inc(egrow_full[d], -1)
                        pool.wait_ge(qkv_here[d], 1).then_inc(qkv_here[d], -1)
                        pool.tensor_tensor(x["egrow"][:, :, :], qkv[d][s][:, 0:B_HEADS, :], x["egrow"][:, :, :], ALU.mult).then_inc(eq_full[d], 1)

                def chunk(s, tiles):
                    spread(s, tiles)
                    first_inverse(s, tiles)
                pool.wait_ge(masks_in, 1).then_inc(masks_in, -1)
                over_chunks(pool, chunk)

            @block.tensor
            def _(pe):
                pe.wait_ge(loaded, 16 * 2 * (LEVELS + 2))

                def heads4(d, j, lhs, rhs, start=True, stop=True):
                    for h in range(B_HEADS):
                        mm = pe.matmul(bank[d][j][:, h, :], lhs(h), rhs(h), start=start, stop=stop)
                    return mm

                def chunk(s, tiles):
                    T = lambda d, n: (lambda h: t[d][n][:, h, :])
                    Q = lambda d: (lambda h: qkv[d][s][:, h, :])
                    K = lambda d: (lambda h: qkv[d][s][:, B_HEADS + h, :])
                    ident = lambda h: sb["ident"][:, :]
                    for d in range(2):
                        pe.wait_ge(ld_full[d], 1).then_inc(ld_full[d], -1)
                        pe.wait_ge(o_read[d], 1).then_inc(o_read[d], -1)
                        heads4(d, 0, T(d, "ld"), lambda h: cum[d][:, :]).then_inc(grow_full[d], 1)
                    for d in range(2):
                        pe.wait_ge(qkv_in[d][s], 16).then_inc(qkv_in[d][s], -16)
                        heads4(d, 1, K(d), K(d)).then_inc(kk_full[d], 1)
                        heads4(d, 2, K(d), Q(d)).then_inc(kq_full[d], 1)
                        pe.wait_ge(s_full[d], 1).then_inc(s_full[d], -1)
                        for h in range(B_HEADS):
                            pe.transpose(bank[d][3][:, h, :], K(d)(h), sb["ident"][:, :])
                        pe.wait_ge(grow_read[d], 1).then_inc(grow_read[d], -1)
                        for h in range(B_HEADS):
                            mm = pe.transpose(bank[d][0][:, h, :], qkv[d][s][:, 2 * B_HEADS + h, :], sb["ident"][:, :])
                        mm.then_inc(tok_full[d], 1)
                    for d in range(2):
                        pe.wait_ge(b_full[d], 1).then_inc(b_full[d], -1)
                        heads4(d, 1, T(d, "b"), ident).then_inc(w_psum[d], 1)
                    for l in range(1, LEVELS):
                        for d in range(2):
                            pe.wait_ge(uv_full[d], 1).then_inc(uv_full[d], -1)
                            if l == 1:
                                pe.wait_ge(tok_read[d], 1).then_inc(tok_read[d], -1)
                            heads4(d, 2, T(d, "b"), T(d, "vv")).then_inc(w_psum[d], 1)
                        for d in range(2):
                            pe.wait_ge(w_full[d], 1).then_inc(w_full[d], -1)
                            if l == 1:
                                pe.wait_ge(tok_copied[d], 1).then_inc(tok_copied[d], -1)
                                pe.wait_ge(first_uu[d], 1).then_inc(first_uu[d], -1)
                            if l < LEVELS - 1:
                                heads4(d, 1, T(d, "uu"), T(d, "ww")).then_inc(v_psum[d], 1)
                            heads4(d, 3, T(d, "ww"), T(d, "uu")).then_inc(u_psum[d], 1)
                    for d in range(2):
                        pe.wait_ge(eq_full[d], 1).then_inc(eq_full[d], -1)
                        heads4(d, 1, K(d), T(d, "state")).then_inc(ks_full[d], 1)
                    for d in range(2):
                        pe.wait_ge(r_full[d], 1).then_inc(r_full[d], -1)
                        heads4(d, 2, T(d, "uu"), T(d, "vv")).then_inc(vn_psum[d], 1)
                    for d in range(2):
                        pe.wait_ge(vn_full[d], 1).then_inc(vn_full[d], -1)
                        for h in range(B_HEADS):
                            pe.matmul(bank[d][0][:, h, :], t[d]["state"][:, h, :], t[d]["egrow"][:, h, :], start=True, stop=False)
                            mm = pe.matmul(bank[d][0][:, h, :], t[d]["vn"][:, h, :], t[d]["aqk"][:, h, :], start=False, stop=True)
                        mm.then_inc(o_full[d], 1)
                        heads4(d, 3, T(d, "ktok"), T(d, "vt")).then_inc(s_psum[d], 1)
                over_chunks(pe, chunk)

            @block.vector
            def _(dve):
                def done(ins, *to):
                    ins.then_inc(step, 1)
                    dve.wait_ge(step, 1).then_inc(step, -1)
                    for x in to:
                        dve.sem_inc(x, 1)

                dve.wait_ge(loaded, 16 * 2 * (LEVELS + 2))
                dve.sem_inc(masks_in, 1)
                for d in range(2):
                    give(dve, qkv_free[d])
                    dve.memset(t[d]["state"][:, :, :], 0.0).then_inc(step, 1)
                dve.wait_ge(step, 2).then_inc(step, -2)
                for g in (ld_free, o_read, s_full):
                    give(dve, g)
                give(dve, col_free, 2)

                def chunk(s, tiles):
                    for d in range(2):
                        x = t[d]
                        dve.wait_ge(col_full[d], 1).then_inc(col_full[d], -1)
                        dve.wait_ge(grow_full[d], 1).then_inc(grow_full[d], -1)
                        dve.sem_inc(ld_free[d], 1)
                        for h in range(B_HEADS):
                            dve.scalar_tensor_tensor(out=x["dec"][:, h, :], in0=bank[d][0][:, h, :], scalar=x["col"][:, s, 1, h:h + 1],
                                                     in1=dmask[d][:, :], op0=ALU.subtract, op1=ALU.add).then_inc(step, 1)
                        dve.wait_ge(step, B_HEADS).then_inc(step, -B_HEADS)
                        dve.sem_inc(decay_raw[d], 1)
                    for d in range(2):
                        x = t[d]
                        dve.wait_ge(kk_full[d], 1).then_inc(kk_full[d], -1)
                        dve.wait_ge(decay_full[d], 1).then_inc(decay_full[d], -1)
                        for h in range(B_HEADS):
                            dve.scalar_tensor_tensor(out=x["b"][:, h, :], in0=bank[d][1][:, h, :], scalar=x["col"][:, s, 2, h:h + 1],
                                                     in1=x["dec"][:, h, :], op0=ALU.mult, op1=ALU.mult).then_inc(step, 1)
                        dve.wait_ge(step, B_HEADS).then_inc(step, -B_HEADS)
                        dve.sem_inc(b_full[d], 1)
                        dve.sem_inc(b_set[d], 1)
                        dve.sem_inc(qkv_here[d], 1)
                    for d in range(2):
                        x = t[d]
                        dve.wait_ge(w_psum[d], 1).then_inc(w_psum[d], -1)
                        done(dve.tensor_tensor(x["vv"][:, :, :], bank[d][1][:, :, :], bc(levels[d][0]), ALU.mult))
                        done(dve.scalar_tensor_tensor(out=x["vv"][:, :, :], in0=x["vv"][:, :, :], scalar=-1.0, in1=bc(sb["ident"]), op0=ALU.mult, op1=ALU.add), uv_full[d])
                    for d in range(2):
                        x = t[d]
                        dve.wait_ge(kq_full[d], 1).then_inc(kq_full[d], -1)
                        done(dve.tensor_tensor(x["aqk"][:, :, :], bank[d][2][:, :, :], x["dec"][:, :, :], ALU.mult), tok_read[d])
                    for l in range(1, LEVELS):
                        for d in range(2):
                            dve.wait_ge(w_psum[d], 1).then_inc(w_psum[d], -1)
                            done(dve.tensor_tensor(t[d]["ww"][:, :, :], bank[d][2][:, :, :], bc(levels[d][l]), ALU.mult), w_full[d])
                        for d in range(2):
                            x = t[d]
                            if l < LEVELS - 1:
                                dve.wait_ge(v_psum[d], 1).then_inc(v_psum[d], -1)
                                done(dve.tensor_tensor(x["vv"][:, :, :], x["vv"][:, :, :], bank[d][1][:, :, :], ALU.subtract))
                            dve.wait_ge(u_psum[d], 1).then_inc(u_psum[d], -1)
                            done(dve.tensor_tensor(x["uu"][:, :, :], x["uu"][:, :, :], bank[d][3][:, :, :], ALU.subtract))
                            if l < LEVELS - 1:
                                dve.sem_inc(uv_full[d], 1)
                    for d in range(2):
                        x = t[d]
                        dve.wait_ge(ks_full[d], 1).then_inc(ks_full[d], -1)
                        dve.wait_ge(vtok_full[d], 1).then_inc(vtok_full[d], -1)
                        dve.sem_inc(qkv_free[d][s], 1)
                        for h in range(B_HEADS):
                            dve.scalar_tensor_tensor(out=x["vv"][:, h, :], in0=bank[d][1][:, h, :], scalar=x["col"][:, s, 3, h:h + 1],
                                                     in1=x["vtok"][:, h, :], op0=ALU.mult, op1=ALU.add).then_inc(step, 1)
                        dve.wait_ge(step, B_HEADS).then_inc(step, -B_HEADS)
                        dve.sem_inc(r_full[d], 1)
                    for d in range(2):
                        x = t[d]
                        dve.wait_ge(vn_psum[d], 1).then_inc(vn_psum[d], -1)
                        done(dve.tensor_tensor(x["vn"][:, :, :], bank[d][2][:, :, :], per_head(d, s, 2), ALU.mult))
                        done(dve.tensor_tensor(x["vt"][:, :, :], bank[d][2][:, :, :], per_head(d, s, 4), ALU.mult), vn_full[d])
                    for d in range(2):
                        x = t[d]
                        dve.wait_ge(s_psum[d], 1).then_inc(s_psum[d], -1)
                        for h in range(B_HEADS):
                            dve.scalar_tensor_tensor(out=x["state"][:, h, :], in0=x["state"][:, h, :], scalar=x["col"][:, s, 5, h:h + 1],
                                                     in1=bank[d][3][:, h, :], op0=ALU.mult, op1=ALU.add).then_inc(step, 1)
                        dve.wait_ge(step, B_HEADS).then_inc(step, -B_HEADS)
                        dve.sem_inc(s_full[d], 1)
                        dve.sem_inc(col_free[d], 1)
                over_chunks(dve, chunk)

            @block.scalar
            def _(act):
                def done(ins, *to):
                    ins.then_inc(act_step, 1)
                    act.wait_ge(act_step, 1).then_inc(act_step, -1)
                    for x in to:
                        act.sem_inc(x, 1)

                def chunk(s, tiles):
                    for d in range(2):
                        x = t[d]
                        act.wait_ge(decay_raw[d], 1).then_inc(decay_raw[d], -1)
                        done(act.activation(x["egrow"][:, :, :], bank[d][0][:, :, :], ACT.Exp), grow_read[d], egrow_full[d])
                        done(act.activation(x["dec"][:, :, :], x["dec"][:, :, :], ACT.Exp), decay_full[d])
                    for d in range(2):
                        x = t[d]
                        act.wait_ge(tok_full[d], 1).then_inc(tok_full[d], -1)
                        act.activation(x["ktok"][:, :, :], bank[d][3][:, :, :], ACT.Copy).then_inc(act_step, 1)
                        act.activation(x["vtok"][:, :, :], bank[d][0][:, :, :], ACT.Copy).then_inc(act_step, 1)
                        act.wait_ge(act_step, 2).then_inc(act_step, -2)
                        act.sem_inc(vtok_full[d], 1)
                        act.sem_inc(tok_copied[d], 1)
                    for d in range(2):
                        act.wait_ge(o_full[d], 1).then_inc(o_full[d], -1)
                        done(act.activation(o_dirs[d][:, :, bass.ds(tiles[d] * P, P)], bank[d][0][:, :, :], ACT.Copy), o_read[d])
                over_chunks(act, chunk)


def head_norm(nc, a, sb, o_f, o_b, gate):
    g_lo, _ = rows_at(ROWS_A, "out_norm")
    with Stage(nc, "hnorm") as st:
        sq = [st.sb(f"sq{h}", P, TOK) for h in range(B_HEADS)]
        silu = [st.sb(f"silu{h}", P, TOK) for h in range(B_HEADS)]
        root, eps = st.sb("root", P, B_HEADS, NT), st.sb("eps", P, 1)
        sums = st.ps("sums", P, B_HEADS, NT)
        norm = [st.ps(f"norm{s}", P, 3 * 512) for s in range(2)]
        eps_set, added, sq_full, sums_full, root_full, inverse_full, silu_full, step = (st.sem(n) for n in
            ("eps_set", "added", "sq_full", "sums_full", "root_full", "inverse_full", "silu_full", "step"))
        norm_full, norm_free = st.sem("norm_full", 2), st.sem("norm_free", 2)
        with nc.Block() as block:
            @block.vector
            def _(dve):
                dve.memset(eps[:, :], EPS).then_inc(eps_set, 1)
                give(dve, norm_free)
                for h in range(B_HEADS):
                    dve.tensor_tensor(o_f[:, h, :], o_f[:, h, :], o_b[:, h, :], ALU.add).then_inc(added, 1)
                dve.wait_ge(root_full, 1).then_inc(root_full, -1)
                dve.reciprocal(root[:, :, :], root[:, :, :]).then_inc(inverse_full, 1)
                dve.wait_ge(silu_full, B_HEADS).then_inc(silu_full, -B_HEADS)
                for h in range(B_HEADS):
                    dve.scalar_tensor_tensor(out=silu[h][:, :], in0=silu[h][:, :], scalar=sb["cols_a"][:, g_lo:g_lo + 1],
                                             in1=o_f[:, h, :], op0=ALU.mult, op1=ALU.mult).then_inc(step, 1)
                    dve.wait_ge(step, 1).then_inc(step, -1)
                    dve.wait_ge(norm_full[h % 2], 1).then_inc(norm_full[h % 2], -1)
                    dve.tensor_tensor(o_f[:, h, :], silu[h][:, :], norm[h % 2][:, 0:TOK], ALU.mult).then_inc(norm_free[h % 2], 1)

            @block.scalar
            def _(act):
                act.wait_ge(eps_set, 1)
                for h in range(B_HEADS):
                    act.wait_ge(added, 1).then_inc(added, -1)
                    act.activation(sq[h][:, :], o_f[:, h, :], ACT.Square).then_inc(sq_full, 1)
                act.wait_ge(sums_full, 1).then_inc(sums_full, -1)
                act.activation(root[:, :, :], sums[:, :, :], ACT.Sqrt, scale=1.0 / B_DIM, bias=eps[:, :]).then_inc(root_full, 1)
                for h in range(B_HEADS):
                    act.activation(silu[h][:, :], gate[:, h, :], ACT.Silu).then_inc(silu_full, 1)

            @block.tensor
            def _(pe):
                for h in range(B_HEADS):
                    pe.wait_ge(sq_full, 1).then_inc(sq_full, -1)
                    for t in range(NT):
                        mm = pe.matmul(sums[:, h, t:t + 1], sq[h][:, t * P:(t + 1) * P], sb["ones"][:, 0:1], start=True, stop=True)
                mm.then_inc(sums_full, 1)
                pe.wait_ge(inverse_full, 1).then_inc(inverse_full, -1)
                for h in range(B_HEADS):
                    pe.wait_ge(norm_free[h % 2], 1).then_inc(norm_free[h % 2], -1)
                    for t in range(NT):
                        mm = pe.matmul(norm[h % 2][:, t * P:(t + 1) * P], root[:, h, t:t + 1].to_broadcast([P, P]), sb["ident"][:, :], start=True, stop=True)
                    mm.then_inc(norm_full[h % 2], 1)




def latent_norms(nc, a, sb, c5, kpe, kpe_rot):
    q_lo, _ = rows_at(ROWS_A, "q_norm")
    with Stage(nc, "lnorm") as st:
        sq = [st.sb(f"sq{b}", P, TOK) for b in range(5)]
        root = [st.sb(f"root{g}", P, NT) for g in range(2)]
        place, swap = st.sb("place", P, P), st.sb("swap", P, P)
        cos, sin = st.sb("cos", P, TOK), st.sb("sin", P, TOK)
        tmp = [st.sb(f"tmp{i}", P, 512) for i in range(2)]
        eps = st.sb("eps", P, 1)
        sums = [st.ps(f"sums{g}", P, NT) for g in range(2)]
        norm = st.ps("norm", P, 3 * 512)
        rot = [st.ps(f"rot{i}", P, 512) for i in range(2)]
        loaded, eps_set, sq_full, sums_full, root_full, inverse_full, norm_full, norm_free, step, rot_full, rot_free = (st.sem(n) for n in
            ("loaded", "eps_set", "sq_full", "sums_full", "root_full", "inverse_full", "norm_full", "norm_free", "step", "rot_full", "rot_free"))
        groups = ((range(0, 3), QR, LAT_CHUNKS), (range(3, 5), KVR, ALL_CHUNKS))
        rr = slice(C_NOPE, C_QK)
        with nc.Block() as block:
            @block.sync
            def _(sp):
                sp.dma_start(place[:, :], a["mats"][MATS.index("kpe_place")]).then_inc(loaded, 16)
                sp.dma_start(swap[:, :], a["mats"][MATS.index("kpe_swap")]).then_inc(loaded, 16)
                sp.dma_start(cos[:, :], a["rope_c"][0]).then_inc(loaded, 16)
                sp.dma_start(sin[:, :], a["rope_c"][1]).then_inc(loaded, 16)

            @block.scalar
            def _(act):
                act.wait_ge(eps_set, 1)
                for b in range(5):
                    lo = CTX_LEN if b < 3 else 0
                    act.activation(sq[b][:, lo:], c5[:, b, lo:], ACT.Square).then_inc(sq_full, 1)
                for g, (blocks, rank, chunks) in enumerate(groups):
                    t_lo = chunks[0][0] // P
                    act.wait_ge(sums_full, 1).then_inc(sums_full, -1)
                    act.activation(root[g][:, t_lo:], sums[g][:, t_lo:], ACT.Sqrt, scale=1.0 / rank, bias=eps[:, :]).then_inc(root_full, 1)

            @block.tensor
            def _(pe):
                for g, (blocks, rank, chunks) in enumerate(groups):
                    pe.wait_ge(sq_full, blocks[-1] + 1)
                    for t in range(chunks[0][0] // P, NT):
                        for b in blocks:
                            mm = pe.matmul(sums[g][:, t:t + 1], sq[b][:, t * P:(t + 1) * P], sb["ones"][:, 0:1], start=(b == blocks[0]), stop=(b == blocks[-1]))
                    mm.then_inc(sums_full, 1)
                for g, (blocks, rank, chunks) in enumerate(groups):
                    pe.wait_ge(inverse_full, 1).then_inc(inverse_full, -1)
                    pe.wait_ge(norm_free, 1).then_inc(norm_free, -1)
                    for t in range(chunks[0][0] // P, NT):
                        mm = pe.matmul(norm[:, t * P:(t + 1) * P], root[g][:, t:t + 1].to_broadcast([P, P]), sb["ident"][:, :], start=True, stop=True)
                    mm.then_inc(norm_full, 1)
                pe.wait_ge(loaded, 64)
                for j, (t0, n) in enumerate(ALL_CHUNKS):
                    pe.wait_ge(rot_free, 1).then_inc(rot_free, -1)
                    pe.matmul(rot[0][:, 0:n], place[0:C_ROPE, :], kpe[:, 0, t0:t0 + n], start=True, stop=True)
                    pe.matmul(rot[1][:, 0:n], swap[0:C_ROPE, :], kpe[:, 0, t0:t0 + n], start=True, stop=True).then_inc(rot_full, 1)

            @block.vector
            def _(dve):
                def done(ins, n=1):
                    ins.then_inc(step, 1)
                    dve.wait_ge(step, 1).then_inc(step, -1)

                dve.memset(eps[:, :], EPS).then_inc(eps_set, 1)
                dve.wait_ge(loaded, 64)
                give(dve, [rot_free, norm_free])
                for g, (blocks, rank, chunks) in enumerate(groups):
                    t_lo = chunks[0][0] // P
                    dve.wait_ge(root_full, 1).then_inc(root_full, -1)
                    dve.reciprocal(root[g][:, t_lo:], root[g][:, t_lo:]).then_inc(inverse_full, 1)
                for g, (blocks, rank, chunks) in enumerate(groups):
                    lo = chunks[0][0]
                    dve.wait_ge(norm_full, 1).then_inc(norm_full, -1)
                    for b in blocks:
                        last = dve.scalar_tensor_tensor(out=c5[:, b, lo:], in0=c5[:, b, lo:], scalar=sb["cols_a"][:, q_lo + b:q_lo + b + 1],
                                                        in1=norm[:, lo:TOK], op0=ALU.mult, op1=ALU.mult)
                    last.then_inc(norm_free, 1)
                for j, (t0, n) in enumerate(ALL_CHUNKS):
                    dve.wait_ge(rot_full, 1).then_inc(rot_full, -1)
                    dve.tensor_tensor(tmp[0][rr, 0:n], rot[0][rr, 0:n], cos[rr, t0:t0 + n], ALU.mult).then_inc(step, 1)
                    dve.tensor_tensor(tmp[1][rr, 0:n], rot[1][rr, 0:n], sin[rr, t0:t0 + n], ALU.mult).then_inc(step, 1)
                    dve.wait_ge(step, 2).then_inc(step, -2)
                    dve.sem_inc(rot_free, 1)
                    done(dve.tensor_tensor(kpe_rot[rr, t0:t0 + n], tmp[0][rr, 0:n], tmp[1][rr, 0:n], ALU.add))


def latent_attention(nc, a, sb, c5, kpe_rot, x):
    scale = float(C_QK) ** -0.5
    NQ = LT
    AUG = C_QK + 1
    rr = slice(C_NOPE, C_QK)
    row = slice(C_QK, AUG)
    units = [(kt, half) for kt in range(NT) for half in range(2)]
    NS, NR = 3, 3
    NPT, LAG = 4, 2
    with Stage(nc, "latt") as st:
        wq = [st.sb(f"wq{s}", P, 3, C_QK) for s in range(2)]
        wkv = [st.sb(f"wkv{s}", P, 2, C_NOPE + C_V) for s in range(2)]
        q_swap = st.sb("q_swap", P, P)
        cos, sin = st.sb("cos", P, SEQ), st.sb("sin", P, SEQ)
        kt, qt = st.sb("kt", P, TOK), st.sb("qt", P, SEQ)
        kt_part = [[st.sb_r(f"kt{s}{x}", P, TOK) for x in range(2)] for s in range(2)]
        qt_part = [[st.sb_r(f"qt{s}{x}", P, SEQ) for x in range(2)] for s in range(2)]
        vt = [st.sb(f"vt{s}", P, NT, C_V + 1) for s in range(2)]
        prob = [st.sb(f"prob{r}", P, 512) for r in range(NPT)]
        tmp = st.sb("tmp", P, 512)
        o_tok = st.sb("o_tok", P, NQ, 2 * C_V)
        part_max = st.sb("part_max", P, NQ, 3)
        neg_max = st.sb("neg_max", P, NQ)
        rec = st.sb("rec", P, 2, 4)
        s_ps = [st.ps(f"s{r}", P, 512) for r in range(NS)]
        ring = [st.ps(f"ring{r}", P, 512) for r in range(NR)]
        o_ps = [st.ps(f"o{half}", P, 4, P) for half in range(2)]
        w_in, w_free = st.sem("w_in", 2), st.sem("w_free", 2)
        loaded, ones_set = st.sem("loaded"), st.sem("ones_set")
        ring_full, ring_free, q_copied = st.sem("ring_full", NR), st.sem("ring_free", NR), st.sem("q_copied")
        r_ready, neg_ready, head_ready = st.sem("r_ready"), st.sem("neg_ready"), st.sem("head_ready")
        rounded, hi_ready = st.sem("rounded"), st.sem("hi_ready")
        s_full, s_free = st.sem("s_full", NS), st.sem("s_free", NS)
        p_full, p_free = st.sem("p_full", NPT), st.sem("p_free", NPT)
        o_full, o_free, step, act_step = st.sem("o_full"), st.sem("o_free"), st.sem("step"), st.sem("act_step")
        pair_done = st.sem("pair_done")
        q_fixed, k_copied = st.sem("q_fixed"), st.sem("k_copied")
        n_units = len(units)

        def turns():
            n = 0
            while True:
                yield n % NR
                n += 1

        def over_heads(eng, prepare, main, pair):
            for piece in prepare(0):
                piece()
            main(0, prepare(1))
            main(1, prepare(0))
            with eng.Fori(1, C_HEADS // 2 - 1) as i:
                main(0, prepare(1, pair(i - 1)))
                main(1, prepare(0))
            main(0, prepare(1, pair(C_HEADS // 2 - 2)))
            main(1, [])
            for piece in pair(C_HEADS // 2 - 1):
                piece()

        with nc.Block() as block:
            @block.sync
            def _(sp):
                sp.dma_start(q_swap[:, :], a["mats"][MATS.index("q_swap")]).then_inc(loaded, 16)
                sp.dma_start(cos[:, :], a["rope_c"][0, :, CTX_LEN:]).then_inc(loaded, 16)
                sp.dma_start(sin[:, :], a["rope_c"][1, :, CTX_LEN:]).then_inc(loaded, 16)
                wq_v = a["mla_w_qb"][0].rearrange("(k p) n -> p k n", p=P)
                wkv_v = a["mla_w_kvb"][0].rearrange("(k p) n -> p k n", p=P)
                with sp.Fori(0, C_HEADS // 2) as i:
                    for s in range(2):
                        sp.wait_ge(w_free[s], 1).then_inc(w_free[s], -1)
                        sp.dma_start(wq[s][:, :, :], wq_v[:, :, bass.ds((2 * i + s) * C_QK, C_QK)]).then_inc(w_in[s], 16)
                        sp.dma_start(wkv[s][:, :, :], wkv_v[:, :, bass.ds((2 * i + s) * (C_NOPE + C_V), C_NOPE + C_V)]).then_inc(w_in[s], 16)

            @block.tensor
            def _(pe):
                turn = turns()
                pe.wait_ge(loaded, 48)
                pe.wait_ge(ones_set, 1)

                def prepare(s, after=()):
                    def query(j):
                        t0, n = LAT_CHUNKS[j]
                        if j == 0:
                            pe.wait_ge(w_in[s], 32).then_inc(w_in[s], -32)
                        r = next(turn)
                        pe.wait_ge(ring_free[r], 1).then_inc(ring_free[r], -1)
                        for k in range(3):
                            mm = pe.matmul(ring[r][0:C_QK, 0:n], wq[s][:, k, :], c5[:, k, t0:t0 + n], start=(k == 0), stop=(k == 2))
                        mm.then_inc(ring_full[r], 1)

                    def rotate(j):
                        pe.wait_ge(q_copied, 1).then_inc(q_copied, -1)
                        r = next(turn)
                        pe.wait_ge(ring_free[r], 1).then_inc(ring_free[r], -1)
                        pe.matmul(ring[r][:, :], q_swap[0:C_QK, :], qt[0:C_QK, j * 512:(j + 1) * 512], start=True, stop=True).then_inc(ring_full[r], 1)

                    def key(j):
                        t0, n = ALL_CHUNKS[j]
                        r = next(turn)
                        pe.wait_ge(ring_free[r], 1).then_inc(ring_free[r], -1)
                        for k in range(2):
                            mm = pe.matmul(ring[r][0:C_NOPE, 0:n], wkv[s][:, k, 0:C_NOPE], c5[:, 3 + k, t0:t0 + n], start=(k == 0), stop=(k == 1))
                        mm.then_inc(ring_full[r], 1)

                    def value(t0, t1):
                        r = next(turn)
                        pe.wait_ge(ring_free[r], 1).then_inc(ring_free[r], -1)
                        for t in range(t0, t1):
                            for k in range(2):
                                mm = pe.matmul(ring[r][:, (t - t0) * C_V:(t - t0 + 1) * C_V], c5[:, 3 + k, t * P:(t + 1) * P], wkv[s][:, k, C_NOPE:], start=(k == 0), stop=(k == 1))
                        mm.then_inc(ring_full[r], 1)

                    def maxima(qb, j):
                        if qb == 0 and j == 0:
                            pe.wait_ge(r_ready, 1).then_inc(r_ready, -1)
                        t0, n = ALL_CHUNKS[j]
                        r = next(turn)
                        pe.wait_ge(ring_free[r], 1).then_inc(ring_free[r], -1)
                        pe.matmul(ring[r][:, 0:n], qt_part[s][0][0:C_QK, qb * P:(qb + 1) * P], kt_part[s][0][0:C_QK, t0:t0 + n], start=True, stop=True).then_inc(ring_full[r], 1)

                    def negated(j):
                        if j == 0:
                            pe.wait_ge(neg_ready, 1).then_inc(neg_ready, -1)
                        r = next(turn)
                        pe.wait_ge(ring_free[r], 1).then_inc(ring_free[r], -1)
                        for q in range(4):
                            mm = pe.matmul(ring[r][C_QK:AUG, q * P:(q + 1) * P], neg_max[:, 4 * j + q:4 * j + q + 1], sb["ident"][:, :], start=True, stop=True)
                        mm.then_inc(ring_full[r], 1)

                    return ([lambda j=j: query(j) for j in range(2)] + [lambda: key(0), lambda: rotate(0), lambda: key(1), lambda: rotate(1), lambda: key(2)]
                            + [lambda: value(0, 8), lambda: value(8, NT)] + list(after) + [lambda: None] * (4 - len(after))
                            + [lambda q=q, j=j: maxima(q, j) for q in range(NQ) for j in range(3)]
                            + [lambda: None] * 3 + [lambda: negated(0), lambda: negated(1)])

                def scores(s, n):
                    t, half = units[n]
                    r = n % NS
                    pe.wait_ge(s_free[r], 1).then_inc(s_free[r], -1)
                    for k_, q_ in ((0, 0), (1, 0), (0, 1)):
                        mm = pe.matmul(s_ps[r][:, :], kt_part[s][k_][0:AUG, t * P:(t + 1) * P], qt_part[s][q_][0:AUG, half * 512:(half + 1) * 512],
                                       start=(k_ + q_ == 0), stop=(q_ == 1))
                    mm.then_inc(s_full[r], 1)

                def values(s, n):
                    t, half = units[n]
                    r = n % NPT
                    if n == 0:
                        pe.wait_ge(o_free, 1).then_inc(o_free, -1)
                    pe.wait_ge(p_full[r], 1).then_inc(p_full[r], -1)
                    for q in range(4):
                        mm = pe.matmul(o_ps[half][:, q, 0:C_V + 1], prob[r][:, q * P:(q + 1) * P], vt[s][:, t, :],
                                       start=(t == 0 and q == 0), stop=(t == NT - 1), skip_group_check=True)
                    mm.then_inc(p_free[r], 1)

                def main(s, pieces):
                    pieces = list(pieces)
                    pe.wait_ge(head_ready, 1).then_inc(head_ready, -1)
                    for n in range(n_units + LAG):
                        if n < n_units:
                            scores(s, n)
                        if pieces:
                            pieces.pop(0)()
                        if n >= LAG:
                            values(s, n - LAG)
                        for _ in range(1 if n < n_units // 3 else 2):
                            if pieces:
                                pieces.pop(0)()
                    assert not pieces
                    pe.drain().then_inc(o_full, 1)

                def pair(i):
                    def turned(j):
                        if j == 0:
                            pe.wait_ge(pair_done, 1).then_inc(pair_done, -1)
                        r = next(turn)
                        pe.wait_ge(ring_free[r], 1).then_inc(ring_free[r], -1)
                        for q in range(4):
                            mm = pe.transpose(ring[r][:, q * P:(q + 1) * P], o_tok[:, 4 * j + q, :], sb["ident"][:, :])
                        mm.then_inc(ring_full[r], 1)
                    return [lambda j=j: turned(j) for j in range(2)]
                over_heads(pe, prepare, main, pair)

            @block.vector
            def _(dve):
                turn = turns()
                def done(ins, *to):
                    ins.then_inc(step, 1)
                    dve.wait_ge(step, 1).then_inc(step, -1)
                    for x_ in to:
                        dve.sem_inc(x_, 1)

                dve.wait_ge(loaded, 48)
                for g in (w_free, ring_free):
                    give(dve, g)
                give(dve, [o_free])
                for s in range(2):
                    hi, lo = kt_part[s]
                    dve.memset(vt[s][:, :, C_V:], 1.0)
                    done(dve.memset(kt[row, :], 1.0))
                    done(dve.tensor_copy(hi[rr, :], kpe_rot[rr, :]))
                    done(dve.tensor_tensor(lo[rr, :], kpe_rot[rr, :], hi[rr, :].bitcast(F32), ALU.subtract))
                    done(dve.tensor_copy(hi[row, :], kt[row, :]))
                    done(dve.tensor_tensor(lo[row, :], kt[row, :], kt[row, :], ALU.subtract))
                dve.sem_inc(ones_set, 1)

                def prepare(s, after=()):
                    def query(j):
                        r = next(turn)
                        dve.wait_ge(ring_full[r], 1).then_inc(ring_full[r], -1)
                        done(dve.tensor_copy(qt[0:C_QK, j * 512:(j + 1) * 512], ring[r][0:C_QK, :]), ring_free[r], q_copied)

                    def rotate(j):
                        c = slice(j * 512, (j + 1) * 512)
                        r = next(turn)
                        dve.wait_ge(ring_full[r], 1).then_inc(ring_full[r], -1)
                        done(dve.tensor_tensor(tmp[rr, :], ring[r][rr, :], sin[rr, c], ALU.mult), ring_free[r])
                        done(dve.tensor_tensor(qt[rr, c], qt[rr, c], cos[rr, c], ALU.mult))
                        done(dve.tensor_tensor(qt[rr, c], qt[rr, c], tmp[rr, :], ALU.add))
                        if j == 1:
                            dve.sem_inc(q_fixed, 1)

                    def key(j):
                        t0, n = ALL_CHUNKS[j]
                        r = next(turn)
                        dve.wait_ge(ring_full[r], 1).then_inc(ring_full[r], -1)
                        done(dve.tensor_copy(kt[0:C_NOPE, t0:t0 + n], ring[r][0:C_NOPE, 0:n]), ring_free[r])
                        if j == 2:
                            dve.sem_inc(k_copied, 1)

                    def value(t0, t1):
                        r = next(turn)
                        dve.wait_ge(ring_full[r], 1).then_inc(ring_full[r], -1)
                        if t1 == NT:
                            dve.sem_inc(w_free[s], 1)
                        done(dve.tensor_copy(vt[s][:, t0:t1, 0:C_V], ring[r][:, 0:(t1 - t0) * C_V].rearrange("p (t d) -> p t d", d=C_V)), ring_free[r])

                    def maxima(qb, j):
                        t0, n = ALL_CHUNKS[j]
                        r = next(turn)
                        dve.wait_ge(ring_full[r], 1).then_inc(ring_full[r], -1)
                        top = dve.tensor_reduce(part_max[:, qb, j:j + 1], ring[r][:, 0:n], AX_X, ALU.max)
                        if qb < NQ - 1:
                            top.then_inc(ring_free[r], 1)
                        else:
                            done(top, ring_free[r])
                        if qb == NQ - 1 and j == 2:
                            done(dve.tensor_reduce(neg_max[:, :], part_max[:, :, :], AX_X, ALU.max))
                            done(dve.tensor_scalar(neg_max[:, :], neg_max[:, :], -1.0, None, ALU.mult), neg_ready)

                    def low_part(x, parts, rows, c):
                        dve.wait_ge(hi_ready, 1).then_inc(hi_ready, -1)
                        done(dve.tensor_tensor(parts[1][rows, c], x[rows, c], parts[0][rows, c].bitcast(F32), ALU.subtract))

                    def negated(j):
                        r = next(turn)
                        dve.wait_ge(ring_full[r], 1).then_inc(ring_full[r], -1)
                        hi, lo = (x_[row, j * 512:(j + 1) * 512] for x_ in qt_part[s])
                        done(dve.tensor_copy(hi, ring[r][row, :]))
                        done(dve.tensor_tensor(lo, ring[r][row, :], hi.bitcast(F32), ALU.subtract), ring_free[r])
                        if j == 1:
                            dve.sem_inc(head_ready, 1)

                    lows = ([lambda j=j: low_part(qt, qt_part[s], slice(0, C_QK), slice(j * 512, (j + 1) * 512)) for j in range(2)]
                            + [lambda t0=t0, n=n: low_part(kt, kt_part[s], slice(0, C_NOPE), slice(t0, t0 + n)) for t0, n in ALL_CHUNKS])
                    return ([lambda j=j: query(j) for j in range(2)] + [lambda: key(0), lambda: rotate(0), lambda: key(1), lambda: rotate(1), lambda: key(2)]
                            + [lambda: value(0, 8), lambda: value(8, NT)] + list(after) + [lambda: None] * (4 - len(after))
                            + [piece for q in range(NQ) for piece in [lambda j=j, q=q: maxima(q, j) for j in range(3)] + lows[q:q + 1]]
                            + [lambda j=j: negated(j) for j in range(2)])

                def main(s, pieces):
                    for piece in pieces:
                        piece()
                    dve.wait_ge(o_full, 1).then_inc(o_full, -1)
                    for half in range(2):
                        done(dve.reciprocal(rec[:, half, :], o_ps[half][:, :, C_V]))
                        done(dve.tensor_tensor(o_tok[:, 4 * half:4 * half + 4, s * C_V:(s + 1) * C_V], o_ps[half][:, :, 0:C_V],
                                               rec[:, half, :].rearrange("p (q o) -> p q o", o=1).to_broadcast([P, 4, C_V]), ALU.mult))
                    dve.sem_inc(o_free, 1)
                    if s == 1:
                        dve.sem_inc(pair_done, 1)

                def pair(i):
                    def output(j):
                        r = next(turn)
                        dve.wait_ge(ring_full[r], 1).then_inc(ring_full[r], -1)
                        done(dve.tensor_copy(x[:, bass.ds(i, 1), CTX_LEN + j * 512:CTX_LEN + (j + 1) * 512], ring[r][:, :].rearrange("p (o n) -> p o n", o=1)), ring_free[r])
                    return [lambda j=j: output(j) for j in range(2)]
                over_heads(dve, prepare, main, pair)

            @block.scalar
            def _(act):
                give(act, s_free)

                def prepare(s, after=()):
                    def round_query(j):
                        c = slice(j * 512, (j + 1) * 512)
                        if j == 0:
                            act.wait_ge(q_fixed, 1).then_inc(q_fixed, -1)
                        act.activation(qt_part[s][0][0:C_QK, c], qt[0:C_QK, c], ACT.Copy).then_inc(rounded, 1)

                    def round_key(j):
                        t0, n = ALL_CHUNKS[j]
                        if j == 0:
                            act.wait_ge(k_copied, 1).then_inc(k_copied, -1)
                        act.activation(kt_part[s][0][0:C_NOPE, t0:t0 + n], kt[0:C_NOPE, t0:t0 + n], ACT.Copy).then_inc(rounded, 1)
                        if j == 2:
                            act.wait_ge(rounded, 5).then_inc(rounded, -5)
                            act.sem_inc(r_ready, 1)
                            act.sem_inc(hi_ready, 5)
                    return [lambda j=j: round_query(j) for j in range(2)] + [lambda j=j: round_key(j) for j in range(3)]

                def main(s, pieces):
                    pieces = list(pieces)
                    for n in range(n_units):
                        r, b = n % NS, n % NPT
                        act.wait_ge(s_full[r], 1).then_inc(s_full[r], -1)
                        act.wait_ge(p_free[b], 1).then_inc(p_free[b], -1)
                        act.activation(prob[b][:, :], s_ps[r][:, :], ACT.Exp, scale=scale).then_inc(act_step, 1)
                        act.wait_ge(act_step, 1).then_inc(act_step, -1)
                        act.sem_inc(s_free[r], 1)
                        act.sem_inc(p_full[b], 1)
                        for _ in range(2 if n >= 3 else 0):
                            if pieces:
                                pieces.pop(0)()
                for r in range(NPT):
                    act.sem_inc(p_free[r], 1)
                over_heads(act, prepare, main, lambda i: ())


def program(nc, a, out):
    Stage.used_semaphores = []
    with ExitStack() as ctx:
        def sbt(name, *shape):
            return ctx.enter_context(nc.sbuf_tensor(name, list(shape), F32))

        sb = {
            "ident": sbt("ident", P, P), "ones": sbt("ones", P, P),
            "cols_a": sbt("cols_a", P, P), "cols_b": sbt("cols_b", P, P),
            "silu_c": sbt("silu_c", P, KD, 2),
            "coef": sbt("coef", P, DEPTH, 2, 2, 3, KD),
        }
        h_ctx = nc.dram_tensor("h_ctx", (CTX_LEN, D_MODEL), F32, kind="Internal").ap()
        h_lat = nc.dram_tensor("h_lat", (SEQ, D_MODEL), F32, kind="Internal").ap()
        x, cx = a["x"][0], a["ctx"][0]
        u = sbt("u", P, KD, TOK)
        load_constants(nc, a, sb)
        adaln(nc, a, sb)
        norms(nc, a, sb, "norm_ab", [(1, 0, CT, cx, None), (0, CT, LT, x, None)], layer_u=(0, 0), u=u)
        x_mix = u
        qkv_dram = nc.dram_tensor("qkv_dram", (12, P, TOK), F32, kind="Internal").ap()
        cols = sbt("cols", P, NT, 2, 6, B_HEADS)
        with Stage(nc, "layer0") as l0:
            pa = l0.sb("pa", P, 10, TOK)
            decay_columns(nc, a, sb, u, cols)
            with Stage(nc, "layer0b") as l0b:
                pb = l0b.sb("pb", P, 12, TOK)
                w = a["ab_w_in"][0]
                project(nc, "in_ab", [(w, 0, P, 6, pa, 0), (w, 2304, P, 4, pa, 6), (w, 768, P, 12, pb, 0)], u, KD, ALL_CHUNKS)
                conv_qkv(nc, a, sb, pb, qkv_dram)
            with Stage(nc, "layer0c") as l0c:
                k_dup = l0c.sb("k_dup", P, A_KV, (NT + 2) * P)
                v_tok = l0c.sb("v_tok", P, NT + 2, P)
                window_prepare(nc, a, sb, pa, k_dup, v_tok)
                window_attention(nc, a, sb, pa, k_dup, v_tok, x_mix)
            Stage.recycle(nc)
            delta_rule(nc, a, sb, qkv_dram, cols, (x_mix[:, 4:8, :], pa[:, 0:4, :]))
            head_norm(nc, a, sb, x_mix[:, 4:8, :], pa[:, 0:4, :], pa[:, 6:10, :])
        Stage.recycle(nc)
        cond_tiles = ((1, 0, CT), (0, CT, LT))
        with Stage(nc, "out0") as st:
            y = st.sb("y", P, KD, TOK)
            project_split(nc, "out_ab", a["ab_w_out"][0], 0, KD, y, x_mix, KD, ALL_CHUNKS)
            norms(nc, a, sb, "res_ab", [(*cond_tiles[0], cx, h_ctx), (*cond_tiles[1], x, h_lat)],
                  layer_y=(0, 0), y=y, layer_u=(0, 1), u=u)

        def ffn_of(layer, chunks):
            ffn(nc, f"ffn{layer}", a["ffn_w_gate"][layer], a["ffn_w_up"][layer], a["ffn_w_down"][layer], u, chunks)

        ffn_of(0, ALL_CHUNKS)
        norms(nc, a, sb, "res_ffn0", [(*cond_tiles[0], h_ctx, None), (*cond_tiles[1], h_lat, h_lat)],
              layer_y=(0, 1), y=u, layer_u=(1, 0), u=u)
        Stage.recycle(nc)

        with Stage(nc, "layer1") as l1:
            c5, kpe, kpe_rot = l1.sb("c5", P, 5, TOK), l1.sb("kpe", C_ROPE, 1, TOK), l1.sb("kpe_rot", P, TOK)
            w = a["mla_w_in"][0]
            project_split(nc, "in_mla", w, 0, 5, c5, u, KD, ALL_CHUNKS, tail=(QR + KVR, C_ROPE, kpe))
            latent_norms(nc, a, sb, c5, kpe, kpe_rot)
            latent_attention(nc, a, sb, c5, kpe_rot, u)
        with Stage(nc, "out1") as st:
            y = st.sb("y", P, KD, TOK)
            project_split(nc, "out_mla", a["mla_w_out"][0], 0, KD, y, u, KD, LAT_CHUNKS)
            Stage.recycle(nc)
            norms(nc, a, sb, "res_mla", [(*cond_tiles[1], h_lat, h_lat)], layer_y=(1, 0), y=y, layer_u=(1, 1), u=u)
        ffn_of(1, LAT_CHUNKS)
        norms(nc, a, sb, "res_ffn1", [(*cond_tiles[1], h_lat, out[0])], layer_y=(1, 1), y=u)


def tables():
    i = np.arange(P)
    eye = np.eye(P, dtype=np.float32)

    def pick(src, rows=P):
        m = np.zeros((P, P), np.float32)
        for out, s in enumerate(src):
            if s is not None:
                m[s, out] = 1.0
        return m

    half = A_DIM // 2
    mats = {"ident": eye, "ones": np.ones((P, P), np.float32)}
    swap = [(m // A_DIM) * A_DIM + (m % A_DIM + half) % A_DIM for m in i]
    mats["swap"] = pick(swap)
    for kv in range(2):
        mats[f"dup{kv}"] = pick([kv * A_DIM + m % A_DIM for m in i])
        mats[f"dupswap{kv}"] = pick([kv * A_DIM + (m % A_DIM + half) % A_DIM for m in i])
    hr = C_ROPE // 2
    mats["kpe_place"] = pick([m - C_NOPE if C_NOPE <= m < C_QK else None for m in i])
    mats["kpe_swap"] = pick([(m - C_NOPE + hr) % C_ROPE if C_NOPE <= m < C_QK else None for m in i])
    mats["q_swap"] = pick([C_NOPE + (m - C_NOPE + hr) % C_ROPE if C_NOPE <= m < C_QK else None for m in i])
    upto = (i[:, None] <= i[None, :])
    mats["cum0"], mats["cum1"] = upto.astype(np.float32), upto.T.astype(np.float32)
    mats["decay_mask0"] = np.where(upto, 0, NEG).astype(np.float32)
    mats["decay_mask1"] = np.where(upto.T, 0, NEG).astype(np.float32)
    for l in range(LEVELS):
        b = i >> l
        m = ((b[:, None] >> 1) == (b[None, :] >> 1)) & (b[:, None] % 2 == 1) & (b[None, :] % 2 == 0)
        mats[f"level0_{l}"], mats[f"level1_{l}"] = m.astype(np.float32), m.T.astype(np.float32)

    def rope(dim):
        n = dim // 4
        inv = (np.float32(10000.0) ** (-np.arange(n, dtype=np.float32) / n)).astype(np.float32)
        t = np.arange(SEQ)
        ang = np.concatenate([(t // GRID_W)[None, :] * inv[:, None], (t % GRID_W)[None, :] * inv[:, None]], 0).astype(np.float32)
        c, s = np.cos(ang), np.sin(ang)
        cos = np.ones((dim, TOK), np.float32)
        sin = np.zeros((dim, TOK), np.float32)
        cos[:, CTX_LEN:] = np.concatenate([c, c], 0)
        sin[:, CTX_LEN:] = np.concatenate([-s, s], 0)
        return cos, sin

    rope_a = np.stack([np.tile(x, (2, 1)) for x in rope(A_DIM)])
    rope_c = np.zeros((2, P, TOK), np.float32)
    rope_c[:, C_NOPE:C_QK] = np.stack(rope(C_ROPE))
    rel = np.arange(3 * P)[None, :] - P - i[:, None]
    window = np.full((NT, P, 3 * P), NEG, np.float32)
    for t in range(CT, NT):
        key = (t - CT) * P - P + np.arange(3 * P)
        window[t] = np.where((np.abs(rel) <= 128) & ((key >= 0) & (key < SEQ))[None, :], 0, NEG)
    return {"mats": np.stack([mats[m] for m in MATS]), "rope_a": rope_a.astype(np.float32),
            "rope_c": rope_c, "window": window}


INPUTS = ["x", "c", "ctx", "c_ctx", "mod_w", "mod_b", "norm_gains", "ffn_w_gate", "ffn_w_up", "ffn_w_down",
          "ab_w_in", "ab_sink", "ab_conv", "ab_a_log", "ab_dt_bias", "ab_out_norm", "ab_w_out",
          "mla_w_in", "mla_q_norm", "mla_kv_norm", "mla_w_qb", "mla_w_kvb", "mla_w_out"]


def kernel(**inputs):
    import concourse.bacc as bacc
    from concourse.bass_utils import run_bass_kernel_spmd

    nc = bacc.Bacc("TRN2", target_bir_lowering=False, num_devices=1)
    arrays = {n: np.ascontiguousarray(inputs[n]) for n in INPUTS}
    arrays.update(tables())
    aps = {n: nc.dram_tensor(f"in_{n}", v.shape, F32, kind="ExternalInput").ap() for n, v in arrays.items()}
    out = nc.dram_tensor("out", (1, SEQ, D_MODEL), F32, kind="ExternalOutput").ap()
    program(nc, aps, out)
    r = run_bass_kernel_spmd(nc, [{f"in_{n}": v for n, v in arrays.items()}], core_ids=[0])
    return r.results[0]["out"]
```
